# Optimizing a Trainium2 kernel written in Bass

```python
import math
import jax, jax.numpy as jnp
from jax import lax
import numpy as np

D_MODEL = 1024
BATCH = 1
SEQ = 512
DEPTH = 1

CHUNK = 64
D_MIX = D_MODEL
D_SSM = D_MIX // 2
SSM_GROUP = 16
N_SSM_GROUPS = D_SSM // SSM_GROUP
SSM_STATE = 64
D_CONV = D_MIX - D_SSM
CONV_WIDTH = 31
D_IN_PROJ = D_SSM + 2 * D_CONV
PEER_HEADS = 8
PEER_KEYS = 128
PEER_EXPERTS = PEER_KEYS * PEER_KEYS
PEER_TOPK = 16
PEER_DKEY = 256
PEER_HALF = PEER_DKEY // 2
PEER_BLOCK = 128
EPS = 1e-6
DT_MIN = 0.001
DT_MAX = 0.1

kernel_name = "hybrid_s5_conformer_peer_block"

def rmsnorm(x, g):
    xf = x.astype(jnp.float32)
    out = xf * lax.rsqrt(jnp.mean(xf * xf, axis=-1, keepdims=True) + EPS) * g.astype(jnp.float32)
    return out.astype(x.dtype)

def s5_mixer(u, lam_re, lam_im, log_dt, b_re, b_im, c_re, c_im, d_skip, glu_w, glu_b):
    bsz, seq, _ = u.shape
    f32 = jnp.float32
    ug = u.astype(f32).reshape(bsz, seq, N_SSM_GROUPS, SSM_GROUP)
    lr = lam_re.astype(f32)
    li = lam_im.astype(f32)
    dt = jnp.exp(log_dt.astype(f32))[:, None]
    mag = jnp.exp(lr * dt)
    ang = li * dt
    lb_re = mag * jnp.cos(ang)
    lb_im = mag * jnp.sin(ang)
    num_re = lb_re - 1.0
    num_im = lb_im
    den = lr * lr + li * li
    f_re = (num_re * lr + num_im * li) / den
    f_im = (num_im * lr - num_re * li) / den
    br = b_re.astype(f32)
    bi = b_im.astype(f32)
    bb_re = f_re[..., None] * br - f_im[..., None] * bi
    bb_im = f_re[..., None] * bi + f_im[..., None] * br
    bu_re = jnp.einsum('blgh,gph->blgp', ug, bb_re)
    bu_im = jnp.einsum('blgh,gph->blgp', ug, bb_im)
    a_re = jnp.broadcast_to(lb_re[None, None], (1, seq, N_SSM_GROUPS, SSM_STATE))
    a_im = jnp.broadcast_to(lb_im[None, None], (1, seq, N_SSM_GROUPS, SSM_STATE))

    def combine(e1, e2):
        a1r, a1i, b1r, b1i = e1
        a2r, a2i, b2r, b2i = e2
        return (a1r * a2r - a1i * a2i,
                a1r * a2i + a1i * a2r,
                a2r * b1r - a2i * b1i + b2r,
                a2r * b1i + a2i * b1r + b2i)

    _, _, s_re, s_im = lax.associative_scan(combine, (a_re, a_im, bu_re, bu_im), axis=1)
    y = (jnp.einsum('blgp,ghp->blgh', s_re, c_re.astype(f32))
         - jnp.einsum('blgp,ghp->blgh', s_im, c_im.astype(f32))
         + d_skip.astype(f32).reshape(N_SSM_GROUPS, SSM_GROUP) * ug)
    y = jax.nn.gelu(y, approximate=False)
    gate = jnp.einsum('blgh,ghk->blgk', y, glu_w.astype(f32)) + glu_b.astype(f32).reshape(N_SSM_GROUPS, SSM_GROUP)
    y = y * jax.nn.sigmoid(gate)
    return y.reshape(bsz, seq, D_SSM).astype(u.dtype)

def conformer_conv(v, g, conv_w, conv_b, ln_g, ln_b):
    h = v * jax.nn.sigmoid(g)
    h = lax.conv_general_dilated(
        h, conv_w[:, None, :], window_strides=(1,), padding=[(CONV_WIDTH - 1, 0)],
        dimension_numbers=('NWC', 'WIO', 'NWC'), feature_group_count=D_CONV) + conv_b
    hf = h.astype(jnp.float32)
    mu = jnp.mean(hf, axis=-1, keepdims=True)
    var = jnp.mean(jnp.square(hf - mu), axis=-1, keepdims=True)
    hn = (hf - mu) * lax.rsqrt(var + EPS) * ln_g.astype(jnp.float32) + ln_b.astype(jnp.float32)
    return jax.nn.silu(hn).astype(v.dtype)

def peer_ffn(xn, w_q, sub_k1, sub_k2, u_tab, v_tab):
    bsz, seq, d = xn.shape
    xt = xn.reshape(-1, PEER_BLOCK, d)
    k1 = sub_k1.astype(jnp.float32)
    k2 = sub_k2.astype(jnp.float32)

    def block(xb):
        q = (xb @ w_q).astype(jnp.float32).reshape(PEER_BLOCK, PEER_HEADS, 2, PEER_HALF)
        s1 = jnp.einsum('thk,nk->thn', q[:, :, 0], k1)
        s2 = jnp.einsum('thk,nk->thn', q[:, :, 1], k2)
        v1, i1 = lax.top_k(s1, PEER_TOPK)
        v2, i2 = lax.top_k(s2, PEER_TOPK)
        cand = (v1[..., :, None] + v2[..., None, :]).reshape(PEER_BLOCK, PEER_HEADS, PEER_TOPK * PEER_TOPK)
        sc, ci = lax.top_k(cand, PEER_TOPK)
        e1 = jnp.take_along_axis(i1, ci // PEER_TOPK, axis=-1)
        e2 = jnp.take_along_axis(i2, ci % PEER_TOPK, axis=-1)
        eid = e1 * PEER_KEYS + e2
        gates = jax.nn.softmax(sc, axis=-1)
        u_sel = u_tab[eid]
        act = jax.nn.gelu(jnp.einsum('td,thkd->thk', xb, u_sel).astype(jnp.float32), approximate=False)
        w = (gates * act).astype(xb.dtype)
        return jnp.einsum('thk,thkd->td', w, v_tab[eid])

    out = lax.map(block, xt)
    return out.reshape(bsz, seq, d)

def setup_inputs(seed: int = 0) -> dict:
    key = jax.random.key(seed)
    ks = jax.random.split(key, 24)
    f32 = jnp.float32
    nrm = lambda k, shape, s: (jax.random.normal(k, shape, f32) * s).astype(f32)
    L_, G, P, H = DEPTH, N_SSM_GROUPS, SSM_STATE, SSM_GROUP
    x = jax.random.normal(ks[0], (BATCH, SEQ, D_MODEL), f32)
    norm1_g = 1.0 + nrm(ks[1], (L_, D_MODEL), 0.02)
    w_in = nrm(ks[2], (L_, D_MODEL, D_IN_PROJ), D_MODEL ** -0.5)
    lam_re = -0.5 + nrm(ks[3], (L_, G, P), 0.01)
    lam_im = math.pi * jnp.arange(P, dtype=f32)[None, None, :] + nrm(ks[4], (L_, G, P), 0.01)
    log_dt = jax.random.uniform(ks[5], (L_, G), f32, math.log(DT_MIN), math.log(DT_MAX))
    ssm_b_re = nrm(ks[6], (L_, G, P, H), (2.0 * H) ** -0.5)
    ssm_b_im = nrm(ks[7], (L_, G, P, H), (2.0 * H) ** -0.5)
    ssm_c_re = nrm(ks[8], (L_, G, H, P), (2.0 * P) ** -0.5)
    ssm_c_im = nrm(ks[9], (L_, G, H, P), (2.0 * P) ** -0.5)
    ssm_d = nrm(ks[10], (L_, D_SSM), 1.0)
    glu_w = nrm(ks[11], (L_, G, H, H), H ** -0.5)
    glu_b = nrm(ks[12], (L_, D_SSM), 0.02)
    conv_w = nrm(ks[13], (L_, CONV_WIDTH, D_CONV), CONV_WIDTH ** -0.5)
    conv_b = nrm(ks[14], (L_, D_CONV), 0.02)
    conv_ln_g = 1.0 + nrm(ks[15], (L_, D_CONV), 0.02)
    conv_ln_b = nrm(ks[16], (L_, D_CONV), 0.02)
    w_out = nrm(ks[17], (L_, D_MIX, D_MODEL), D_MIX ** -0.5)
    norm2_g = 1.0 + nrm(ks[18], (L_, D_MODEL), 0.02)
    peer_wq = nrm(ks[19], (L_, D_MODEL, PEER_HEADS * PEER_DKEY), D_MODEL ** -0.5)
    peer_k1 = nrm(ks[20], (L_, PEER_KEYS, PEER_HALF), PEER_HALF ** -0.5)
    peer_k2 = nrm(ks[21], (L_, PEER_KEYS, PEER_HALF), PEER_HALF ** -0.5)
    peer_u = nrm(ks[22], (L_, PEER_EXPERTS, D_MODEL), D_MODEL ** -0.5)
    kv, kf = jax.random.split(ks[23])
    peer_v = nrm(kv, (L_, PEER_EXPERTS, D_MODEL), 0.5)
    final_g = 1.0 + nrm(kf, (D_MODEL,), 0.02)
    return {"x": x, "norm1_g": norm1_g, "w_in": w_in, "lam_re": lam_re, "lam_im": lam_im,
            "log_dt": log_dt, "ssm_b_re": ssm_b_re, "ssm_b_im": ssm_b_im, "ssm_c_re": ssm_c_re,
            "ssm_c_im": ssm_c_im, "ssm_d": ssm_d, "glu_w": glu_w, "glu_b": glu_b,
            "conv_w": conv_w, "conv_b": conv_b, "conv_ln_g": conv_ln_g, "conv_ln_b": conv_ln_b,
            "w_out": w_out, "norm2_g": norm2_g, "peer_wq": peer_wq, "peer_k1": peer_k1,
            "peer_k2": peer_k2, "peer_u": peer_u, "peer_v": peer_v, "final_g": final_g}

def reference(x, norm1_g, w_in, lam_re, lam_im, log_dt, ssm_b_re, ssm_b_im, ssm_c_re, ssm_c_im,
              ssm_d, glu_w, glu_b, conv_w, conv_b, conv_ln_g, conv_ln_b, w_out, norm2_g,
              peer_wq, peer_k1, peer_k2, peer_u, peer_v, final_g):
    for l in range(DEPTH):
        h = rmsnorm(x, norm1_g[l])
        z = h @ w_in[l]
        u_ssm = z[..., :D_SSM]
        v_conv = z[..., D_SSM:D_SSM + D_CONV]
        g_conv = z[..., D_SSM + D_CONV:]
        y_ssm = s5_mixer(u_ssm, lam_re[l], lam_im[l], log_dt[l], ssm_b_re[l], ssm_b_im[l],
                         ssm_c_re[l], ssm_c_im[l], ssm_d[l], glu_w[l], glu_b[l])
        y_conv = conformer_conv(v_conv, g_conv, conv_w[l], conv_b[l], conv_ln_g[l], conv_ln_b[l])
        x = x + jnp.concatenate([y_ssm, y_conv], axis=-1) @ w_out[l]
        x = x + peer_ffn(rmsnorm(x, norm2_g[l]), peer_wq[l], peer_k1[l], peer_k2[l], peer_u[l], peer_v[l])
    return rmsnorm(x, final_g)


_drawn_inputs = setup_inputs


def setup_inputs(seed=0):
    import zlib

    import numpy as np

    out = dict(_drawn_inputs(seed))
    spreads = {}
    factors = {'lam_re': 200.0,
     'glu_b': 5.871,
     'final_g': 21.493,
     'lam_im': 16.087,
     'log_dt': 15.995,
     'ssm_b_re': 22.163,
     'ssm_b_im': 21.469,
     'ssm_c_re': 22.646,
     'ssm_c_im': 24.207}
    for name, (base, spread) in spreads.items():
        noise = np.random.default_rng([zlib.crc32(name.encode()), seed]).standard_normal(out[name].shape)
        drawn = base * np.exp(spread * noise) if base else spread * noise
        out[name] = __import__('jax').numpy.asarray(drawn.astype(out[name].dtype))
    for name, factor in factors.items():
        out[name] = (out[name] * factor).astype(out[name].dtype)
    return out
```

```python
from contextlib import ExitStack

import numpy as np

import concourse.bass as bass
from concourse import mybir

F32 = mybir.dt.float32
F32R = mybir.dt.float32r
F16 = mybir.dt.float16
U32 = mybir.dt.uint32
ALU = mybir.AluOpType
ACT = mybir.ActivationFunctionType
AX_X = mybir.AxisListType.X

P = 128
D = 1024
T = 512
NC = D // P
GROUPS, CH, STATE = 32, 16, 64
PAIRS = GROUPS // 2
SUB = P // CH
NSUB = T // SUB
CT = 4
GPT = GROUPS // CT
WIDTH = 31
PAD = WIDTH - 1
HEADS, KEYS, TOPK = 8, 128, 16
TB = T // P
EPS = 1e-6

WIN, WOUT, WQ = 0, 12, 20
UT = WQ + 2 * HEADS
VT = UT + KEYS
NTILES = VT + KEYS

ALONE = 32
STEP_TOK = 8
SPREAD = T // STEP_TOK
GROUP = 4
GCH = 64
PIECES = 4
OH = 4
GSCALE = 16384.0
EXP_AT = 18

V_G1, V_G2, V_GF, V_CB, V_LG, V_LB, V_D, V_GB, V_CW = 0, 8, 16, 24, 28, 32, 36, 40, 44
NV = V_CW + CT * WIDTH
S_LR, S_LI, S_DT, S_BR, S_BI, S_CR, S_CI = 0, 16, 32, 48, 304, 560, 816
NS = 1072
NEG = -3.0e38
TWO_PI = (6.28125, 0.0019350051879882812, 3.019916050e-07)
MAGIC = 12582912.0
PI_IN = 3.1415925


def wait(eng, sem, value):
    if not (isinstance(value, int) and value <= 0):
        eng.wait_ge(sem, value)


class Chain:

    def __init__(self, eng, sem):
        self.eng, self.sem, self.n = eng, sem, 0

    def step(self, ins):
        ins.then_inc(self.sem, 1)
        self.n += 1
        self.eng.wait_ge(self.sem, self.n)


def build(nc, vecs, ssm, xT, glu_bd, keys, tiles, outT):
    with ExitStack() as ctx:
        def sb(name, shape, dt=F32, c=ctx):
            return c.enter_context(nc.sbuf_tensor(name, shape, dt))

        def sem(name):
            return ctx.enter_context(nc.semaphore(name))

        vec = sb("vec", [P, NV])
        ones = sb("ones", [P, P])
        ident = sb("ident", [P, P])
        iota_row = sb("iota_row", [P, P])
        iota16 = sb("iota16", [P, TOPK])
        epsc = sb("epsc", [P, 1])
        rstd = sb("rstd", [P, T])
        x2 = sb("x2", [P, NC, T])
        rhs_hi = sb("rhs_hi", [P, NC, T], F32R)
        rhs_lo = sb("rhs_lo", [P, NC, T], F32R)
        raw = sb("raw", [P, 2, D])
        w_hi = sb("w_hi", [P, 2, D], F32R)
        w_lo = sb("w_lo", [P, 2, D], F32R)
        keyT = sb("keyT", [P, 2, KEYS])
        PS = ctx.enter_context(nc.psum_tensor("PS", [P, 8, T], F32))

        u_scr = nc.dram_tensor("u_scr", [SUB, CH, GROUPS, NSUB], F32).ap()
        y_scr = nc.dram_tensor("y_scr", [GROUPS, CH, SUB, NSUB], F32).ap()
        act_scr = nc.dram_tensor("act_scr", [KEYS, P, T], F32).ap()
        gate_scr = nc.dram_tensor("gate_scr", [P, T // GCH, KEYS * GCH], F32).ap()

        pre = ExitStack()
        prm = sb("prm", [P, NS], F32, pre)
        bd = sb("bd", [P, CT, P], F32, pre)
        xuc = sb("xuc", [P, NC, T], F32, pre)
        hc = sb("hc", [P, CT, PAD + T], F32, pre)
        sg = sb("sg", [P, 2, T], F32, pre)
        names = ("kk", "exps", "phi", "turns", "red", "half", "mag", "sin", "sinh", "cos", "pr", "pi",
                 "fpr", "fpi", "t9")
        tab = {n: sb("tab_" + n, [P, PAIRS, SUB + 1], F32, pre) for n in names}
        rev_r = sb("rev_r", [P, PAIRS, SUB], F32, pre)
        rev_i = sb("rev_i", [P, PAIRS, SUB], F32, pre)
        small = sb("small", [P, 12, PAIRS], F32, pre)
        cp_r = sb("cp_r", [P, PAIRS, SUB + 1, CH], F32, pre)
        cp_i = sb("cp_i", [P, PAIRS, SUB + 1, CH], F32, pre)
        m1 = sb("m1", [P, 2, PAIRS, P], F32, pre)
        rot_r = sb("rot_r", [P, PAIRS, NSUB + 1], F32, pre)
        rot_i = sb("rot_i", [P, PAIRS, NSUB + 1], F32, pre)
        big = sb("big", [P, 8320], F32, pre)
        pre.close()
        u_t = xuc[:, 0:CT, :]
        cv = xuc[:, CT:NC, :]
        m2 = x2[:].rearrange("p c t -> p (c t)").rearrange("p (g m) -> p g m", g=GROUPS)
        tmp = big[:, 0:PAIRS * (SUB + 1) * CH]
        kimp = big[:, 0:4096].rearrange("p (g m) -> p g m", g=GROUPS)
        za, zb, zc, zt = (big[:, i * 1024:(i + 1) * 1024] for i in range(4))
        ysb = big[:, 0:2048]
        sq = big[:, 4096:8192].rearrange("p (c t) -> p c t", c=NC)
        ab_r = big[:, 4096:6144].rearrange("p (a j h) -> p a j h", a=PAIRS, j=SUB)
        ab_i = big[:, 6144:8192].rearrange("p (a j h) -> p a j h", a=PAIRS, j=SUB)
        u_sub = big[:, 4096:6144].rearrange("p (g c) -> p g c", g=GROUPS)
        sp_r = big[:, 6144:7184].rearrange("p (a c) -> p a c", a=PAIRS)
        sp_i = big[:, 7184:8224].rearrange("p (a c) -> p a c", a=PAIRS)
        y_t = big[:, 4096:6144].rearrange("p (a t) -> p a t", a=CT)

        peer = ExitStack()
        act_sb = sb("act_sb", [P, 2, T], F32, peer)
        q_sb = sb("q_sb", [P, 2, T], F32, peer)
        oh_1 = sb("oh_1", [P, OH, GROUP, KEYS], F16, peer)
        oh_gh = sb("oh_gh", [P, OH, GROUP, KEYS], F16, peer)
        oh_gl = sb("oh_gl", [P, OH, GROUP, KEYS], F16, peer)
        iota_h = sb("iota_h", [P, KEYS], F16, peer)
        e1T = sb("e1T", [P, P], F32, peer)
        e2T = sb("e2T", [P, P], F32, peer)
        gT = sb("gT", [P, P], F32, peer)
        ghT = sb("ghT", [P, P], F16, peer)
        ghTf = sb("ghTf", [P, P], F32, peer)
        glT = sb("glT", [P, P], F32, peer)
        topv = sb("topv", [P, 2, TB, TOPK], F32, peer)
        topi = sb("topi", [P, 2, TB, TOPK], U32, peer)
        selv = sb("selv", [P, TB, TOPK], F32, peer)
        seli = sb("seli", [P, TB, TOPK], U32, peer)
        sel_all = sb("sel_all", [P, TB, HEADS, TOPK], F32, peer)
        ci_all = sb("ci_all", [P, TB, HEADS, TOPK], U32, peer)
        i1_all = sb("i1_all", [P, TB, HEADS, TOPK], F32, peer)
        i2_all = sb("i2_all", [P, TB, HEADS, TOPK], F32, peer)
        pos = sb("pos", [P, TB, P], U32, peer)
        pos_a = sb("pos_a", [P, TB, P], F32, peer)
        pos_b = sb("pos_b", [P, TB, P], F32, peer)
        e1 = sb("e1", [P, TB, P], F32, peer)
        e2 = sb("e2", [P, TB, P], F32, peer)
        sel_now = sb("sel_now", [P, 3, P], F32, peer)
        gsum = sb("gsum", [P, 2, TB * HEADS], F32, peer)
        route = ExitStack()
        s_all = sb("s_all", [P, 2 * HEADS, T], F32, route)
        s_cur = sb("s_cur", [P, 2, TB, KEYS], F32, route)
        s_cut = sb("s_cut", [P, 2, TB, KEYS], F32, route)
        cand = sb("cand", [P, TB, TOPK * TOPK], F32, route)
        cand_cut = sb("cand_cut", [P, TB, TOPK * TOPK], F32, route)
        eq = sb("eq", [P, P * TOPK], F32, route)
        route.close()
        gst = sb("gst", [P, 2, KEYS, GCH], F32, peer)
        peer.close()
        late = ExitStack()
        g_in = sb("g_in", [P, 2, T // GCH, 2, GCH], F32, late)
        a_in = sb("a_in", [P, 2, 2, T], F32, late)
        wt = sb("wt", [P, 2, T], F32, late)
        wt_hi = sb("wt_hi", [P, 2, T], F32R, late)
        wt_lo = sb("wt_lo", [P, 2, T], F32R, late)
        fsq = sb("fsq", [P, NC, T], F32, late)
        late.close()

        vec_in, prm_in, x_in, bd_in, key_in, x_again = map(sem, (
            "vec_in", "prm_in", "x_in", "bd_in", "key_in", "x_again"))
        raw_full = [sem(f"raw_full{s}") for s in range(2)]
        hi_done = [sem(f"hi_done{s}") for s in range(2)]
        lo_done = [sem(f"lo_done{s}") for s in range(2)]
        mm_done = [sem(f"mm_done{s}") for s in range(2)]
        evacuated = [sem(f"evacuated{s}") for s in range(2)]
        act_stored = [sem(f"act_stored{s}") for s in range(2)]
        const_ok, iota_ok = sem("const_ok"), sem("iota_ok")
        dve_chain, act_chain = sem("dve_chain"), sem("act_chain")
        sq_done, ms_done, std_done, h_done, rhs_hi_done, rhs_done = map(sem, (
            "sq_done", "ms_done", "std_done", "h_done", "rhs_hi_done", "rhs_done"))
        dt_done, angle_done, trig_done, ab_done, cp_done = map(sem, (
            "dt_done", "angle_done", "trig_done", "ab_done", "cp_done"))
        m1_part, m1_out, k_part, k_out, m2_zero, m2_in = map(sem, (
            "m1_part", "m1_out", "k_part", "k_out", "m2_zero", "m2_in"))
        u_stored, u_in, z_done, z_read, sp_done, y_done, y_out, y_stored, y_in = map(sem, (
            "u_stored", "u_in", "z_done", "z_read", "sp_done", "y_done", "y_out", "y_stored", "y_in"))
        ypre_done, gelu_done, glu_done, gsig_done, yssm_done = map(sem, (
            "ypre_done", "gelu_done", "glu_done", "gsig_done", "yssm_done"))
        tap_done, mean_done, xc_done, csq_done, var_done, cstd_done, hn_done, silu_done = map(
            sem, ("tap_done", "mean_done", "xc_done", "csq_done", "var_done",
                  "cstd_done", "hn_done", "silu_done"))
        sq2_done, ms2_done, std2_done, xn_done, xhi_done, xn_ready = map(sem, (
            "sq2_done", "ms2_done", "std2_done", "xn_done", "xhi_done", "xn_ready"))
        s_done, s_out, top_done, key_done, sub_done, exp_done, sel_done, selT_done, selT_out, wt_part = map(sem, (
            "s_done", "s_out", "top_done", "key_done", "sub_done", "exp_done", "sel_done", "selT_done", "selT_out",
            "wt_part"))
        oh_done = [sem(f"oh_done{s}") for s in range(OH)]
        g_mm = [sem(f"g_mm{s}") for s in range(OH)]
        g_out = [sem(f"g_out{s}") for s in range(OH)]
        g_stored = [sem(f"g_stored{s}") for s in range(2)]
        ga_in = [sem(f"ga_in{s}") for s in range(2)]
        wt_done = [sem(f"wt_done{s}") for s in range(2)]
        peer_done, fin_done, fsq_done, fms_done, fstd_done, out_ready, out_stored = map(sem, (
            "peer_done", "fin_done", "fsq_done", "fms_done", "fstd_done", "out_ready", "out_stored"))

        block = ctx.enter_context(nc.Block())

        TURN_TILES = SPREAD // TB
        TILE_GROUPS = STEP_TOK // GROUP
        SLOT_USES = P // GROUP // OH
        R_WOUT, R_WQ, R_U, R_V = WOUT // 2, WQ // 2, UT // 2, VT // 2
        R_SPREAD = R_U + ALONE // 2
        R_REST = R_SPREAD + SPREAD // 2

        @block.sync
        def _(sp):
            def load(r, s):
                wait(sp, lo_done[s], r)
                sp.dma_start(raw[:, s, :], tiles[2 * r + s, :, :] if isinstance(r, int) else
                             tiles[bass.ds(r * 2 + s, 1), :, :].rearrange("a p n -> (a p) n")
                             ).then_inc(raw_full[s], 16)

            sp.dma_start(prm[:], ssm).then_inc(prm_in, 16)
            sp.dma_start(vec[:], vecs).then_inc(vec_in, 16)
            for c in range(0, NC, 4):
                sp.dma_start(xuc[:, c:c + 4, :], xT[:, c:c + 4, :]).then_inc(x_in, 16)
            load(0, 0)
            load(0, 1)
            sp.dma_start(bd[:], glu_bd).then_inc(bd_in, 16)
            sp.dma_start(keyT[:], keys).then_inc(key_in, 16)
            for r in range(1, 4):
                load(r, 0)
                load(r, 1)
            for s in range(2):
                sp.wait_ge(evacuated[s], 2)
            for q in range(GPT):
                for a in range(CT):
                    sp.dma_start(u_scr[:, :, a * GPT + q, :].rearrange("j h c -> h j c"),
                                 u_t[q * CH:(q + 1) * CH, a, :].rearrange("h (j c) -> h j c", j=SUB)
                                 ).then_inc(u_stored, 16)
            for r in range(4, R_WOUT + 1):
                load(r, 0)
                load(r, 1)
            sp.wait_ge(u_stored, 16 * GROUPS)
            sp.wait_ge(m1_part, 8)
            sp.dma_start(u_sub, u_scr.rearrange("j h g c -> (j h) g c")).then_inc(u_in, 16)
            sp.wait_ge(m2_zero, 1)
            sp.wait_ge(k_out, 8)
            for j in range(SUB):
                n = (SUB - j) * CH
                sp.dma_start(m2[j * CH:(j + 1) * CH, :, j * CH:P], kimp[0:CH, :, 0:n]).then_inc(m2_in, 16)
            sp.wait_ge(y_out, 4)
            for i in range(SUB):
                for e in range(2):
                    sp.dma_start(y_scr.rearrange("(a e) h i c -> e i h a c", e=2)[e, i],
                                 ysb[i * CH:(i + 1) * CH, e * 1024:(e + 1) * 1024].rearrange("h (a c) -> h a c", a=PAIRS)
                                 ).then_inc(y_stored, 16)
            sp.dma_start(x2[:], xT).then_inc(x_again, 16)
            sp.wait_ge(y_stored, 16 * SUB * 2)
            sp.dma_start(y_t, y_scr.rearrange("(a q) h i c -> (q h) a (i c)", a=CT)).then_inc(y_in, 16)
            for r in range(R_WOUT + 1, R_WQ + 1):
                load(r, 0)
                load(r, 1)
            with sp.Fori(0, HEADS) as it:
                for s in range(2):
                    load(it + (R_WQ + 1), s)

            def u_step(r, j, s):
                load(r + 1, s)
                sp.wait_ge(evacuated[s], r + 1)
                sp.dma_start(act_scr[j, :, :] if isinstance(j, int) else
                             act_scr[bass.ds(j, 1), :, :].rearrange("a p t -> (a p) t"),
                             act_sb[:, s, :]).then_inc(act_stored[s], 16)

            with sp.Fori(0, ALONE // 2) as it:
                for s in range(2):
                    u_step(it + R_U, it * 2 + s, s)

            def store_piece(turn, half, k):
                if k == 0:
                    for b in range(OH):
                        sp.wait_ge(g_out[b], turn * SLOT_USES + ((half + 1) * SLOT_USES // 2 + 1))
                n = KEYS // PIECES
                chunk = turn * 2 + half
                dst = gate_scr[:, chunk:chunk + 1] if isinstance(turn, int) else gate_scr[:, bass.ds(chunk, 1)]
                sp.dma_start(dst[:, :, k * n * GCH:(k + 1) * n * GCH].rearrange("p a n -> p (a n)"),
                             gst[:, half, k * n:(k + 1) * n].rearrange("p i t -> p (i t)")
                             ).then_inc(g_stored[half], 16)

            def spread_step(turn, q):
                u_step(turn * (TURN_TILES // 2) + (R_SPREAD + q // 2), turn * TURN_TILES + (ALONE + q), q % 2)
                if TURN_TILES // 2 <= q < TURN_TILES // 2 + PIECES:
                    store_piece(turn, 0, q - TURN_TILES // 2)

            for q in range(PIECES):
                spread_step(0, q)
            with sp.Fori(0, TB - 1) as it:
                for q in range(PIECES, TURN_TILES):
                    spread_step(it, q)
                for q in range(PIECES):
                    spread_step(it + 1, q)
                    store_piece(it, 1, q)
            for q in range(PIECES, TURN_TILES):
                spread_step(TB - 1, q)
            for q in range(PIECES):
                u_step(R_REST + q // 2, ALONE + SPREAD + q, q % 2)
                store_piece(TB - 1, 1, q)
            with sp.Fori(PIECES // 2, (KEYS - ALONE - SPREAD) // 2) as it:
                for s in range(2):
                    u_step(it + R_REST, it * 2 + (ALONE + SPREAD + s), s)

            for s in range(2):
                sp.wait_ge(act_stored[s], 16 * (KEYS // 2 + 1))
                sp.wait_ge(g_stored[s], 16 * PIECES * (TB + 1))
            g_rows = gate_scr.rearrange("p a (i n) -> i p a n", n=2 * GCH)
            a_rows = act_scr.rearrange("(i b) p t -> i p b t", b=2)

            def load_ga(j, s, k):
                for b in range(2):
                    wait(sp, wt_done[b], k)
                sp.dma_start(g_in[:, s].rearrange("p a b t -> p a (b t)"),
                             g_rows[bass.ds(j, 1)].rearrange("i p a n -> (i p) a n")).then_inc(ga_in[s], 16)
                sp.dma_start(a_in[:, s], a_rows[bass.ds(j, 1)].rearrange("i p b t -> (i p) b t")
                             ).then_inc(ga_in[s], 16)

            load_ga(0, 0, 0)
            load_ga(1, 1, 0)
            with sp.Fori(0, KEYS // 4 - 1) as it:
                for g in range(2):
                    load(it * 2 + (R_V + 1 + g), 0)
                    load(it * 2 + (R_V + 1 + g), 1)
                    load_ga(it * 2 + (2 + g), g, it * 2 + (1 + g))
            load(R_V + KEYS // 2 - 1, 0)
            load(R_V + KEYS // 2 - 1, 1)
            for c in range(NC):
                sp.wait_ge(out_ready, c + 1)
                sp.dma_start(outT[:, c, :], x2[:, c, :]).then_inc(out_stored, 16)
            sp.wait_ge(out_stored, 16 * NC)

        @block.gpsimd
        def _(pool):
            def split_lo(r, s):
                pool.wait_ge(hi_done[s], r + 1)
                pool.tensor_tensor(w_lo[:, s, :], raw[:, s, :], w_hi[:, s, :].bitcast(F32), ALU.subtract
                                   ).then_inc(lo_done[s], 1)

            for s in range(2):
                pool.sem_inc(act_stored[s], 16)
                pool.sem_inc(g_stored[s], 16 * PIECES)
            for b in range(OH):
                pool.sem_inc(g_out[b], 1)
                pool.sem_inc(g_mm[b], 1)
            pool.sem_inc(s_out, 1)
            pool.sem_inc(selT_out, 1)
            pool.iota(tab["kk"][:], [[0, PAIRS], [1, SUB + 1]], base=0, channel_multiplier=0,
                      allow_small_or_imprecise_dtypes=True).then_inc(iota_ok, 1)
            pool.memset(ones[:], 1.0).then_inc(const_ok, 1)
            pool.memset(epsc[:], EPS).then_inc(const_ok, 1)
            pool.memset(ident[:], 0.0).then_inc(const_ok, 1)
            pool.wait_ge(const_ok, 3)
            pool.affine_select(out=ident[:], in_=ident[:], compare_op=ALU.not_equal, fill=1.0, base=0,
                               pattern=[[-1, P]], channel_multiplier=1).then_inc(const_ok, 1)
            pool.memset(hc[:, :, 0:PAD], 0.0).then_inc(const_ok, 1)
            pool.iota(iota_row[:], [[1, P]], base=0, channel_multiplier=0,
                      allow_small_or_imprecise_dtypes=True).then_inc(const_ok, 1)
            pool.iota(iota16[:], [[1, TOPK]], base=0, channel_multiplier=0,
                      allow_small_or_imprecise_dtypes=True).then_inc(const_ok, 1)
            pool.memset(m2, 0.0).then_inc(m2_zero, 1)
            for r in range(R_WQ):
                split_lo(r, 0)
                split_lo(r, 1)
            with pool.Fori(R_WQ, NTILES // 2) as r:
                split_lo(r, 0)
                split_lo(r, 1)
            
        @block.scalar
        def _(act):
            def split_hi(r, s):
                wait(act, mm_done[s], r)
                act.wait_ge(raw_full[s], r * 16 + 16)
                act.activation(w_hi[:, s, :], raw[:, s, :], ACT.Copy).then_inc(hi_done[s], 1)

            act.wait_ge(prm_in, 16)
            act.activation(small[:, 0, :], prm[:, S_DT:S_DT + PAIRS], ACT.Exp).then_inc(dt_done, 1)
            split_hi(0, 0)
            for c in range(NC):
                act.wait_ge(x_in, 32)
                act.activation(sq[:, c, :], xuc[:, c, :], ACT.Square).then_inc(sq_done, 1)
            act.wait_ge(ms_done, 1)
            act.wait_ge(const_ok, 7)
            act.activation(rstd[:], PS[:, 2, :], ACT.Sqrt, bias=epsc[:], scale=1.0 / D).then_inc(std_done, 1)
            for c in range(NC):
                act.wait_ge(h_done, c + 1)
                act.activation(rhs_hi[:, c, :], xuc[:, c, :], ACT.Copy).then_inc(rhs_hi_done, 1)
            for n in range(CT):
                split_hi((n + 1) // 2, (n + 1) % 2)
                act.wait_ge(mm_done[n % 2], n // 2 + 1)
                act.activation(u_t[:, n, :].rearrange("p (j c) -> p c j", j=SUB),
                               PS[:, n % 2, :].rearrange("p (c j) -> p c j", j=SUB), ACT.Copy
                               ).then_inc(evacuated[n % 2], 1)
            act.wait_ge(angle_done, 1)
            act.activation(tab["mag"][:], tab["exps"][:], ACT.Exp).then_inc(trig_done, 1)
            act.activation(tab["sin"][:], tab["red"][:], ACT.Sin).then_inc(trig_done, 1)
            act.activation(tab["sinh"][:], tab["half"][:], ACT.Sin).then_inc(trig_done, 1)
            for a in range(CT):
                r = CT // 2 + a
                split_hi(r, 1)
                split_hi(r + 1, 0)
                act.wait_ge(mm_done[1], r + 1)
                if a >= 2:
                    act.wait_ge(evacuated[0], a + 1)
                act.activation(sg[:, a % 2, :], PS[:, 1, :], ACT.Sigmoid).then_inc(evacuated[1], 1)
            split_hi(R_WOUT, 1)
            for k in range(8):
                act.wait_ge(m1_part, k + 1)
                act.activation(m1[:, k // 4, (k % 4) * 4:(k % 4) * 4 + 4, :].rearrange("p a m -> p (a m)"),
                               PS[:, 4 + k % 4, :], ACT.Copy).then_inc(m1_out, 1)
            for k in range(8):
                act.wait_ge(k_part, k + 1)
                g0 = (k // 2) * 8
                act.activation(kimp[0:CH, g0:g0 + 8, :].rearrange("p (a e) m -> p e a m", e=2)[:, k % 2],
                               PS[0:CH, 4 + k % 4, :].rearrange("p (a m) -> p a m", a=4), ACT.Copy).then_inc(k_out, 1)
            act.wait_ge(y_done, 1)
            for b in range(4):
                act.activation(ysb[:, b * T:(b + 1) * T], PS[:, 4 + b, :], ACT.Copy).then_inc(y_out, 1)
            for a in range(CT):
                act.wait_ge(xc_done, a + 1)
                act.activation(hc[:, a, 0:T], cv[:, a, :], ACT.Square).then_inc(csq_done, 1)
            act.wait_ge(var_done, 1)
            act.activation(sg[:, 0, :], PS[:, 3, :], ACT.Sqrt, bias=epsc[:], scale=1.0 / T).then_inc(cstd_done, 1)
            for a in range(CT):
                act.wait_ge(ypre_done, a + 1)
                act.activation(y_t[:, a, :], y_t[:, a, :], ACT.Gelu).then_inc(gelu_done, 1)
            for a in range(CT):
                act.wait_ge(glu_done, a + 1)
                act.activation(ysb[:, a * T:(a + 1) * T], PS[:, 4 + a, :], ACT.Sigmoid,
                               bias=vec[:, V_GB + a:V_GB + a + 1]).then_inc(gsig_done, 1)
            for a in range(CT):
                act.wait_ge(hn_done, a + 1)
                act.activation(cv[:, a, :], cv[:, a, :], ACT.Silu, bias=vec[:, V_LB + a:V_LB + a + 1],
                               scale=vec[:, V_LG + a:V_LG + a + 1]).then_inc(silu_done, 1)
            for a in range(CT):
                act.wait_ge(silu_done, a + 1)
                act.activation(rhs_hi[:, CT + a, :], cv[:, a, :], ACT.Copy).then_inc(rhs_hi_done, 1)
            for a in range(CT):
                act.wait_ge(yssm_done, a + 1)
                act.activation(rhs_hi[:, a, :].rearrange("p (c i) -> p i c", i=SUB),
                               y_t[:, a, :].rearrange("p (i c) -> p i c", i=SUB), ACT.Copy
                               ).then_inc(rhs_hi_done, 1)
            for m in range(NC):
                r, s = R_WOUT + m // 2, m % 2
                split_hi(r + 1, s)
                act.wait_ge(evacuated[s], r + 1)
                act.activation(sq[:, m, :], x2[:, m, :], ACT.Square).then_inc(sq2_done, 1)
            act.wait_ge(ms2_done, 1)
            act.activation(rstd[:], PS[:, 2, :], ACT.Sqrt, bias=epsc[:], scale=1.0 / D).then_inc(std2_done, 1)
            for c in range(NC):
                act.wait_ge(xn_done, c + 1)
                act.activation(rhs_hi[:, c, :], sq[:, c, :], ACT.Copy).then_inc(xhi_done, 1)
            with act.Fori(0, HEADS) as it:
                for s in range(2):
                    act.wait_ge(mm_done[s], it + (R_WQ + 1))
                    act.activation(q_sb[:, s, :], PS[:, s, :], ACT.Copy).then_inc(evacuated[s], 1)
                    split_hi(it + (R_WQ + 1), s)
                for s in range(2):
                    act.wait_ge(s_done, it * 2 + (s + 1))
                    act.activation(s_all[:, bass.ds(it * 2 + s, 1), :].rearrange("p a t -> p (a t)"),
                                   PS[:, 4 + s, :], ACT.Copy).then_inc(s_out, 1)

            def u_step(r, k, s):
                act.wait_ge(mm_done[s], r + 1)
                act.wait_ge(act_stored[s], k * 16 + 16)
                act.activation(act_sb[:, s, :], PS[:, s, :], ACT.Gelu).then_inc(evacuated[s], 1)
                split_hi(r + 1, s)

            with act.Fori(0, EXP_AT // 2) as it:
                for s in range(2):
                    u_step(it + R_U, it, s)
            act.wait_ge(sub_done, 1)
            act.activation(sel_all[:], sel_all[:], ACT.Exp).then_inc(exp_done, 1)
            with act.Fori(EXP_AT // 2, ALONE // 2) as it:
                for s in range(2):
                    u_step(it + R_U, it, s)
            with act.Fori(0, TB) as it:
                for q in range(TURN_TILES):
                    u_step(it * (TURN_TILES // 2) + (R_SPREAD + q // 2),
                           it * (TURN_TILES // 2) + (ALONE // 2 + q // 2), q % 2)
                    half, w = q // (TURN_TILES // 2), q % (TURN_TILES // 2)
                    if w == 0:
                        act.wait_ge(g_stored[half], it * (16 * PIECES) + 16 * PIECES)
                    for b in range(TILE_GROUPS):
                        t0, o = w * STEP_TOK + b * GROUP, (q % 2) * TILE_GROUPS + b
                        act.wait_ge(g_mm[o], it * SLOT_USES + (q // 2 + 2))
                        act.activation(gst[:, half, :, t0:t0 + GROUP].rearrange("p i t -> p t i"),
                                       PS[:, 2 + o, :].rearrange("p (t i) -> p t i", t=GROUP), ACT.Copy,
                                       scale=1.0 / GSCALE).then_inc(g_out[o], 1)
            with act.Fori(0, (KEYS - ALONE - SPREAD) // 2) as it:
                for s in range(2):
                    u_step(it + R_REST, it + (ALONE + SPREAD) // 2, s)
            with act.Fori(0, KEYS // 2 - 1) as it:
                for s in range(2):
                    split_hi(it + (R_V + 1), s)
            for c in range(NC):
                act.wait_ge(fin_done, c + 1)
                act.activation(fsq[:, c, :], x2[:, c, :], ACT.Square).then_inc(fsq_done, 1)
            act.wait_ge(fms_done, 1)
            act.activation(rstd[:], PS[:, 0, :], ACT.Sqrt, bias=epsc[:], scale=1.0 / D).then_inc(fstd_done, 1)

        @block.tensor
        def _(pe):
            def product(r, s, out, last=None):
                pe.wait_ge(hi_done[s], r + 1)
                pe.wait_ge(lo_done[s], r + 1)
                for c in range(NC):
                    hi, lo = w_hi[:, s, c * P:(c + 1) * P], w_lo[:, s, c * P:(c + 1) * P]
                    pe.matmul(out, hi, rhs_hi[:, c, :], start=(c == 0), stop=False)
                    pe.matmul(out, hi, rhs_lo[:, c, :], start=False, stop=False)
                    mm = pe.matmul(out, lo, rhs_hi[:, c, :], start=False, stop=(c == NC - 1))
                mm.then_inc(mm_done[s], 1)

            def stream(r, s):
                wait(pe, evacuated[s], r)
                product(r, s, PS[:, s, :])

            pe.wait_ge(const_ok, 7)
            for c in range(NC):
                pe.wait_ge(sq_done, c + 1)
                mm = pe.matmul(PS[:, 2, :], ones[:], sq[:, c, :], start=(c == 0), stop=(c == NC - 1))
            mm.then_inc(ms_done, 1)
            pe.wait_ge(rhs_done, NC)
            for r in range(R_WOUT):
                stream(r, 0)
                stream(r, 1)
            for k in range(8):
                pe.wait_ge(ab_done, 1)
                if k >= 4:
                    pe.wait_ge(m1_out, k - 3)
                for a in range(4):
                    src = (ab_r, ab_i)[k // 4][:, (k % 4) * 4 + a].rearrange("p j h -> p (j h)")
                    mm = pe.transpose(PS[:, 4 + k % 4, a * P:(a + 1) * P], src, ident[:])
                mm.then_inc(m1_part, 1)
            for k in range(8):
                pe.wait_ge(cp_done, 1)
                pe.wait_ge(m1_out if k < 4 else k_out, 5 + k if k < 4 else k - 3)
                for w in range(4):
                    a, rows = (k // 2) * 4 + w, slice((k % 2) * STATE, (k % 2 + 1) * STATE)
                    for ri, (b0, cp) in enumerate(((S_BR, cp_r), (S_BI, cp_i))):
                        mm = pe.matmul(PS[0:CH, 4 + k % 4, w * P:(w + 1) * P],
                                       prm[rows, b0 + a * CH:b0 + (a + 1) * CH],
                                       cp[rows, a, 0:SUB, :].rearrange("p k h -> p (k h)"),
                                       start=(ri == 0), stop=(ri == 1))
                mm.then_inc(k_part, 1)
            pe.wait_ge(u_in, 16)
            pe.wait_ge(k_out, 8)
            for ri in range(2):
                for g in range(GROUPS):
                    a, rows = g // 2, slice((g % 2) * STATE, (g % 2 + 1) * STATE)
                    mm = pe.matmul(PS[rows, 4 + 2 * ri + a // 8, (a % 8) * NSUB:(a % 8 + 1) * NSUB],
                                   m1[:, ri, a, rows], u_sub[:, g, :], start=True, stop=True)
            mm.then_inc(z_done, 1)
            pe.wait_ge(m2_in, 16 * SUB)
            pe.wait_ge(sp_done, 1)
            for g in range(GROUPS):
                a, rows = g // 2, slice((g % 2) * STATE, (g % 2 + 1) * STATE)
                out = PS[:, 4 + 2 * (g % 2) + a // 8, (a % 8) * NSUB:(a % 8 + 1) * NSUB]
                pe.matmul(out, m2[:, g, :], u_sub[:, g, :], start=True, stop=False)
                pe.matmul(out, cp_r[rows, a, 1:SUB + 1, :].rearrange("p k h -> p (k h)"),
                          sp_r[rows, a, 0:NSUB], start=False, stop=False)
                mm = pe.matmul(out, cp_i[rows, a, 1:SUB + 1, :].rearrange("p k h -> p (k h)"),
                               sp_i[rows, a, 0:NSUB], start=False, stop=True)
            mm.then_inc(y_done, 1)
            for a in range(CT):
                pe.wait_ge(tap_done, CT * WIDTH)
                mm = pe.matmul(PS[:, 2, :], ones[:], cv[:, a, :], start=(a == 0), stop=(a == CT - 1))
            mm.then_inc(mean_done, 1)
            for a in range(CT):
                pe.wait_ge(csq_done, a + 1)
                mm = pe.matmul(PS[:, 3, :], ones[:], hc[:, a, 0:T], start=(a == 0), stop=(a == CT - 1))
            mm.then_inc(var_done, 1)
            pe.wait_ge(bd_in, 16)
            pe.wait_ge(y_out, 4)
            for a in range(CT):
                pe.wait_ge(gelu_done, a + 1)
                pe.matmul(PS[:, 4 + a, :], bd[:, a, :], y_t[:, a, :], start=True, stop=True).then_inc(glu_done, 1)
            pe.wait_ge(rhs_done, 2 * NC)
            for r in range(R_WOUT, R_WQ):
                stream(r, 0)
                stream(r, 1)
            for c in range(NC):
                pe.wait_ge(sq2_done, c + 1)
                mm = pe.matmul(PS[:, 2, :], ones[:], sq[:, c, :], start=(c == 0), stop=(c == NC - 1))
            mm.then_inc(ms2_done, 1)
            pe.wait_ge(xn_ready, NC)
            pe.wait_ge(key_in, 16)
            with pe.Fori(0, HEADS) as it:
                for s in range(2):
                    stream(it + R_WQ, s)
                for s in range(2):
                    pe.wait_ge(evacuated[s], it + (R_WQ + 1))
                    pe.wait_ge(s_out, it * 2 + 1)
                    for b in range(TB):
                        mm = pe.matmul(PS[:, 4 + s, b * P:(b + 1) * P], q_sb[:, s, b * P:(b + 1) * P],
                                       keyT[:, s, :], start=True, stop=True)
                    mm.then_inc(s_done, 1)
            with pe.Fori(0, ALONE // 2) as it:
                for s in range(2):
                    stream(it + R_U, s)
            with pe.Fori(0, TB) as it:
                pe.wait_ge(sel_done, it + 1)
                pe.wait_ge(selT_out, it * 2 + 1)
                for k in range(3):
                    mm = pe.transpose(PS[:, 6, k * P:(k + 1) * P], sel_now[:, k, :], ident[:])
                mm.then_inc(selT_done, 1)
                for q in range(TURN_TILES):
                    stream(it * (TURN_TILES // 2) + (R_SPREAD + q // 2), q % 2)
                    for b in range(TILE_GROUPS):
                        n, o = it * SLOT_USES + q // 2, (q % 2) * TILE_GROUPS + b
                        pe.wait_ge(oh_done[o], n + 1)
                        pe.wait_ge(g_out[o], n + 1)
                        for t in range(GROUP):
                            out = PS[:, 2 + o, t * P:(t + 1) * P]
                            pe.matmul(out, oh_1[:, o, t, :], oh_gh[:, o, t, :], start=True, stop=False)
                            mm = pe.matmul(out, oh_1[:, o, t, :], oh_gl[:, o, t, :], start=False, stop=True)
                        mm.then_inc(g_mm[o], 1)
            with pe.Fori(0, (KEYS - ALONE - SPREAD) // 2) as it:
                for s in range(2):
                    stream(it + R_REST, s)

            def v_step(r, k, s, first, last):
                pe.wait_ge(hi_done[s], r + 1)
                pe.wait_ge(lo_done[s], r + 1)
                pe.wait_ge(wt_done[s], k + 1)
                for m in range(NC):
                    hi, lo = w_hi[:, s, m * P:(m + 1) * P], w_lo[:, s, m * P:(m + 1) * P]
                    pe.matmul(PS[:, m, :], hi, wt_hi[:, s, :], start=first, stop=False, skip_group_check=True)
                    pe.matmul(PS[:, m, :], hi, wt_lo[:, s, :], start=False, stop=False, skip_group_check=True)
                    mm = pe.matmul(PS[:, m, :], lo, wt_hi[:, s, :], start=False, stop=last, skip_group_check=True)
                    if last:
                        mm.then_inc(peer_done, 1)
                if not last:
                    mm.then_inc(mm_done[s], 1)

            for s in range(2):
                pe.wait_ge(evacuated[s], R_V)
                pe.wait_ge(g_out[s], TB * SLOT_USES + 1)
                pe.wait_ge(g_out[s + 2], TB * SLOT_USES + 1)
            for s in range(2):
                v_step(R_V, 0, s, s == 0, False)
            with pe.Fori(0, KEYS // 2 - 2) as it:
                for s in range(2):
                    v_step(it + (R_V + 1), it + 1, s, False, False)
            for s in range(2):
                v_step(R_V + KEYS // 2 - 1, KEYS // 2 - 1, s, False, s == 1)
            for c in range(NC):
                pe.wait_ge(fsq_done, c + 1)
                mm = pe.matmul(PS[:, 0, :], ones[:], fsq[:, c, :], start=(c == 0), stop=(c == NC - 1))
            mm.then_inc(fms_done, 1)

        @block.vector
        def _(dve):
            ch = Chain(dve, dve_chain)
            step = ch.step
            tt, ts, stt = dve.tensor_tensor, dve.tensor_scalar, dve.scalar_tensor_tensor
            dt, lrdt, lidt, den, fr, fi, t1, t2, nr = (small[:, i, :] for i in range(9))
            lr, li = prm[:, S_LR:S_LR + PAIRS], prm[:, S_LI:S_LI + PAIRS]

            def per_k(x):
                return x.rearrange("p (a k) -> p a k", k=1).broadcast_to([P, PAIRS, SUB + 1])

            dve.wait_ge(dt_done, 1)
            dve.wait_ge(iota_ok, 1)
            tt(lrdt, lr, dt, ALU.mult)
            step(tt(lidt, li, dt, ALU.mult))
            tt(tab["exps"][:], per_k(lrdt), tab["kk"][:], ALU.mult)
            step(tt(tab["phi"][:], per_k(lidt), tab["kk"][:], ALU.mult))
            step(ts(tab["turns"][:], tab["phi"][:], 0.15915494309189535, MAGIC, ALU.mult, ALU.add))
            step(ts(tab["turns"][:], tab["turns"][:], -MAGIC, None, ALU.add))
            step(stt(tab["red"][:], tab["turns"][:], -TWO_PI[0], tab["phi"][:], ALU.mult, ALU.add))
            step(stt(tab["phi"][:], tab["turns"][:], -TWO_PI[1], tab["red"][:], ALU.mult, ALU.add))
            step(stt(tab["red"][:], tab["turns"][:], -TWO_PI[2], tab["phi"][:], ALU.mult, ALU.add))
            step(ts(tab["red"][:], tab["red"][:], PI_IN, -PI_IN, ALU.min, ALU.max))
            ts(tab["half"][:], tab["red"][:], 0.5, None, ALU.mult).then_inc(angle_done, 1)
            dve.wait_ge(vec_in, 16)
            dve.wait_ge(std_done, 1)
            step(dve.reciprocal(rstd[:], rstd[:]))

            def scale_rows(dst, src, g0, done):
                for c in range(NC):
                    stt(dst[:, c, :], src[:, c, :], vec[:, g0 + c:g0 + c + 1], rstd[:], ALU.mult, ALU.mult
                        ).then_inc(done, 1)

            dve.wait_ge(x_in, 32)
            scale_rows(xuc, xuc, V_G1, h_done)
            for c in range(NC):
                dve.wait_ge(rhs_hi_done, c + 1)
                tt(rhs_lo[:, c, :], xuc[:, c, :], rhs_hi[:, c, :].bitcast(F32), ALU.subtract).then_inc(rhs_done, 1)

            dve.wait_ge(trig_done, 3)
            step(tt(tab["cos"][:], tab["sinh"][:], tab["sinh"][:], ALU.mult))
            step(ts(tab["cos"][:], tab["cos"][:], -2.0, 1.0, ALU.mult, ALU.add))
            tt(tab["pr"][:], tab["mag"][:], tab["cos"][:], ALU.mult)
            step(tt(tab["pi"][:], tab["mag"][:], tab["sin"][:], ALU.mult))
            a_i = tab["pi"][:, :, 1]
            ts(nr, tab["pr"][:, :, 1], -1.0, None, ALU.add)
            tt(t1, lr, lr, ALU.mult)
            step(tt(t2, li, li, ALU.mult))
            step(tt(den, t1, t2, ALU.add))
            dve.reciprocal(den, den)
            tt(t1, nr, lr, ALU.mult)
            step(tt(t2, a_i, li, ALU.mult))
            tt(fr, t1, t2, ALU.add)
            step(tt(small[:, 9, :], a_i, lr, ALU.mult))
            step(tt(small[:, 10, :], nr, li, ALU.mult))
            step(tt(fi, small[:, 9, :], small[:, 10, :], ALU.subtract))
            tt(fr, fr, den, ALU.mult)
            step(tt(fi, fi, den, ALU.mult))
            tt(tab["fpr"][:], per_k(fr), tab["pr"][:], ALU.mult)
            step(tt(tab["t9"][:], per_k(fi), tab["pi"][:], ALU.mult))
            step(tt(tab["fpr"][:], tab["fpr"][:], tab["t9"][:], ALU.subtract))
            tt(tab["fpi"][:], per_k(fr), tab["pi"][:], ALU.mult)
            step(tt(tab["t9"][:], per_k(fi), tab["pr"][:], ALU.mult))
            tt(tab["fpi"][:], tab["fpi"][:], tab["t9"][:], ALU.add)
            for j in range(SUB):
                dve.tensor_copy(rev_r[:, :, j], tab["pr"][:, :, SUB - 1 - j])
                ins = dve.tensor_copy(rev_i[:, :, j], tab["pi"][:, :, SUB - 1 - j])
            step(ins)

            def outer(k, x):
                n = k.shape[-1]
                return (k.rearrange("p a (k o) -> p a k o", o=1).broadcast_to([P, PAIRS, n, CH]),
                        x.rearrange("p (a o h) -> p a o h", a=PAIRS, o=1).broadcast_to([P, PAIRS, n, CH]))

            def cols(c0):
                return prm[:, c0:c0 + PAIRS * CH]

            t8 = tmp[:, 0:PAIRS * SUB * CH].rearrange("p (a k h) -> p a k h", a=PAIRS, k=SUB)
            t9 = tmp.rearrange("p (a k h) -> p a k h", a=PAIRS, k=SUB + 1)
            flat = "p a k h -> p (a k h)"
            dve.wait_ge(ms_done, 1)
            tt(ab_r, *outer(rev_r[:], cols(S_BR)), ALU.mult)
            step(tt(t8, *outer(rev_i[:], cols(S_BI)), ALU.mult))
            step(tt(ab_r, ab_r, t8, ALU.subtract))
            tt(ab_i, *outer(rev_r[:], cols(S_BI)), ALU.mult)
            step(tt(t8, *outer(rev_i[:], cols(S_BR)), ALU.mult))
            tt(ab_i, ab_i, t8, ALU.add).then_inc(ab_done, 1)
            dve.wait_ge(ab_done, 1)
            tt(cp_r[:], *outer(tab["fpr"][:], cols(S_CR)), ALU.mult)
            step(tt(t9, *outer(tab["fpi"][:], cols(S_CI)), ALU.mult))
            step(tt(cp_r[:], cp_r[:], t9, ALU.subtract))
            tt(cp_i[:], *outer(tab["fpr"][:], cols(S_CI)), ALU.mult)
            step(tt(t9, *outer(tab["fpi"][:], cols(S_CR)), ALU.mult))
            stt(cp_i[:].rearrange(flat), cp_i[:].rearrange(flat), -1.0, tmp, ALU.mult, ALU.subtract
                ).then_inc(cp_done, 1)
            dve.memset(rot_r[:, :, 0:1], 1.0)
            dve.memset(rot_i[:, :, 0:1], 0.0)
            dve.tensor_copy(rot_r[:, :, 1:2], tab["cos"][:, :, SUB:SUB + 1])
            step(dve.tensor_copy(rot_i[:, :, 1:2], tab["sin"][:, :, SUB:SUB + 1]))
            dve.wait_ge(cp_done, 1)
            n = 1
            while n < NSUB:
                lo, hi = slice(1, n + 1), slice(n + 1, 2 * n + 1)
                wr = rot_r[:, :, n:n + 1].broadcast_to([P, PAIRS, n])
                wi = rot_i[:, :, n:n + 1].broadcast_to([P, PAIRS, n])
                ta = hc[:, 0, PAD:PAD + PAIRS * n].rearrange("p (a k) -> p a k", a=PAIRS)
                tb = hc[:, 1, PAD:PAD + PAIRS * n].rearrange("p (a k) -> p a k", a=PAIRS)
                tt(rot_r[:, :, hi], rot_r[:, :, lo], wr, ALU.mult)
                tt(ta, rot_i[:, :, lo], wi, ALU.mult)
                tt(rot_i[:, :, hi], rot_r[:, :, lo], wi, ALU.mult)
                step(tt(tb, rot_i[:, :, lo], wr, ALU.mult))
                tt(rot_r[:, :, hi], rot_r[:, :, hi], ta, ALU.subtract)
                step(tt(rot_i[:, :, hi], rot_i[:, :, hi], tb, ALU.add))
                n *= 2

            for a in range(CT):
                r = CT // 2 + a
                dve.wait_ge(mm_done[0], r + 1)
                dve.wait_ge(evacuated[1], r + 1)
                tt(hc[:, a, PAD:PAD + T], PS[:, 0, :], sg[:, a % 2, :], ALU.mult).then_inc(evacuated[0], 1)
                dve.wait_ge(evacuated[0], r + 1)
                if a == 0:
                    dve.wait_ge(const_ok, 7)
                ts(cv[:, a, :], hc[:, a, 0:T], vec[:, V_CW + a * WIDTH:V_CW + a * WIDTH + 1],
                   vec[:, V_CB + a:V_CB + a + 1], ALU.mult, ALU.add).then_inc(tap_done, 1)
            with dve.Fori(0, WIDTH - 1) as k:
                for a in range(CT):
                    dve.wait_ge(tap_done, k * CT + (a + 1))
                    w = vec[:, bass.ds(k + (V_CW + a * WIDTH + 1), 1)]
                    stt(cv[:, a, :], hc[:, a, bass.ds(k + 1, T)], w, cv[:, a, :], ALU.mult, ALU.add
                        ).then_inc(tap_done, 1)
            dve.wait_ge(tap_done, CT * WIDTH)

            dve.wait_ge(z_done, 1)
            dve.wait_ge(m2_in, 16 * SUB)
            z_r = PS[:, 4:6, :].rearrange("p b (a c) -> p (b a) c", a=8)
            z_i = PS[:, 6:8, :].rearrange("p b (a c) -> p (b a) c", a=8)
            v3 = lambda x: x.rearrange("p (a c) -> p a c", a=PAIRS)
            rr, ri = rot_r[:, :, 0:NSUB], rot_i[:, :, 0:NSUB]
            tt(v3(za), z_r, rr, ALU.mult)
            step(tt(v3(zt), z_i, ri, ALU.mult))
            step(tt(za, za, zt, ALU.add))
            tt(v3(zb), z_i, rr, ALU.mult)
            step(tt(v3(zt), z_r, ri, ALU.mult))
            step(tt(zb, zb, zt, ALU.subtract))
            dve.tensor_copy(v3(zt), tab["mag"][:, :, SUB:SUB + 1].broadcast_to([P, PAIRS, NSUB]))
            step(dve.memset(small[:, 11, :], 0.0))
            step(dve.tensor_copy(v3(zt)[:, :, 0], small[:, 11, :]))
            step(dve.tensor_tensor_scan(zc, zt, za, 0.0, ALU.mult, ALU.add))
            step(dve.tensor_tensor_scan(za, zt, zb, 0.0, ALU.mult, ALU.add))
            dve.tensor_copy(sp_r[:, :, 0], small[:, 11, :])
            dve.tensor_copy(sp_i[:, :, 0], small[:, 11, :])
            tt(v3(zb), v3(zc), rr, ALU.mult)
            step(tt(v3(zt), v3(za), ri, ALU.mult))
            tt(sp_r[:, :, 1:NSUB + 1], v3(zb), v3(zt), ALU.subtract)
            step(tt(sp_i[:, :, 1:NSUB + 1], v3(zc), ri, ALU.mult))
            step(tt(v3(zb), v3(za), rr, ALU.mult))
            tt(sp_i[:, :, 1:NSUB + 1], sp_i[:, :, 1:NSUB + 1], v3(zb), ALU.add).then_inc(sp_done, 1)

            dve.wait_ge(mean_done, 1)
            step(ts(sg[:, 1, :], PS[:, 2, :], 1.0 / (CT * P), None, ALU.mult))
            for a in range(CT):
                tt(cv[:, a, :], cv[:, a, :], sg[:, 1, :], ALU.subtract).then_inc(xc_done, 1)
            dve.wait_ge(cstd_done, 1)
            step(dve.reciprocal(sg[:, 0, :], sg[:, 0, :]))
            for a in range(CT):
                dve.wait_ge(csq_done, a + 1)
                dve.wait_ge(xc_done, a + 1)
                tt(cv[:, a, :], cv[:, a, :], sg[:, 0, :], ALU.mult).then_inc(hn_done, 1)
            dve.wait_ge(y_in, 16)
            for a in range(CT):
                stt(y_t[:, a, :], u_t[:, a, :], vec[:, V_D + a:V_D + a + 1], y_t[:, a, :], ALU.mult, ALU.add
                    ).then_inc(ypre_done, 1)
            for a in range(CT):
                dve.wait_ge(gsig_done, a + 1)
                tt(y_t[:, a, :], y_t[:, a, :], ysb[:, a * T:(a + 1) * T], ALU.mult).then_inc(yssm_done, 1)
            for a in range(CT):
                dve.wait_ge(rhs_hi_done, NC + a + 1)
                tt(rhs_lo[:, CT + a, :], cv[:, a, :], rhs_hi[:, CT + a, :].bitcast(F32), ALU.subtract
                   ).then_inc(rhs_done, 1)
            for a in range(CT):
                dve.wait_ge(rhs_hi_done, NC + CT + a + 1)
                order = "p (c i) -> p i c"
                tt(rhs_lo[:, a, :].rearrange(order, i=SUB), y_t[:, a, :].rearrange("p (i c) -> p i c", i=SUB),
                   rhs_hi[:, a, :].bitcast(F32).rearrange(order, i=SUB), ALU.subtract).then_inc(rhs_done, 1)
            dve.wait_ge(x_again, 16)
            for m in range(NC):
                r, s = R_WOUT + m // 2, m % 2
                dve.wait_ge(mm_done[s], r + 1)
                tt(x2[:, m, :], PS[:, s, :], x2[:, m, :], ALU.add).then_inc(evacuated[s], 1)
            dve.wait_ge(std2_done, 1)
            step(dve.reciprocal(rstd[:], rstd[:]))
            scale_rows(sq, x2, V_G2, xn_done)
            for c in range(NC):
                dve.wait_ge(xhi_done, c + 1)
                tt(rhs_lo[:, c, :], sq[:, c, :], rhs_hi[:, c, :].bitcast(F32), ALU.subtract).then_inc(xn_ready, 1)

            blocks = range(TB)
            halves = [(h, b) for h in range(2) for b in blocks]
            STAGES = 11
            with dve.Fori(0, HEADS) as it:
                n = 0

                def stage(ins):
                    nonlocal n
                    n += 1
                    ins.then_inc(top_done, 1)
                    dve.wait_ge(top_done, it * STAGES + n)
                    dve.tensor_copy(gsum[:, 1, 0:1], epsc[:])

                def top16(v, i, src, cut):
                    rows = range(len(v))
                    for j in rows:
                        ins = dve.max(v[j][:, 0:8], src[j])
                    stage(ins)
                    for j in rows:
                        dve.max_index(i[j][:, 0:8], v[j][:, 0:8], src[j])
                        ins = dve.match_replace(cut[j], v[j][:, 0:8], src[j], NEG)
                    stage(ins)
                    for j in rows:
                        ins = dve.max(v[j][:, 8:16], cut[j])
                    stage(ins)
                    for j in rows:
                        ins = dve.max_index(i[j][:, 8:16], v[j][:, 8:16], cut[j])
                    stage(ins)

                dve.wait_ge(s_out, it * 2 + 3)
                stage(dve.tensor_copy(s_cur[:].rearrange("p a b n -> p a (b n)"), s_all[:, bass.ds(it * 2, 2), :]))
                top16([topv[:, h, b, :] for h, b in halves], [topi[:, h, b, :] for h, b in halves],
                      [s_cur[:, h, b, :] for h, b in halves], [s_cut[:, h, b, :] for h, b in halves])
                for k, dst in enumerate((i1_all, i2_all)):
                    dve.tensor_copy(dst[:, :, bass.ds(it, 1), :].rearrange("p b o k -> p b (o k)"), topi[:, k])
                for b in blocks:
                    ins = tt(cand[:, b, :].rearrange("p (i j) -> p i j", i=TOPK),
                             topv[:, 0, b, :].rearrange("p (i j) -> p i j", j=1).broadcast_to([P, TOPK, TOPK]),
                             topv[:, 1, b, :].rearrange("p (i j) -> p i j", i=1).broadcast_to([P, TOPK, TOPK]),
                             ALU.add)
                stage(ins)
                top16([selv[:, b, :] for b in blocks], [seli[:, b, :] for b in blocks],
                      [cand[:, b, :] for b in blocks], [cand_cut[:, b, :] for b in blocks])
                dve.tensor_copy(sel_all[:, :, bass.ds(it, 1), :].rearrange("p b o k -> p b (o k)"), selv[:])
                stage(dve.tensor_copy(ci_all[:, :, bass.ds(it, 1), :].rearrange("p b o k -> p b (o k)"), seli[:]))
            scores = sel_all[:].rearrange("p b h k -> p (b h) k")
            per_head = lambda x: x.rearrange("p (n o) -> p n o", o=1).broadcast_to([P, TB * HEADS, TOPK])
            step(dve.tensor_copy(gsum[:, 0, :], scores[:, :, 0]))
            tt(scores, scores, per_head(gsum[:, 0, :]), ALU.subtract).then_inc(sub_done, 1)
            ci = ci_all[:].rearrange("p b h k -> p b (h k)")
            step(ts(pos[:], ci, 4, None, ALU.logical_shift_right))
            step(dve.tensor_copy(pos_a[:], pos[:]))
            step(ts(pos[:], ci, TOPK - 1, None, ALU.bitwise_and))
            step(dve.tensor_copy(pos_b[:], pos[:]))
            eq3 = eq[:].rearrange("p (n j) -> p n j", j=TOPK)
            eq4 = eq[:].rearrange("p (h k j) -> p h k j", h=HEADS, k=TOPK)
            with dve.Fori(0, TB) as it:
                for k, (where, idx, dst) in enumerate(((pos_a, i1_all, e1), (pos_b, i2_all, e2))):
                    w = where[:, bass.ds(it, 1), :].rearrange("p b (n o) -> p (b n) o", o=1)
                    tt(eq3, w.broadcast_to([P, P, TOPK]),
                       iota16[:].rearrange("p (n j) -> p n j", n=1).broadcast_to([P, P, TOPK]), ALU.is_equal
                       ).then_inc(key_done, 1)
                    dve.wait_ge(key_done, it * 6 + (3 * k + 1))
                    i4 = idx[:, bass.ds(it, 1), :, :].rearrange("p b h (o j) -> p (b h) o j", o=1)
                    tt(eq4, eq4, i4.broadcast_to([P, HEADS, TOPK, TOPK]), ALU.mult).then_inc(key_done, 1)
                    dve.wait_ge(key_done, it * 6 + (3 * k + 2))
                    dve.tensor_reduce(dst[:, bass.ds(it, 1), :].rearrange("p b n -> p (b n)"), eq3, AX_X, ALU.add
                                      ).then_inc(key_done, 1)
                    dve.wait_ge(key_done, it * 6 + (3 * k + 3))
            dve.wait_ge(exp_done, 1)
            step(dve.tensor_reduce(gsum[:, 0, :], scores, AX_X, ALU.add))
            step(dve.reciprocal(gsum[:, 1, :], gsum[:, 0, :]))
            step(tt(scores, scores, per_head(gsum[:, 1, :]), ALU.mult))
            dve.tensor_copy(iota_h[:], iota_row[:])
            with dve.Fori(0, TB) as it:
                for k, src in enumerate((e1, e2, sel_all)):
                    view = src[:] if k < 2 else src[:].rearrange("p b h k -> p b (h k)")
                    ins = dve.tensor_copy(sel_now[:, k, :], view[:, bass.ds(it, 1), :].rearrange("p a n -> p (a n)"))
                ins.then_inc(sel_done, 1)
                dve.wait_ge(selT_done, it + 1)
                dve.tensor_copy(e1T[:], PS[:, 6, 0:P])
                dve.tensor_copy(e2T[:], PS[:, 6, P:2 * P])
                ts(gT[:], PS[:, 6, 2 * P:3 * P], GSCALE, None, ALU.mult)
                ts(ghT[:], PS[:, 6, 2 * P:3 * P], GSCALE, None, ALU.mult).then_inc(selT_out, 1)
                dve.wait_ge(selT_out, it * 2 + 2)
                dve.tensor_copy(ghTf[:], ghT[:])
                tt(glT[:], gT[:], ghT[:], ALU.subtract).then_inc(selT_out, 1)
                dve.wait_ge(selT_out, it * 2 + 3)
                for q in range(TURN_TILES):
                    for b in range(TILE_GROUPS):
                        o = (q % 2) * TILE_GROUPS + b
                        dve.wait_ge(g_mm[o], it * SLOT_USES + (q // 2 + 1))
                        for t in range(GROUP):
                            col = slice(q * STEP_TOK + b * GROUP + t, q * STEP_TOK + b * GROUP + t + 1)
                            ts(oh_1[:, o, t, :], iota_h[:], e1T[:, col], None, ALU.is_equal)
                            ts(oh_gh[:, o, t, :], iota_h[:], e2T[:, col], ghTf[:, col], ALU.is_equal, ALU.mult)
                            ins = ts(oh_gl[:, o, t, :], iota_h[:], e2T[:, col], glT[:, col],
                                     ALU.is_equal, ALU.mult)
                        ins.then_inc(oh_done[o], 1)
            with dve.Fori(0, KEYS // 4) as it:
                for g in range(2):
                    dve.wait_ge(ga_in[g], it * 32 + 32)
                    for s in range(2):
                        dve.wait_ge(mm_done[s], it * 2 + (R_V + g))
                        n = it * 8 + (4 * g + 2 * s)
                        tt(wt[:, s, :].rearrange("p (a t) -> p a t", t=GCH),
                           a_in[:, g, s, :].rearrange("p (a t) -> p a t", t=GCH), g_in[:, g, :, s, :], ALU.mult
                           ).then_inc(wt_part, 1)
                        dve.wait_ge(wt_part, n + 1)
                        dve.tensor_copy(wt_hi[:, s, :], wt[:, s, :]).then_inc(wt_part, 1)
                        dve.wait_ge(wt_part, n + 2)
                        tt(wt_lo[:, s, :], wt[:, s, :], wt_hi[:, s, :].bitcast(F32), ALU.subtract
                           ).then_inc(wt_done[s], 1)
            for m in range(NC):
                dve.wait_ge(peer_done, m + 1)
                tt(x2[:, m, :], PS[:, m, :], x2[:, m, :], ALU.add).then_inc(fin_done, 1)
            dve.wait_ge(fstd_done, 1)
            step(dve.reciprocal(rstd[:], rstd[:]))
            scale_rows(x2, x2, V_GF, out_ready)


def kernel(**inputs):
    import concourse.bacc as bacc
    from concourse.bass_utils import run_bass_kernel_spmd

    a = {k: np.asarray(v) for k, v in inputs.items()}
    layer = {k: v[0] for k, v in a.items() if k not in ("x", "final_g")}

    def channels(v):
        return v.reshape(-1, P).T

    def states(v):
        return v.reshape(PAIRS, 2, STATE, -1).transpose(1, 2, 0, 3).reshape(P, -1)

    cw = layer["conv_w"].T.reshape(CT, P, WIDTH).transpose(1, 0, 2).reshape(P, -1)
    vecs = np.concatenate([channels(layer["norm1_g"]), channels(layer["norm2_g"]), channels(a["final_g"]),
                           channels(layer["conv_b"]), channels(layer["conv_ln_g"]), channels(layer["conv_ln_b"]),
                           channels(layer["ssm_d"]), channels(layer["glu_b"]), cw], axis=1)
    log_dt = np.broadcast_to(layer["log_dt"][:, None], (GROUPS, STATE))
    ssm = np.concatenate([states(layer["lam_re"]), states(layer["lam_im"]), states(log_dt),
                          states(layer["ssm_b_re"]), states(layer["ssm_b_im"]),
                          states(layer["ssm_c_re"].transpose(0, 2, 1)),
                          states(layer["ssm_c_im"].transpose(0, 2, 1))], axis=1)
    xT = a["x"][0].T.reshape(NC, P, T).transpose(1, 0, 2)
    glu_bd = np.zeros((P, CT, P), np.float32)
    for g in range(GROUPS):
        q = g % GPT
        glu_bd[q * CH:(q + 1) * CH, g // GPT, q * CH:(q + 1) * CH] = layer["glu_w"][g]
    keys = np.stack([layer["peer_k1"].T, layer["peer_k2"].T], axis=1)

    def columns(w):
        return w.reshape(NC, P, -1, P).transpose(2, 1, 0, 3).reshape(-1, P, D)

    w_in = columns(layer["w_in"])
    order = [0, 1, 2, 3] + [i for a4 in range(CT) for i in (CT + a4, 2 * CT + a4)]
    u = layer["peer_u"].reshape(KEYS, KEYS, NC, P).transpose(1, 3, 2, 0).reshape(KEYS, P, D)
    v = layer["peer_v"].reshape(KEYS, KEYS, D).transpose(1, 0, 2)
    tiles = np.concatenate([w_in[order], columns(layer["w_out"]), columns(layer["peer_wq"]), u, v])

    nc = bacc.Bacc("TRN2", target_bir_lowering=False, num_devices=1)
    arrays, args = {}, []
    for name, arr in (("vecs", vecs), ("ssm", ssm), ("xT", xT), ("glu_bd", glu_bd), ("keys", keys),
                      ("tiles", tiles)):
        arrays[name] = np.ascontiguousarray(arr)
        args.append(nc.dram_tensor(name, arrays[name].shape, F32, kind="ExternalInput").ap())
    outT = nc.dram_tensor("outT", (P, NC, T), F32, kind="ExternalOutput").ap()
    build(nc, *args, outT)
    result = run_bass_kernel_spmd(nc, [arrays], core_ids=[0])
    got = result.results[0]["outT"]
    return got.transpose(1, 0, 2).reshape(D, T).T[None]
```

```python
from contextlib import ExitStack

import numpy as np

import concourse.bass as bass
from concourse import mybir

F32 = mybir.dt.float32
F32R = mybir.dt.float32r
F16 = mybir.dt.float16
U32 = mybir.dt.uint32
ALU = mybir.AluOpType
ACT = mybir.ActivationFunctionType
AX_X = mybir.AxisListType.X

P = 128
D = 1024
T = 512
NC = D // P
GROUPS, CH, STATE = 32, 16, 64
PAIRS = GROUPS // 2
SUB = P // CH
NSUB = T // SUB
CT = 4
GPT = GROUPS // CT
WIDTH = 31
DCT = 3
DIAGS = 8
PAD = WIDTH - 1
HEADS, KEYS, TOPK = 8, 128, 16
TB = T // P
EPS = 1e-6

WIN, WOUT, WQ = 0, 12, 20
UT = WQ + 2 * HEADS
VT = UT + KEYS
NTILES = VT + KEYS

ALONE = 32
STEP_TOK = 8
SPREAD = T // STEP_TOK
GROUP = 4
GCH = 64
PIECES = 4
OH = 4
GSCALE = 16384.0
MEAN_AT = 8
GLU_AT = 3
SCAN_AT = 13
EXP_AT = 18

V_G1, V_G2, V_GF, V_CB, V_LG, V_LB, V_D, V_GB, V_CW = 0, 8, 16, 24, 28, 32, 36, 40, 44
NV = V_CW + CT * WIDTH
S_LR, S_LI, S_DT, S_BR, S_BI, S_CR, S_CI = 0, 16, 32, 48, 304, 560, 816
NS = 1072
NEG = -3.0e38
TWO_PI = (6.28125, 0.0019350051879882812, 3.019916050e-07)
MAGIC = 12582912.0
PI_IN = 3.1415925


def wait(eng, sem, value):
    if not (isinstance(value, int) and value <= 0):
        eng.wait_ge(sem, value)


class Chain:

    def __init__(self, eng, sem):
        self.eng, self.sem, self.n = eng, sem, 0

    def step(self, ins):
        ins.then_inc(self.sem, 1)
        self.n += 1
        self.eng.wait_ge(self.sem, self.n)


def build(nc, vecs, ssm, xT, glu_bd, keys, tiles, outT):
    with ExitStack() as ctx:
        def sb(name, shape, dt=F32, c=ctx):
            return c.enter_context(nc.sbuf_tensor(name, shape, dt))

        def sem(name):
            return ctx.enter_context(nc.semaphore(name))

        vec = sb("vec", [P, NV])
        ones = sb("ones", [P, P])
        ident = sb("ident", [P, P])
        iota_row = sb("iota_row", [P, P])
        iota16 = sb("iota16", [P, TOPK])
        epsc = sb("epsc", [P, 1])
        gelu_warm = sb("gelu_warm", [P, 1])
        rstd = sb("rstd", [P, T])
        x2 = sb("x2", [P, NC, T])
        rhs_hi = sb("rhs_hi", [P, NC, T], F32R)
        rhs_lo = sb("rhs_lo", [P, NC, T], F32R)
        raw = sb("raw", [P, 2, D])
        w_hi = sb("w_hi", [P, 2, D], F32R)
        w_lo = sb("w_lo", [P, 2, D], F32R)
        keyT = sb("keyT", [P, 2, KEYS])
        PS = ctx.enter_context(nc.psum_tensor("PS", [P, 8, T], F32))

        u_scr = nc.dram_tensor("u_scr", [SUB, CH, GROUPS, NSUB], F32).ap()
        y_scr = nc.dram_tensor("y_scr", [SUB, CH, GROUPS, NSUB], F32).ap()
        act_scr = nc.dram_tensor("act_scr", [KEYS, P, T], F32).ap()
        gate_scr = nc.dram_tensor("gate_scr", [P, T // GCH, KEYS * GCH], F32).ap()

        pre = ExitStack()
        prm = sb("prm", [P, NS], F32, pre)
        bd = sb("bd", [P, CT, P], F32, pre)
        xuc = sb("xuc", [P, NC, T], F32, pre)
        hc = sb("hc", [P, CT, PAD + T], F32, pre)
        sg = sb("sg", [P, 2, T], F32, pre)
        names = ("kk", "exps", "phi", "turns", "red", "half", "mag", "sin", "sinh", "cos", "pr", "pi",
                 "fpr", "fpi", "nfpr", "nfpi", "t9")
        tab = {n: sb("tab_" + n, [P, PAIRS, SUB + 1], F32, pre) for n in names}
        rev_r = sb("rev_r", [P, PAIRS, SUB], F32, pre)
        rev_i = sb("rev_i", [P, PAIRS, SUB], F32, pre)
        small = sb("small", [P, 12, PAIRS], F32, pre)
        cp_r = sb("cp_r", [P, PAIRS, SUB + 1, CH], F32, pre)
        cp_i = sb("cp_i", [P, PAIRS, SUB + 1, CH], F32, pre)
        m1 = sb("m1", [P, 2, PAIRS, P], F32, pre)
        rot_r = sb("rot_r", [P, PAIRS, NSUB + 1], F32, pre)
        rot_i = sb("rot_i", [P, PAIRS, NSUB + 1], F32, pre)
        big = sb("big", [P, 8320], F32, pre)
        diag = sb("diag", [P, DIAGS, P], F32, pre)
        pre.close()
        u_t = xuc[:, 0:CT, :]
        cv = xuc[:, CT:NC, :]
        m2 = x2[:].rearrange("p c t -> p (c t)").rearrange("p (g m) -> p g m", g=GROUPS)
        tmp = big[:, 0:PAIRS * (SUB + 1) * CH]
        kimp = big[:, 0:4096].rearrange("p (g m) -> p g m", g=GROUPS)
        za, zb, zc, zt = (big[:, i * 1024:(i + 1) * 1024] for i in range(4))
        ysb = big[:, 0:2048]
        sq = big[:, 4096:8192].rearrange("p (c t) -> p c t", c=NC)
        ab_r = big[:, 4096:6144].rearrange("p (a j h) -> p a j h", a=PAIRS, j=SUB)
        ab_i = big[:, 6144:8192].rearrange("p (a j h) -> p a j h", a=PAIRS, j=SUB)
        u_sub = big[:, 4096:6144].rearrange("p (g c) -> p g c", g=GROUPS)
        sp_r = big[:, 6144:7184].rearrange("p (a c) -> p a c", a=PAIRS)
        sp_i = big[:, 7184:8224].rearrange("p (a c) -> p a c", a=PAIRS)
        y_t = big[:, 4096:6144].rearrange("p (a t) -> p a t", a=CT)

        peer = ExitStack()
        act_sb = sb("act_sb", [P, 2, T], F32, peer)
        q_sb = sb("q_sb", [P, 2, T], F32, peer)
        oh_1 = sb("oh_1", [P, OH, GROUP, KEYS], F16, peer)
        oh_gh = sb("oh_gh", [P, OH, GROUP, KEYS], F16, peer)
        oh_gl = sb("oh_gl", [P, OH, GROUP, KEYS], F16, peer)
        iota_h = sb("iota_h", [P, KEYS], F16, peer)
        e1T = sb("e1T", [P, P], F32, peer)
        e2T = sb("e2T", [P, P], F32, peer)
        gT = sb("gT", [P, P], F32, peer)
        ghT = sb("ghT", [P, P], F16, peer)
        ghTf = sb("ghTf", [P, P], F32, peer)
        glT = sb("glT", [P, P], F32, peer)
        topv = sb("topv", [P, 2, TB, TOPK], F32, peer)
        topi = sb("topi", [P, 2, TB, TOPK], U32, peer)
        selv = sb("selv", [P, TB, TOPK], F32, peer)
        seli = sb("seli", [P, TB, TOPK], U32, peer)
        sel_all = sb("sel_all", [P, TB, HEADS, TOPK], F32, peer)
        ci_all = sb("ci_all", [P, TB, HEADS, TOPK], U32, peer)
        i1_all = sb("i1_all", [P, TB, HEADS, TOPK], F32, peer)
        i2_all = sb("i2_all", [P, TB, HEADS, TOPK], F32, peer)
        pos = sb("pos", [P, TB, P], U32, peer)
        pos_a = sb("pos_a", [P, TB, P], F32, peer)
        pos_b = sb("pos_b", [P, TB, P], F32, peer)
        e1 = sb("e1", [P, TB, P], F32, peer)
        e2 = sb("e2", [P, TB, P], F32, peer)
        sel_now = sb("sel_now", [P, 3, P], F32, peer)
        gsum = sb("gsum", [P, 2, TB * HEADS], F32, peer)
        route = ExitStack()
        s_all = sb("s_all", [P, 2 * HEADS, T], F32, route)
        s_cur = sb("s_cur", [P, 2, TB, KEYS], F32, route)
        s_cut = sb("s_cut", [P, 2, TB, KEYS], F32, route)
        cand = sb("cand", [P, TB, TOPK * TOPK], F32, route)
        cand_cut = sb("cand_cut", [P, TB, TOPK * TOPK], F32, route)
        eq = sb("eq", [P, P * TOPK], F32, route)
        route.close()
        gst = sb("gst", [P, 2, KEYS, GCH], F32, peer)
        peer.close()
        late = ExitStack()
        fsq = sb("fsq", [P, NC, T], F32, late)
        wt = sb("wt", [P, 2, T], F32, late)
        wt_hi = sb("wt_hi", [P, 2, T], F32R, late)
        wt_lo = sb("wt_lo", [P, 2, T], F32R, late)
        g_in = sb("g_in", [P, 2, T // GCH, 2, GCH], F32, late)
        a_in = sb("a_in", [P, 2, 2, T], F32, late)
        late.close()

        vec_in, prm_in, bd_in, key_in, x_again = map(sem, (
            "vec_in", "prm_in", "bd_in", "key_in", "x_again"))
        x_in = [sem(f"x_in{c}") for c in range(NC // 2)]
        raw_full = [sem(f"raw_full{s}") for s in range(2)]
        hi_done = [sem(f"hi_done{s}") for s in range(2)]
        lo_done = [sem(f"lo_done{s}") for s in range(2)]
        mm_done = [sem(f"mm_done{s}") for s in range(2)]
        evacuated = [sem(f"evacuated{s}") for s in range(2)]
        act_stored = [sem(f"act_stored{s}") for s in range(2)]
        const_ok, iota_ok = sem("const_ok"), sem("iota_ok")
        dve_chain, act_chain = sem("dve_chain"), sem("act_chain")
        sq_done, ms_done, std_done, rhs_hi_done, rhs_done = map(sem, (
            "sq_done", "ms_done", "std_done", "rhs_hi_done", "rhs_done"))
        dt_done, angle_done, trig_done, tab_done, ab_done, cp_done = map(sem, (
            "dt_done", "angle_done", "trig_done", "tab_done", "ab_done", "cp_done"))
        m1_part, m1_out, k_part, k_out, m2_zero, m2_in = map(sem, (
            "m1_part", "m1_out", "k_part", "k_out", "m2_zero", "m2_in"))
        u_stored, u_in, z_done, z_read, sp_done, m2_used, y_done, y_out, y_stored, y_in = map(sem, (
            "u_stored", "u_in", "z_done", "z_read", "sp_done", "m2_used", "y_done", "y_out", "y_stored", "y_in"))
        ypre_done, gelu_done, glu_done, gsig_done, yssm_done = map(sem, (
            "ypre_done", "gelu_done", "glu_done", "gsig_done", "yssm_done"))
        tap_done = [sem(f"tap_done{a}") for a in range(DCT)]
        h_ready, pool_chain, sig_done, diag_done, diag_used, cv3_done = map(sem, (
            "h_ready", "pool_chain", "sig_done", "diag_done", "diag_used", "cv3_done"))
        mean_done, xc_done, csq_done, var_done, cstd_done, hn_done, silu_done = map(
            sem, ("mean_done", "xc_done", "csq_done", "var_done",
                  "cstd_done", "hn_done", "silu_done"))
        half_done, x2_done = sem("half_done"), sem("x2_done")
        sq2_done, ms2_done, std2_done, xn_done, xhi_done, xn_ready = map(sem, (
            "sq2_done", "ms2_done", "std2_done", "xn_done", "xhi_done", "xn_ready"))
        s_done, s_out, top_done, key_done, sub_done, exp_done, sel_done, selT_done, selT_out, wt_part = map(sem, (
            "s_done", "s_out", "top_done", "key_done", "sub_done", "exp_done", "sel_done", "selT_done", "selT_out",
            "wt_part"))
        oh_done = [sem(f"oh_done{s}") for s in range(OH)]
        g_mm = [sem(f"g_mm{s}") for s in range(OH)]
        g_out = [sem(f"g_out{s}") for s in range(OH)]
        g_stored = [sem(f"g_stored{s}") for s in range(2)]
        ga_in = [sem(f"ga_in{s}") for s in range(2)]
        wt_done = [sem(f"wt_done{s}") for s in range(2)]
        peer_done, fin_done, fsq_done, fms_done, fstd_done, out_ready, out_stored = map(sem, (
            "peer_done", "fin_done", "fsq_done", "fms_done", "fstd_done", "out_ready", "out_stored"))

        block = ctx.enter_context(nc.Block())

        TURN_TILES = SPREAD // TB
        TILE_GROUPS = STEP_TOK // GROUP
        SLOT_USES = P // GROUP // OH
        R_WOUT, R_WQ, R_U, R_V = WOUT // 2, WQ // 2, UT // 2, VT // 2
        R_SPREAD = R_U + ALONE // 2
        R_REST = R_SPREAD + SPREAD // 2

        @block.sync
        def _(sp):
            def load(r, s):
                wait(sp, lo_done[s], r)
                sp.dma_start(raw[:, s, :], tiles[2 * r + s, :, :] if isinstance(r, int) else
                             tiles[bass.ds(r * 2 + s, 1), :, :].rearrange("a p n -> (a p) n")
                             ).then_inc(raw_full[s], 16)

            sp.dma_start(vec[:], vecs).then_inc(vec_in, 16)
            for c in range(NC // 2):
                sp.dma_start(xuc[:, 2 * c:2 * c + 2, :], xT[:, 2 * c:2 * c + 2, :]).then_inc(x_in[c], 16)
            load(0, 0)
            sp.dma_start(prm[:], ssm).then_inc(prm_in, 16)
            load(0, 1)
            sp.dma_start(bd[:], glu_bd).then_inc(bd_in, 16)
            sp.dma_start(keyT[:], keys).then_inc(key_in, 16)
            for r in range(1, 4):
                load(r, 0)
                load(r, 1)
            for s in range(2):
                sp.wait_ge(evacuated[s], 2)
            for q in range(GPT):
                sp.dma_start(u_scr.rearrange("j h (a q) c -> q h a j c", q=GPT)[q],
                             u_t[q * CH:(q + 1) * CH].rearrange("h a (j c) -> h a j c", j=SUB)
                             ).then_inc(u_stored, 16)
            for r in range(4, R_WOUT + 1):
                load(r, 0)
                load(r, 1)
            sp.wait_ge(u_stored, 16 * GPT)
            sp.wait_ge(m1_part, 8)
            sp.dma_start(u_sub, u_scr.rearrange("j h g c -> (j h) g c")).then_inc(u_in, 16)
            sp.wait_ge(m2_zero, 1)
            sp.wait_ge(k_out, 8)
            for j in range(SUB):
                n = (SUB - j) * CH
                sp.dma_start(m2[j * CH:(j + 1) * CH, :, j * CH:P], kimp[0:CH, :, 0:n]).then_inc(m2_in, 16)
            load(R_WOUT + 1, 0)
            load(R_WOUT + 1, 1)
            sp.wait_ge(m2_used, 1)
            sp.dma_start(x2[:], xT).then_inc(x_again, 16)
            sp.wait_ge(y_out, 4)
            sp.dma_start(y_scr.rearrange("i h g c -> (i h) (g c)"), ysb).then_inc(y_stored, 16)
            sp.wait_ge(y_stored, 16)
            for q in range(GPT):
                sp.dma_start(y_t[q * CH:(q + 1) * CH].rearrange("h a (i c) -> h a i c", i=SUB),
                             y_scr.rearrange("i h (a q) c -> q h a i c", q=GPT)[q]).then_inc(y_in, 16)
            for r in range(R_WOUT + 2, R_WQ + 1):
                load(r, 0)
                load(r, 1)
            with sp.Fori(0, HEADS) as it:
                for s in range(2):
                    load(it + (R_WQ + 1), s)

            def u_step(r, j, s):
                load(r + 1, s)
                sp.wait_ge(evacuated[s], r + 1)
                sp.dma_start(act_scr[j, :, :] if isinstance(j, int) else
                             act_scr[bass.ds(j, 1), :, :].rearrange("a p t -> (a p) t"),
                             act_sb[:, s, :]).then_inc(act_stored[s], 16)

            with sp.Fori(0, ALONE // 2) as it:
                for s in range(2):
                    u_step(it + R_U, it * 2 + s, s)

            def store_piece(turn, half, k):
                if k == 0:
                    for b in range(OH):
                        sp.wait_ge(g_out[b], turn * SLOT_USES + ((half + 1) * SLOT_USES // 2 + 1))
                n = KEYS // PIECES
                chunk = turn * 2 + half
                dst = gate_scr[:, chunk:chunk + 1] if isinstance(turn, int) else gate_scr[:, bass.ds(chunk, 1)]
                sp.dma_start(dst[:, :, k * n * GCH:(k + 1) * n * GCH].rearrange("p a n -> p (a n)"),
                             gst[:, half, k * n:(k + 1) * n].rearrange("p i t -> p (i t)")
                             ).then_inc(g_stored[half], 16)

            def spread_step(turn, q):
                u_step(turn * (TURN_TILES // 2) + (R_SPREAD + q // 2), turn * TURN_TILES + (ALONE + q), q % 2)
                if TURN_TILES // 2 <= q < TURN_TILES // 2 + PIECES:
                    store_piece(turn, 0, q - TURN_TILES // 2)

            for q in range(PIECES):
                spread_step(0, q)
            with sp.Fori(0, TB - 1) as it:
                for q in range(PIECES, TURN_TILES):
                    spread_step(it, q)
                for q in range(PIECES):
                    spread_step(it + 1, q)
                    store_piece(it, 1, q)
            for q in range(PIECES, TURN_TILES):
                spread_step(TB - 1, q)
            for q in range(PIECES):
                u_step(R_REST + q // 2, ALONE + SPREAD + q, q % 2)
                store_piece(TB - 1, 1, q)
            rest = (KEYS - ALONE - SPREAD) // 2
            with sp.Fori(PIECES // 2, rest - 1) as it:
                for s in range(2):
                    u_step(it + R_REST, it * 2 + (ALONE + SPREAD + s), s)

            g_rows = gate_scr.rearrange("p a (i n) -> i p a n", n=2 * GCH)
            a_rows = act_scr.rearrange("(i b) p t -> i p b t", b=2)

            def load_ga(j, s, k):
                for b in range(2):
                    wait(sp, wt_done[b], k)
                sp.dma_start(g_in[:, s].rearrange("p a b t -> p a (b t)"),
                             g_rows[bass.ds(j, 1)].rearrange("i p a n -> (i p) a n")).then_inc(ga_in[s], 16)
                sp.dma_start(a_in[:, s], a_rows[bass.ds(j, 1)].rearrange("i p b t -> (i p) b t")
                             ).then_inc(ga_in[s], 16)

            for s in range(2):
                sp.wait_ge(g_stored[s], 16 * PIECES * (TB + 1))
                sp.wait_ge(act_stored[s], 16 * (2 + 1))
            load_ga(0, 0, 0)
            load_ga(1, 1, 0)
            for s in range(2):
                u_step(R_REST + rest - 1, ALONE + SPREAD + 2 * (rest - 1) + s, s)
            for s in range(2):
                sp.wait_ge(act_stored[s], 16 * (KEYS // 2 + 1))
            with sp.Fori(0, KEYS // 4 - 1) as it:
                for g in range(2):
                    load(it * 2 + (R_V + 1 + g), 0)
                    load(it * 2 + (R_V + 1 + g), 1)
                    load_ga(it * 2 + (2 + g), g, it * 2 + (1 + g))
            load(R_V + KEYS // 2 - 1, 0)
            load(R_V + KEYS // 2 - 1, 1)
            for c in range(NC):
                sp.wait_ge(out_ready, c + 1)
                sp.dma_start(outT[:, c, :], x2[:, c, :]).then_inc(out_stored, 16)
            sp.wait_ge(out_stored, 16 * NC)

        @block.gpsimd
        def _(pool):
            def split_lo(r, s):
                pool.wait_ge(hi_done[s], r + 1)
                pool.tensor_tensor(w_lo[:, s, :], raw[:, s, :], w_hi[:, s, :].bitcast(F32), ALU.subtract
                                   ).then_inc(lo_done[s], 1)

            for s in range(2):
                pool.sem_inc(act_stored[s], 16)
                pool.sem_inc(g_stored[s], 16 * PIECES)
            for b in range(OH):
                pool.sem_inc(g_out[b], 1)
                pool.sem_inc(g_mm[b], 1)
            pool.sem_inc(s_out, 1)
            pool.sem_inc(selT_out, 1)
            pool.iota(tab["kk"][:], [[0, PAIRS], [1, SUB + 1]], base=0, channel_multiplier=0,
                      allow_small_or_imprecise_dtypes=True).then_inc(iota_ok, 1)
            pool.memset(ones[:], 1.0).then_inc(const_ok, 1)
            pool.memset(epsc[:], EPS).then_inc(const_ok, 1)
            pool.memset(ident[:], 0.0).then_inc(const_ok, 1)
            pool.wait_ge(const_ok, 3)
            pool.affine_select(out=ident[:], in_=ident[:], compare_op=ALU.not_equal, fill=1.0, base=0,
                               pattern=[[-1, P]], channel_multiplier=1).then_inc(const_ok, 1)
            pool.memset(hc[:, :, 0:PAD], 0.0).then_inc(const_ok, 1)
            pool.iota(iota_row[:], [[1, P]], base=0, channel_multiplier=0,
                      allow_small_or_imprecise_dtypes=True).then_inc(const_ok, 1)
            pool.iota(iota16[:], [[1, TOPK]], base=0, channel_multiplier=0,
                      allow_small_or_imprecise_dtypes=True).then_inc(const_ok, 1)
            pool.memset(m2, 0.0).then_inc(m2_zero, 1)
            chain = Chain(pool, pool_chain)
            step, tt = chain.step, pool.tensor_tensor

            def outer(k, x):
                n = k.shape[-1]
                return (k.rearrange("p a (k o) -> p a k o", o=1).broadcast_to([P, PAIRS, n, CH]),
                        x.rearrange("p (a o h) -> p a o h", a=PAIRS, o=1).broadcast_to([P, PAIRS, n, CH]))

            def cols(c0):
                return prm[:, c0:c0 + PAIRS * CH]

            t8 = tmp[:, 0:PAIRS * SUB * CH].rearrange("p (a k h) -> p a k h", a=PAIRS, k=SUB)
            t9 = tmp.rearrange("p (a k h) -> p a k h", a=PAIRS, k=SUB + 1)
            pool.wait_ge(prm_in, 16)
            pool.wait_ge(tab_done, 1)
            pool.wait_ge(ms_done, 1)
            tt(ab_r, *outer(rev_r[:], cols(S_BR)), ALU.mult)
            step(tt(t8, *outer(rev_i[:], cols(S_BI)), ALU.mult))
            step(tt(ab_r, ab_r, t8, ALU.subtract))
            tt(ab_i, *outer(rev_r[:], cols(S_BI)), ALU.mult)
            step(tt(t8, *outer(rev_i[:], cols(S_BR)), ALU.mult))
            step(tt(ab_i, ab_i, t8, ALU.add))
            pool.sem_inc(ab_done, 1)
            tt(cp_r[:], *outer(tab["fpr"][:], cols(S_CR)), ALU.mult)
            step(tt(t9, *outer(tab["fpi"][:], cols(S_CI)), ALU.mult))
            step(tt(cp_r[:], cp_r[:], t9, ALU.subtract))
            tt(cp_i[:], *outer(tab["nfpr"][:], cols(S_CI)), ALU.mult)
            step(tt(t9, *outer(tab["nfpi"][:], cols(S_CR)), ALU.mult))
            tt(cp_i[:], cp_i[:], t9, ALU.add).then_inc(cp_done, 1)
            for r in range(R_WOUT, R_WQ):
                split_lo(r, 0)
                split_lo(r, 1)
            with pool.Fori(R_WQ, NTILES // 2) as r:
                split_lo(r, 0)
                split_lo(r, 1)
            
        @block.scalar
        def _(act):
            def split_hi(r, s):
                wait(act, mm_done[s], r)
                act.wait_ge(raw_full[s], r * 16 + 16)
                act.activation(w_hi[:, s, :], raw[:, s, :], ACT.Copy).then_inc(hi_done[s], 1)

            act.wait_ge(vec_in, 16)
            for c in range(NC):
                act.wait_ge(x_in[c // 2], 16)
                act.activation(rhs_hi[:, c, :], xuc[:, c, :], ACT.Copy, scale=vec[:, V_G1 + c:V_G1 + c + 1]
                               ).then_inc(rhs_hi_done, 1)
            split_hi(0, 0)
            split_hi(0, 1)
            for c in range(NC):
                act.activation(sq[:, c, :], xuc[:, c, :], ACT.Square).then_inc(sq_done, 1)
            act.wait_ge(prm_in, 16)
            act.activation(small[:, 0, :], prm[:, S_DT:S_DT + PAIRS], ACT.Exp).then_inc(dt_done, 1)
            act.wait_ge(angle_done, 1)
            act.activation(tab["mag"][:], tab["exps"][:], ACT.Exp).then_inc(trig_done, 1)
            act.activation(tab["sin"][:], tab["red"][:], ACT.Sin).then_inc(trig_done, 1)
            act.activation(tab["sinh"][:], tab["half"][:], ACT.Sin).then_inc(trig_done, 1)
            act.wait_ge(ms_done, 1)
            act.wait_ge(const_ok, 7)
            act.activation(rstd[:], PS[:, 2, :], ACT.Sqrt, bias=epsc[:], scale=1.0 / D).then_inc(std_done, 1)
            for n in range(WOUT):
                split_hi(n // 2 + 1, n % 2)
                if n >= CT and n % 2 == 1:
                    a = (n - CT) // 2
                    act.wait_ge(evacuated[1], CT // 2 + a + 1)
                    act.activation(sg[:, a % 2, :], sg[:, a % 2, :], ACT.Sigmoid).then_inc(sig_done, 1)
            for k in range(8):
                act.wait_ge(m1_part, k + 1)
                act.activation(m1[:, k // 4, (k % 4) * 4:(k % 4) * 4 + 4, :].rearrange("p a m -> p (a m)"),
                               PS[:, 4 + k % 4, :], ACT.Copy).then_inc(m1_out, 1)
            for k in range(8):
                act.wait_ge(k_part, k + 1)
                g0 = (k // 2) * 8
                act.activation(kimp[0:CH, g0:g0 + 8, :].rearrange("p (a e) m -> p e a m", e=2)[:, k % 2],
                               PS[0:CH, 4 + k % 4, :].rearrange("p (a m) -> p a m", a=4), ACT.Copy).then_inc(k_out, 1)
            for k in range(WIDTH):
                wait(act, diag_used, k - DIAGS + 1)
                w0 = V_CW + DCT * WIDTH + k
                act.activation(diag[:, k % DIAGS, :], ident[:], ACT.Copy, scale=vec[:, w0:w0 + 1]
                               ).then_inc(diag_done, 1)
            act.wait_ge(y_done, 1)
            for b in range(4):
                act.activation(ysb.rearrange("p (b a e c) -> p e b a c", b=2, a=PAIRS // 2, e=2)[:, b // 2, b % 2],
                               PS[:, 4 + b, :].rearrange("p (a c) -> p a c", c=NSUB), ACT.Copy).then_inc(y_out, 1)
            for a in range(CT):
                act.wait_ge(xc_done, a + 1)
                act.activation(hc[:, a, 0:T], cv[:, a, :], ACT.Square).then_inc(csq_done, 1)
            act.wait_ge(var_done, 1)
            act.activation(sg[:, 0, :], PS[:, 3, :], ACT.Sqrt, bias=epsc[:], scale=1.0 / T).then_inc(cstd_done, 1)
            for a in range(CT):
                act.wait_ge(hn_done, a + 1)
                act.activation(cv[:, a, :], cv[:, a, :], ACT.Silu, bias=vec[:, V_LB + a:V_LB + a + 1],
                               scale=vec[:, V_LG + a:V_LG + a + 1]).then_inc(silu_done, 1)
            for a in range(CT):
                act.wait_ge(silu_done, a + 1)
                act.activation(rhs_hi[:, CT + a, :], cv[:, a, :], ACT.Copy).then_inc(rhs_hi_done, 1)
            split_hi(R_WOUT + 1, 0)
            for a in range(CT):
                act.wait_ge(ypre_done, a + 1)
                act.activation(y_t[:, a, :], y_t[:, a, :], ACT.Gelu).then_inc(gelu_done, 1)
            split_hi(R_WOUT + 1, 1)
            split_hi(R_WOUT + 2, 0)
            for a in range(CT):
                act.wait_ge(glu_done, a + 1)
                act.activation(ysb[:, a * T:(a + 1) * T], PS[:, 4 + a, :], ACT.Sigmoid,
                               bias=vec[:, V_GB + a:V_GB + a + 1]).then_inc(gsig_done, 1)
            for a in range(CT):
                act.wait_ge(yssm_done, a + 1)
                act.activation(rhs_hi[:, a, :].rearrange("p (c i) -> p i c", i=SUB),
                               y_t[:, a, :].rearrange("p (i c) -> p i c", i=SUB), ACT.Copy
                               ).then_inc(rhs_hi_done, 1)
            split_hi(R_WOUT + 2, 1)
            for n in range(NC // 2):
                r, s = R_WOUT + (n + 4) // 2, n % 2
                split_hi(r + 1, s)
                act.wait_ge(x2_done, NC // 2 + n + 1)
                act.activation(sq[:, 2 * n, :], x2[:, 2 * n, :], ACT.Square).then_inc(sq2_done, 1)
                act.wait_ge(evacuated[s], r + 1)
                act.activation(sq[:, 2 * n + 1, :], x2[:, 2 * n + 1, :], ACT.Square).then_inc(sq2_done, 1)
            act.wait_ge(ms2_done, 1)
            act.activation(rstd[:], PS[:, 4, :], ACT.Sqrt, bias=epsc[:], scale=1.0 / D).then_inc(std2_done, 1)
            for c in range(NC):
                act.wait_ge(xn_done, c + 1)
                act.activation(rhs_hi[:, c, :], sq[:, c, :], ACT.Copy).then_inc(xhi_done, 1)
            with act.Fori(0, HEADS) as it:
                for s in range(2):
                    act.wait_ge(mm_done[s], it + (R_WQ + 1))
                    act.activation(q_sb[:, s, :], PS[:, s, :], ACT.Copy).then_inc(evacuated[s], 1)
                    split_hi(it + (R_WQ + 1), s)
                for s in range(2):
                    act.wait_ge(s_done, it * 2 + (s + 1))
                    act.activation(s_all[:, bass.ds(it * 2 + s, 1), :].rearrange("p a t -> p (a t)"),
                                   PS[:, 4 + s, :], ACT.Copy).then_inc(s_out, 1)

            def u_step(r, k, s):
                act.wait_ge(mm_done[s], r + 1)
                act.wait_ge(act_stored[s], k * 16 + 16)
                act.activation(act_sb[:, s, :], PS[:, s, :], ACT.Gelu).then_inc(evacuated[s], 1)
                split_hi(r + 1, s)

            act.activation(gelu_warm[:], epsc[:], ACT.Gelu)
            with act.Fori(0, EXP_AT // 2) as it:
                for s in range(2):
                    u_step(it + R_U, it, s)
            act.wait_ge(sub_done, 1)
            act.activation(sel_all[:], sel_all[:], ACT.Exp).then_inc(exp_done, 1)
            act.activation(gelu_warm[:], epsc[:], ACT.Gelu)
            with act.Fori(EXP_AT // 2, ALONE // 2) as it:
                for s in range(2):
                    u_step(it + R_U, it, s)
            with act.Fori(0, TB) as it:
                for q in range(TURN_TILES):
                    u_step(it * (TURN_TILES // 2) + (R_SPREAD + q // 2),
                           it * (TURN_TILES // 2) + (ALONE // 2 + q // 2), q % 2)
                    half, w = q // (TURN_TILES // 2), q % (TURN_TILES // 2)
                    if w == 0:
                        act.wait_ge(g_stored[half], it * (16 * PIECES) + 16 * PIECES)
                    for b in range(TILE_GROUPS):
                        t0, o = w * STEP_TOK + b * GROUP, (q % 2) * TILE_GROUPS + b
                        act.wait_ge(g_mm[o], it * SLOT_USES + (q // 2 + 2))
                        act.activation(gst[:, half, :, t0:t0 + GROUP].rearrange("p i t -> p t i"),
                                       PS[:, 2 + o, :].rearrange("p (t i) -> p t i", t=GROUP), ACT.Copy,
                                       scale=1.0 / GSCALE).then_inc(g_out[o], 1)
            with act.Fori(0, (KEYS - ALONE - SPREAD) // 2) as it:
                for s in range(2):
                    u_step(it + R_REST, it + (ALONE + SPREAD) // 2, s)
            with act.Fori(0, KEYS // 2 - 1) as it:
                for s in range(2):
                    split_hi(it + (R_V + 1), s)
            for c in range(NC):
                act.wait_ge(fin_done, c + 1)
                act.activation(fsq[:, c, :], x2[:, c, :], ACT.Square).then_inc(fsq_done, 1)
            act.wait_ge(fms_done, 1)
            act.activation(rstd[:], PS[:, 0, :], ACT.Sqrt, bias=epsc[:], scale=1.0 / D).then_inc(fstd_done, 1)

        @block.tensor
        def _(pe):
            def product(r, s, out, ready=None, n0=0):
                pe.wait_ge(hi_done[s], r + 1)
                pe.wait_ge(lo_done[s], r + 1)
                for c in range(NC):
                    if ready:
                        pe.wait_ge(ready, n0 + c + 1)
                    hi, lo = w_hi[:, s, c * P:(c + 1) * P], w_lo[:, s, c * P:(c + 1) * P]
                    pe.matmul(out, hi, rhs_hi[:, c, :], start=(c == 0), stop=False)
                    pe.matmul(out, hi, rhs_lo[:, c, :], start=False, stop=False)
                    mm = pe.matmul(out, lo, rhs_hi[:, c, :], start=False, stop=(c == NC - 1))
                mm.then_inc(mm_done[s], 1)

            def stream(r, s, ready=None, n0=0):
                wait(pe, evacuated[s], r)
                product(r, s, PS[:, s, :], ready, n0)

            stream(0, 0, rhs_done)
            stream(0, 1)
            pe.wait_ge(const_ok, 7)
            for c in range(NC):
                pe.wait_ge(sq_done, c + 1)
                mm = pe.matmul(PS[:, 2, :], ones[:], sq[:, c, :], start=(c == 0), stop=(c == NC - 1))
            mm.then_inc(ms_done, 1)
            for r in range(1, R_WOUT):
                stream(r, 0)
                stream(r, 1)
            for k in range(8):
                pe.wait_ge(ab_done, 1)
                if k >= 4:
                    pe.wait_ge(m1_out, k - 3)
                for a in range(4):
                    src = (ab_r, ab_i)[k // 4][:, (k % 4) * 4 + a].rearrange("p j h -> p (j h)")
                    mm = pe.transpose(PS[:, 4 + k % 4, a * P:(a + 1) * P], src, ident[:])
                mm.then_inc(m1_part, 1)
            for k in range(8):
                pe.wait_ge(cp_done, 1)
                pe.wait_ge(m1_out if k < 4 else k_out, 5 + k if k < 4 else k - 3)
                for w in range(4):
                    a, rows = (k // 2) * 4 + w, slice((k % 2) * STATE, (k % 2 + 1) * STATE)
                    for ri, (b0, cp) in enumerate(((S_BR, cp_r), (S_BI, cp_i))):
                        mm = pe.matmul(PS[0:CH, 4 + k % 4, w * P:(w + 1) * P],
                                       prm[rows, b0 + a * CH:b0 + (a + 1) * CH],
                                       cp[rows, a, 0:SUB, :].rearrange("p k h -> p (k h)"),
                                       start=(ri == 0), stop=(ri == 1))
                mm.then_inc(k_part, 1)
            pe.wait_ge(u_in, 16)
            pe.wait_ge(k_out, 8)
            for ri in range(2):
                for g in range(GROUPS):
                    a, rows = g // 2, slice((g % 2) * STATE, (g % 2 + 1) * STATE)
                    mm = pe.matmul(PS[rows, 4 + 2 * ri + a // 8, (a % 8) * NSUB:(a % 8 + 1) * NSUB],
                                   m1[:, ri, a, rows], u_sub[:, g, :], start=True, stop=True)
            mm.then_inc(z_done, 1)
            pe.wait_ge(h_ready, 1)
            for k in range(WIDTH):
                pe.wait_ge(diag_done, k + 1)
                pe.matmul(PS[:, 3, :], diag[:, k % DIAGS, :], hc[:, DCT, k:k + T], start=(k == 0),
                          stop=(k == WIDTH - 1)).then_inc(diag_used, 1)
            pe.wait_ge(m2_in, 16 * SUB)
            pe.wait_ge(z_read, 1)

            def y_bank(g):
                a = g // 2
                return PS[:, 4 + 2 * (g % 2) + a // 8, (a % 8) * NSUB:(a % 8 + 1) * NSUB]

            for g in range(GROUPS):
                mm = pe.matmul(y_bank(g), m2[:, g, :], u_sub[:, g, :], start=(g % 16 < 2), stop=False,
                               skip_group_check=True)
            mm.then_inc(m2_used, 1)
            pe.wait_ge(sp_done, 1)

            def from_states(pairs):
                for a in pairs:
                    for cp, sp in ((cp_r, sp_r), (cp_i, sp_i)):
                        for e in range(2):
                            rows = slice(e * STATE, (e + 1) * STATE)
                            mm = pe.matmul(y_bank(2 * a + e), cp[rows, a, 1:SUB + 1, :].rearrange("p k h -> p (k h)"),
                                           sp[rows, a, 0:NSUB], start=False, stop=(cp is cp_i),
                                           skip_group_check=True)
                return mm

            from_states(range(MEAN_AT))
            for a in range(DCT):
                pe.wait_ge(tap_done[a], WIDTH)
                pe.matmul(PS[:, 2, :], ones[:], cv[:, a, :], start=(a == 0), stop=False)
            pe.wait_ge(cv3_done, 1)
            pe.matmul(PS[:, 2, :], ones[:], cv[:, DCT, :], start=False, stop=True).then_inc(mean_done, 1)
            mm = from_states(range(MEAN_AT, PAIRS))
            mm.then_inc(y_done, 1)
            for a in range(CT):
                pe.wait_ge(csq_done, a + 1)
                mm = pe.matmul(PS[:, 3, :], ones[:], hc[:, a, 0:T], start=(a == 0), stop=(a == CT - 1))
            mm.then_inc(var_done, 1)

            def w_out_tile(n):
                r, s, first = R_WOUT + n // 2, n % 2, n % 4 == 0
                pe.wait_ge(evacuated[s], r)
                pe.wait_ge(hi_done[s], r + 1)
                pe.wait_ge(lo_done[s], r + 1)
                for m in range(2):
                    for i in range(CT):
                        if first and m == 0:
                            pe.wait_ge(rhs_done, NC + (n // 4) * CT + i + 1)
                        c, out = CT * (1 - n // 4) + i, PS[:, 2 * s + m, :]
                        cut = slice((m * CT + i) * P, (m * CT + i + 1) * P)
                        pe.matmul(out, w_hi[:, s, cut], rhs_hi[:, c, :], start=(i == 0), stop=False)
                        pe.matmul(out, w_hi[:, s, cut], rhs_lo[:, c, :], start=False, stop=False)
                        mm = pe.matmul(out, w_lo[:, s, cut], rhs_hi[:, c, :], start=False, stop=(i == CT - 1))
                    mm.then_inc(mm_done[s] if m else half_done, 1)

            for n in range(GLU_AT):
                w_out_tile(n)
            pe.wait_ge(bd_in, 16)
            pe.wait_ge(y_out, 4)
            for a in range(CT):
                pe.wait_ge(gelu_done, a + 1)
                pe.matmul(PS[:, 4 + a, :], bd[:, a, :], y_t[:, a, :], start=True, stop=True).then_inc(glu_done, 1)
            for n in range(GLU_AT, 4):
                w_out_tile(n)

            def squares_of(n):
                for c in (2 * n, 2 * n + 1):
                    pe.wait_ge(sq2_done, c + 1)
                    mm = pe.matmul(PS[:, 4, :], ones[:], sq[:, c, :], start=(c == 0), stop=(c == NC - 1),
                                   skip_group_check=True)
                return mm

            for n in range(4):
                w_out_tile(4 + n)
                if n > 0:
                    squares_of(n - 1)
            squares_of(3).then_inc(ms2_done, 1)
            pe.wait_ge(key_in, 16)
            with pe.Fori(0, HEADS) as it:
                stream(it + R_WQ, 0, xn_ready)
                stream(it + R_WQ, 1)
                for s in range(2):
                    pe.wait_ge(evacuated[s], it + (R_WQ + 1))
                    pe.wait_ge(s_out, it * 2 + 1)
                    for b in range(TB):
                        mm = pe.matmul(PS[:, 4 + s, b * P:(b + 1) * P], q_sb[:, s, b * P:(b + 1) * P],
                                       keyT[:, s, :], start=True, stop=True)
                    mm.then_inc(s_done, 1)
            with pe.Fori(0, ALONE // 2) as it:
                for s in range(2):
                    stream(it + R_U, s)
            with pe.Fori(0, TB) as it:
                pe.wait_ge(sel_done, it + 1)
                pe.wait_ge(selT_out, it * 2 + 1)
                for k in range(3):
                    mm = pe.transpose(PS[:, 6, k * P:(k + 1) * P], sel_now[:, k, :], ident[:])
                mm.then_inc(selT_done, 1)
                for q in range(TURN_TILES):
                    stream(it * (TURN_TILES // 2) + (R_SPREAD + q // 2), q % 2)
                    for b in range(TILE_GROUPS):
                        n, o = it * SLOT_USES + q // 2, (q % 2) * TILE_GROUPS + b
                        pe.wait_ge(oh_done[o], n + 1)
                        pe.wait_ge(g_out[o], n + 1)
                        for t in range(GROUP):
                            out = PS[:, 2 + o, t * P:(t + 1) * P]
                            pe.matmul(out, oh_1[:, o, t, :], oh_gh[:, o, t, :], start=True, stop=False)
                            mm = pe.matmul(out, oh_1[:, o, t, :], oh_gl[:, o, t, :], start=False, stop=True)
                        mm.then_inc(g_mm[o], 1)
            with pe.Fori(0, (KEYS - ALONE - SPREAD) // 2) as it:
                for s in range(2):
                    stream(it + R_REST, s)

            def v_step(r, k, s, first, last):
                pe.wait_ge(hi_done[s], r + 1)
                pe.wait_ge(lo_done[s], r + 1)
                pe.wait_ge(wt_done[s], k + 1)
                for m in [*range(2, NC), 0, 1] if first else range(NC):
                    if first and m < 2:
                        pe.wait_ge(evacuated[m], R_V)
                    hi, lo = w_hi[:, s, m * P:(m + 1) * P], w_lo[:, s, m * P:(m + 1) * P]
                    pe.matmul(PS[:, m, :], hi, wt_hi[:, s, :], start=first, stop=False, skip_group_check=True)
                    pe.matmul(PS[:, m, :], hi, wt_lo[:, s, :], start=False, stop=False, skip_group_check=True)
                    mm = pe.matmul(PS[:, m, :], lo, wt_hi[:, s, :], start=False, stop=last, skip_group_check=True)
                    if last:
                        mm.then_inc(peer_done, 1)
                if not last:
                    mm.then_inc(mm_done[s], 1)

            for s in range(2):
                pe.wait_ge(g_out[s], TB * SLOT_USES + 1)
                pe.wait_ge(g_out[s + 2], TB * SLOT_USES + 1)
            for s in range(2):
                v_step(R_V, 0, s, s == 0, False)
            with pe.Fori(0, KEYS // 2 - 2) as it:
                for s in range(2):
                    v_step(it + (R_V + 1), it + 1, s, False, False)
            for s in range(2):
                v_step(R_V + KEYS // 2 - 1, KEYS // 2 - 1, s, False, s == 1)
            for c in range(NC):
                pe.wait_ge(fsq_done, c + 1)
                mm = pe.matmul(PS[:, 0, :], ones[:], fsq[:, c, :], start=(c == 0), stop=(c == NC - 1))
            mm.then_inc(fms_done, 1)

        @block.vector
        def _(dve):
            ch = Chain(dve, dve_chain)
            step = ch.step
            tt, ts, stt = dve.tensor_tensor, dve.tensor_scalar, dve.scalar_tensor_tensor
            dt, lrdt, lidt, den, fr, fi, t1, t2, nr = (small[:, i, :] for i in range(9))
            lr, li = prm[:, S_LR:S_LR + PAIRS], prm[:, S_LI:S_LI + PAIRS]

            def per_k(x):
                return x.rearrange("p (a k) -> p a k", k=1).broadcast_to([P, PAIRS, SUB + 1])

            def angles():
                dve.wait_ge(dt_done, 1)
                dve.wait_ge(iota_ok, 1)
                tt(lrdt, lr, dt, ALU.mult)
                step(tt(lidt, li, dt, ALU.mult))
                tt(tab["exps"][:], per_k(lrdt), tab["kk"][:], ALU.mult)
                step(tt(tab["phi"][:], per_k(lidt), tab["kk"][:], ALU.mult))
                step(ts(tab["turns"][:], tab["phi"][:], 0.15915494309189535, MAGIC, ALU.mult, ALU.add))
                step(ts(tab["turns"][:], tab["turns"][:], -MAGIC, None, ALU.add))
                step(stt(tab["red"][:], tab["turns"][:], -TWO_PI[0], tab["phi"][:], ALU.mult, ALU.add))
                step(stt(tab["phi"][:], tab["turns"][:], -TWO_PI[1], tab["red"][:], ALU.mult, ALU.add))
                step(stt(tab["red"][:], tab["turns"][:], -TWO_PI[2], tab["phi"][:], ALU.mult, ALU.add))
                step(ts(tab["red"][:], tab["red"][:], PI_IN, -PI_IN, ALU.min, ALU.max))
                ts(tab["half"][:], tab["red"][:], 0.5, None, ALU.mult).then_inc(angle_done, 1)

            def powers():
                dve.wait_ge(trig_done, 3)
                step(tt(tab["cos"][:], tab["sinh"][:], tab["sinh"][:], ALU.mult))
                step(ts(tab["cos"][:], tab["cos"][:], -2.0, 1.0, ALU.mult, ALU.add))
                tt(tab["pr"][:], tab["mag"][:], tab["cos"][:], ALU.mult)
                step(tt(tab["pi"][:], tab["mag"][:], tab["sin"][:], ALU.mult))
                a_i = tab["pi"][:, :, 1]
                ts(nr, tab["pr"][:, :, 1], -1.0, None, ALU.add)
                tt(t1, lr, lr, ALU.mult)
                step(tt(t2, li, li, ALU.mult))
                step(tt(den, t1, t2, ALU.add))
                dve.reciprocal(den, den)
                tt(t1, nr, lr, ALU.mult)
                tt(small[:, 9, :], a_i, lr, ALU.mult)
                tt(small[:, 10, :], nr, li, ALU.mult)
                step(tt(t2, a_i, li, ALU.mult))
                tt(fr, t1, t2, ALU.add)
                step(tt(fi, small[:, 9, :], small[:, 10, :], ALU.subtract))
                tt(fr, fr, den, ALU.mult)
                step(tt(fi, fi, den, ALU.mult))

            def f_powers():
                tt(tab["fpr"][:], per_k(fr), tab["pr"][:], ALU.mult)
                tt(tab["fpi"][:], per_k(fr), tab["pi"][:], ALU.mult)
                step(tt(tab["t9"][:], per_k(fi), tab["pi"][:], ALU.mult))
                step(tt(tab["fpr"][:], tab["fpr"][:], tab["t9"][:], ALU.subtract))
                step(tt(tab["t9"][:], per_k(fi), tab["pr"][:], ALU.mult))
                step(tt(tab["fpi"][:], tab["fpi"][:], tab["t9"][:], ALU.add))
                ts(tab["nfpr"][:], tab["fpr"][:], -1.0, None, ALU.mult)
                ts(tab["nfpi"][:], tab["fpi"][:], -1.0, None, ALU.mult)
                for j in range(SUB):
                    dve.tensor_copy(rev_r[:, :, j], tab["pr"][:, :, SUB - 1 - j])
                    ins = dve.tensor_copy(rev_i[:, :, j], tab["pi"][:, :, SUB - 1 - j])
                ins.then_inc(tab_done, 1)

            def rotations(n):
                if n == 1:
                    dve.memset(rot_r[:, :, 0:1], 1.0)
                    dve.memset(rot_i[:, :, 0:1], 0.0)
                    dve.tensor_copy(rot_r[:, :, 1:2], tab["cos"][:, :, SUB:SUB + 1])
                    step(dve.tensor_copy(rot_i[:, :, 1:2], tab["sin"][:, :, SUB:SUB + 1]))
                lo, hi = slice(1, n + 1), slice(n + 1, 2 * n + 1)
                wr = rot_r[:, :, n:n + 1].broadcast_to([P, PAIRS, n])
                wi = rot_i[:, :, n:n + 1].broadcast_to([P, PAIRS, n])
                ta = hc[:, 1, PAD:PAD + PAIRS * n].rearrange("p (a k) -> p a k", a=PAIRS)
                tb = hc[:, 2, PAD:PAD + PAIRS * n].rearrange("p (a k) -> p a k", a=PAIRS)
                tt(rot_r[:, :, hi], rot_r[:, :, lo], wr, ALU.mult)
                tt(ta, rot_i[:, :, lo], wi, ALU.mult)
                tt(rot_i[:, :, hi], rot_r[:, :, lo], wi, ALU.mult)
                step(tt(tb, rot_i[:, :, lo], wr, ALU.mult))
                tt(rot_r[:, :, hi], rot_r[:, :, hi], ta, ALU.subtract)
                step(tt(rot_i[:, :, hi], rot_i[:, :, hi], tb, ALU.add))

            def tap(a, k):
                w = vec[:, V_CW + a * WIDTH + k:V_CW + a * WIDTH + k + 1]
                if k == 0:
                    ins = ts(cv[:, a, :], hc[:, a, 0:T], w, vec[:, V_CB + a:V_CB + a + 1], ALU.mult, ALU.add)
                else:
                    dve.wait_ge(tap_done[a], k)
                    ins = stt(cv[:, a, :], hc[:, a, k:k + T], w, cv[:, a, :], ALU.mult, ALU.add)
                ins.then_inc(tap_done[a], 1)

            def scale_rows(dst, src, g0, done):
                for c in range(NC):
                    stt(dst[:, c, :], src[:, c, :], vec[:, g0 + c:g0 + c + 1], rstd[:], ALU.mult, ALU.mult
                        ).then_inc(done, 1)

            def split_lo(n):
                r, s = n // 2, n % 2
                dve.wait_ge(hi_done[s], r + 1)
                tt(w_lo[:, s, :], raw[:, s, :], w_hi[:, s, :].bitcast(F32), ALU.subtract).then_inc(lo_done[s], 1)

            def gate_h(a):
                dve.wait_ge(sig_done, a + 1)
                step(tt(hc[:, a, PAD:PAD + T], hc[:, a, PAD:PAD + T], sg[:, a % 2, :], ALU.mult))
                if a < DCT:
                    tap(a, 0)
                else:
                    dve.sem_inc(h_ready, 1)

            dve.wait_ge(vec_in, 16)
            for c in range(NC):
                dve.wait_ge(rhs_hi_done, c + 1)
                stt(rhs_lo[:, c, :], xuc[:, c, :], vec[:, V_G1 + c:V_G1 + c + 1], rhs_hi[:, c, :].bitcast(F32),
                    ALU.mult, ALU.subtract).then_inc(rhs_done, 1)
            split_lo(0)
            split_lo(1)
            angles()
            dve.wait_ge(std_done, 1)
            step(dve.reciprocal(rstd[:], rstd[:]))
            dve.wait_ge(const_ok, 7)
            between = {0: [powers], 1: [f_powers], 2: [lambda: [rotations(n) for n in (1, 2, 4, 8)]],
                       3: [lambda: rotations(16)], 4: [lambda: rotations(32)]}
            TAPS_A_TILE = 4
            n_taps = 1
            for n in range(WOUT):
                r, s, a = n // 2, n % 2, (n - CT) // 2
                dve.wait_ge(mm_done[s], r + 1)
                if n < CT:
                    tt(u_t[:, n, :].rearrange("p (j c) -> p c j", j=SUB),
                       PS[:, s, :].rearrange("p (c j) -> p c j", j=SUB),
                       rstd[:].rearrange("p (c j) -> p c j", j=SUB), ALU.mult).then_inc(evacuated[s], 1)
                elif s == 0:
                    tt(hc[:, a, PAD:PAD + T], PS[:, 0, :], rstd[:], ALU.mult).then_inc(evacuated[0], 1)
                else:
                    tt(sg[:, a % 2, :], PS[:, 1, :], rstd[:], ALU.mult).then_inc(evacuated[1], 1)
                if n + 2 < WOUT:
                    split_lo(n + 2)
                for work in between.get(n, []):
                    work()
                if n > CT and s == 0:
                    gate_h(a - 1)
                if n > CT + 1:
                    for k in range(n_taps, n_taps + TAPS_A_TILE):
                        tap(0, k)
                    n_taps += TAPS_A_TILE
            gate_h(CT - 1)
            for k in range(n_taps, WIDTH):
                tap(0, k)
            def taps(k0, k1):
                with dve.Fori(k0, k1) as k:
                    for a in range(1, DCT):
                        dve.wait_ge(tap_done[a], k)
                        w = vec[:, bass.ds(k + (V_CW + a * WIDTH), 1)]
                        stt(cv[:, a, :], hc[:, a, bass.ds(k, T)], w, cv[:, a, :], ALU.mult, ALU.add
                            ).then_inc(tap_done[a], 1)

            taps(1, SCAN_AT)
            dve.wait_ge(z_done, 1)
            dve.wait_ge(m2_in, 16 * SUB)
            z_r = PS[:, 4:6, :].rearrange("p b (a c) -> p (b a) c", a=8)
            z_i = PS[:, 6:8, :].rearrange("p b (a c) -> p (b a) c", a=8)
            v3 = lambda x: x.rearrange("p (a c) -> p a c", a=PAIRS)
            rr, ri = rot_r[:, :, 0:NSUB], rot_i[:, :, 0:NSUB]
            tt(v3(za), z_r, rr, ALU.mult)
            step(tt(v3(zt), z_i, ri, ALU.mult))
            step(tt(za, za, zt, ALU.add))
            tt(v3(zb), z_i, rr, ALU.mult)
            tt(v3(zt), z_r, ri, ALU.mult).then_inc(z_read, 1)
            dve.wait_ge(z_read, 1)
            step(tt(zb, zb, zt, ALU.subtract))
            dve.tensor_copy(v3(zt), tab["mag"][:, :, SUB:SUB + 1].broadcast_to([P, PAIRS, NSUB]))
            step(dve.memset(small[:, 11, :], 0.0))
            step(dve.tensor_copy(v3(zt)[:, :, 0], small[:, 11, :]))
            step(dve.tensor_tensor_scan(zc, zt, za, 0.0, ALU.mult, ALU.add))
            step(dve.tensor_tensor_scan(za, zt, zb, 0.0, ALU.mult, ALU.add))
            dve.tensor_copy(sp_r[:, :, 0], small[:, 11, :])
            dve.tensor_copy(sp_i[:, :, 0], small[:, 11, :])
            tt(v3(zb), v3(zc), rr, ALU.mult)
            step(tt(v3(zt), v3(za), ri, ALU.mult))
            tt(sp_r[:, :, 1:NSUB + 1], v3(zb), v3(zt), ALU.subtract)
            step(tt(sp_i[:, :, 1:NSUB + 1], v3(zc), ri, ALU.mult))
            step(tt(v3(zb), v3(za), rr, ALU.mult))
            tt(sp_i[:, :, 1:NSUB + 1], sp_i[:, :, 1:NSUB + 1], v3(zb), ALU.add).then_inc(sp_done, 1)
            taps(SCAN_AT, WIDTH)

            dve.wait_ge(diag_used, WIDTH)
            ts(cv[:, DCT, :], PS[:, 3, :], vec[:, V_CB + DCT:V_CB + DCT + 1], None, ALU.add).then_inc(cv3_done, 1)
            dve.wait_ge(mean_done, 1)
            step(ts(sg[:, 1, :], PS[:, 2, :], 1.0 / (CT * P), None, ALU.mult))
            for a in range(CT):
                tt(cv[:, a, :], cv[:, a, :], sg[:, 1, :], ALU.subtract).then_inc(xc_done, 1)
            dve.wait_ge(cstd_done, 1)
            step(dve.reciprocal(sg[:, 0, :], sg[:, 0, :]))
            for a in range(CT):
                dve.wait_ge(csq_done, a + 1)
                dve.wait_ge(xc_done, a + 1)
                tt(cv[:, a, :], cv[:, a, :], sg[:, 0, :], ALU.mult).then_inc(hn_done, 1)
            for a in range(CT):
                dve.wait_ge(rhs_hi_done, NC + a + 1)
                tt(rhs_lo[:, CT + a, :], cv[:, a, :], rhs_hi[:, CT + a, :].bitcast(F32), ALU.subtract
                   ).then_inc(rhs_done, 1)

            def residual(n):
                r, s = R_WOUT + n // 2, n % 2
                if n >= 4:
                    dve.wait_ge(evacuated[s], r - 1)
                dve.wait_ge(half_done, n + 1)
                m = (n % 4) * 2
                tt(x2[:, m, :], PS[:, 2 * s, :], x2[:, m, :], ALU.add).then_inc(x2_done, 1)
                dve.wait_ge(mm_done[s], r + 1)
                tt(x2[:, m + 1, :], PS[:, 2 * s + 1, :], x2[:, m + 1, :], ALU.add).then_inc(evacuated[s], 1)

            dve.wait_ge(y_in, 16 * GPT)
            for a in range(CT):
                stt(y_t[:, a, :], u_t[:, a, :], vec[:, V_D + a:V_D + a + 1], y_t[:, a, :], ALU.mult, ALU.add
                    ).then_inc(ypre_done, 1)
            dve.wait_ge(x_again, 16)
            for n in range(GLU_AT):
                residual(n)
            for a in range(CT):
                dve.wait_ge(gsig_done, a + 1)
                tt(y_t[:, a, :], y_t[:, a, :], ysb[:, a * T:(a + 1) * T], ALU.mult).then_inc(yssm_done, 1)
            for a in range(CT):
                dve.wait_ge(rhs_hi_done, NC + CT + a + 1)
                order = "p (c i) -> p i c"
                tt(rhs_lo[:, a, :].rearrange(order, i=SUB), y_t[:, a, :].rearrange("p (i c) -> p i c", i=SUB),
                   rhs_hi[:, a, :].bitcast(F32).rearrange(order, i=SUB), ALU.subtract).then_inc(rhs_done, 1)
            for n in range(GLU_AT, NC):
                residual(n)
            dve.wait_ge(std2_done, 1)
            step(dve.reciprocal(rstd[:], rstd[:]))
            scale_rows(sq, x2, V_G2, xn_done)
            for c in range(NC):
                dve.wait_ge(xhi_done, c + 1)
                tt(rhs_lo[:, c, :], sq[:, c, :], rhs_hi[:, c, :].bitcast(F32), ALU.subtract).then_inc(xn_ready, 1)

            blocks = range(TB)
            halves = [(h, b) for h in range(2) for b in blocks]
            STAGES = 11
            with dve.Fori(0, HEADS) as it:
                n = 0

                def stage(ins):
                    nonlocal n
                    n += 1
                    ins.then_inc(top_done, 1)
                    dve.wait_ge(top_done, it * STAGES + n)
                    dve.tensor_copy(gsum[:, 1, 0:1], epsc[:])

                def top16(v, i, src, cut):
                    rows = range(len(v))
                    for j in rows:
                        ins = dve.max(v[j][:, 0:8], src[j])
                    stage(ins)
                    for j in rows:
                        dve.max_index(i[j][:, 0:8], v[j][:, 0:8], src[j])
                        ins = dve.match_replace(cut[j], v[j][:, 0:8], src[j], NEG)
                    stage(ins)
                    for j in rows:
                        ins = dve.max(v[j][:, 8:16], cut[j])
                    stage(ins)
                    for j in rows:
                        ins = dve.max_index(i[j][:, 8:16], v[j][:, 8:16], cut[j])
                    stage(ins)

                dve.wait_ge(s_out, it * 2 + 3)
                stage(dve.tensor_copy(s_cur[:].rearrange("p a b n -> p a (b n)"), s_all[:, bass.ds(it * 2, 2), :]))
                top16([topv[:, h, b, :] for h, b in halves], [topi[:, h, b, :] for h, b in halves],
                      [s_cur[:, h, b, :] for h, b in halves], [s_cut[:, h, b, :] for h, b in halves])
                for k, dst in enumerate((i1_all, i2_all)):
                    dve.tensor_copy(dst[:, :, bass.ds(it, 1), :].rearrange("p b o k -> p b (o k)"), topi[:, k])
                for b in blocks:
                    ins = tt(cand[:, b, :].rearrange("p (i j) -> p i j", i=TOPK),
                             topv[:, 0, b, :].rearrange("p (i j) -> p i j", j=1).broadcast_to([P, TOPK, TOPK]),
                             topv[:, 1, b, :].rearrange("p (i j) -> p i j", i=1).broadcast_to([P, TOPK, TOPK]),
                             ALU.add)
                stage(ins)
                top16([selv[:, b, :] for b in blocks], [seli[:, b, :] for b in blocks],
                      [cand[:, b, :] for b in blocks], [cand_cut[:, b, :] for b in blocks])
                dve.tensor_copy(sel_all[:, :, bass.ds(it, 1), :].rearrange("p b o k -> p b (o k)"), selv[:])
                stage(dve.tensor_copy(ci_all[:, :, bass.ds(it, 1), :].rearrange("p b o k -> p b (o k)"), seli[:]))
            scores = sel_all[:].rearrange("p b h k -> p (b h) k")
            per_head = lambda x: x.rearrange("p (n o) -> p n o", o=1).broadcast_to([P, TB * HEADS, TOPK])
            step(dve.tensor_copy(gsum[:, 0, :], scores[:, :, 0]))
            tt(scores, scores, per_head(gsum[:, 0, :]), ALU.subtract).then_inc(sub_done, 1)
            ci = ci_all[:].rearrange("p b h k -> p b (h k)")
            step(ts(pos[:], ci, 4, None, ALU.logical_shift_right))
            step(dve.tensor_copy(pos_a[:], pos[:]))
            step(ts(pos[:], ci, TOPK - 1, None, ALU.bitwise_and))
            step(dve.tensor_copy(pos_b[:], pos[:]))
            eq3 = eq[:].rearrange("p (n j) -> p n j", j=TOPK)
            eq4 = eq[:].rearrange("p (h k j) -> p h k j", h=HEADS, k=TOPK)
            with dve.Fori(0, TB) as it:
                for k, (where, idx, dst) in enumerate(((pos_a, i1_all, e1), (pos_b, i2_all, e2))):
                    w = where[:, bass.ds(it, 1), :].rearrange("p b (n o) -> p (b n) o", o=1)
                    tt(eq3, w.broadcast_to([P, P, TOPK]),
                       iota16[:].rearrange("p (n j) -> p n j", n=1).broadcast_to([P, P, TOPK]), ALU.is_equal
                       ).then_inc(key_done, 1)
                    dve.wait_ge(key_done, it * 6 + (3 * k + 1))
                    i4 = idx[:, bass.ds(it, 1), :, :].rearrange("p b h (o j) -> p (b h) o j", o=1)
                    tt(eq4, eq4, i4.broadcast_to([P, HEADS, TOPK, TOPK]), ALU.mult).then_inc(key_done, 1)
                    dve.wait_ge(key_done, it * 6 + (3 * k + 2))
                    dve.tensor_reduce(dst[:, bass.ds(it, 1), :].rearrange("p b n -> p (b n)"), eq3, AX_X, ALU.add
                                      ).then_inc(key_done, 1)
                    dve.wait_ge(key_done, it * 6 + (3 * k + 3))
            dve.wait_ge(exp_done, 1)
            step(dve.tensor_reduce(gsum[:, 0, :], scores, AX_X, ALU.add))
            step(dve.reciprocal(gsum[:, 1, :], gsum[:, 0, :]))
            step(tt(scores, scores, per_head(gsum[:, 1, :]), ALU.mult))
            dve.tensor_copy(iota_h[:], iota_row[:])
            with dve.Fori(0, TB) as it:
                for k, src in enumerate((e1, e2, sel_all)):
                    view = src[:] if k < 2 else src[:].rearrange("p b h k -> p b (h k)")
                    ins = dve.tensor_copy(sel_now[:, k, :], view[:, bass.ds(it, 1), :].rearrange("p a n -> p (a n)"))
                ins.then_inc(sel_done, 1)
                dve.wait_ge(selT_done, it + 1)
                dve.tensor_copy(e1T[:], PS[:, 6, 0:P])
                dve.tensor_copy(e2T[:], PS[:, 6, P:2 * P])
                ts(gT[:], PS[:, 6, 2 * P:3 * P], GSCALE, None, ALU.mult)
                ts(ghT[:], PS[:, 6, 2 * P:3 * P], GSCALE, None, ALU.mult).then_inc(selT_out, 1)
                dve.wait_ge(selT_out, it * 2 + 2)
                dve.tensor_copy(ghTf[:], ghT[:])
                tt(glT[:], gT[:], ghT[:], ALU.subtract).then_inc(selT_out, 1)
                dve.wait_ge(selT_out, it * 2 + 3)
                for q in range(TURN_TILES):
                    for b in range(TILE_GROUPS):
                        o = (q % 2) * TILE_GROUPS + b
                        dve.wait_ge(g_mm[o], it * SLOT_USES + (q // 2 + 1))
                        for t in range(GROUP):
                            col = slice(q * STEP_TOK + b * GROUP + t, q * STEP_TOK + b * GROUP + t + 1)
                            ts(oh_1[:, o, t, :], iota_h[:], e1T[:, col], None, ALU.is_equal)
                            ts(oh_gh[:, o, t, :], iota_h[:], e2T[:, col], ghTf[:, col], ALU.is_equal, ALU.mult)
                            ins = ts(oh_gl[:, o, t, :], iota_h[:], e2T[:, col], glT[:, col],
                                     ALU.is_equal, ALU.mult)
                        ins.then_inc(oh_done[o], 1)
            with dve.Fori(0, KEYS // 4) as it:
                for g in range(2):
                    dve.wait_ge(ga_in[g], it * 32 + 32)
                    for s in range(2):
                        dve.wait_ge(mm_done[s], it * 2 + (R_V + g))
                        n = it * 8 + (4 * g + 2 * s)
                        tt(wt[:, s, :].rearrange("p (a t) -> p a t", t=GCH),
                           a_in[:, g, s, :].rearrange("p (a t) -> p a t", t=GCH), g_in[:, g, :, s, :], ALU.mult
                           ).then_inc(wt_part, 1)
                        dve.wait_ge(wt_part, n + 1)
                        dve.tensor_copy(wt_hi[:, s, :], wt[:, s, :]).then_inc(wt_part, 1)
                        dve.wait_ge(wt_part, n + 2)
                        tt(wt_lo[:, s, :], wt[:, s, :], wt_hi[:, s, :].bitcast(F32), ALU.subtract
                           ).then_inc(wt_done[s], 1)
            for m in range(NC):
                dve.wait_ge(peer_done, m + 1)
                tt(x2[:, m, :], PS[:, m, :], x2[:, m, :], ALU.add).then_inc(fin_done, 1)
            dve.wait_ge(fstd_done, 1)
            step(dve.reciprocal(rstd[:], rstd[:]))
            scale_rows(x2, x2, V_GF, out_ready)


def kernel(**inputs):
    import concourse.bacc as bacc
    from concourse.bass_utils import run_bass_kernel_spmd

    a = {k: np.asarray(v) for k, v in inputs.items()}
    layer = {k: v[0] for k, v in a.items() if k not in ("x", "final_g")}

    def channels(v):
        return v.reshape(-1, P).T

    def states(v):
        return v.reshape(PAIRS, 2, STATE, -1).transpose(1, 2, 0, 3).reshape(P, -1)

    cw = layer["conv_w"].T.reshape(CT, P, WIDTH).transpose(1, 0, 2).reshape(P, -1)
    vecs = np.concatenate([channels(layer["norm1_g"]), channels(layer["norm2_g"]), channels(a["final_g"]),
                           channels(layer["conv_b"]), channels(layer["conv_ln_g"]), channels(layer["conv_ln_b"]),
                           channels(layer["ssm_d"]), channels(layer["glu_b"]), cw], axis=1)
    log_dt = np.broadcast_to(layer["log_dt"][:, None], (GROUPS, STATE))
    ssm = np.concatenate([states(layer["lam_re"]), states(layer["lam_im"]), states(log_dt),
                          states(layer["ssm_b_re"]), states(layer["ssm_b_im"]),
                          states(layer["ssm_c_re"].transpose(0, 2, 1)),
                          states(layer["ssm_c_im"].transpose(0, 2, 1))], axis=1)
    xT = a["x"][0].T.reshape(NC, P, T).transpose(1, 0, 2)
    glu_bd = np.zeros((P, CT, P), np.float32)
    for g in range(GROUPS):
        q = g % GPT
        glu_bd[q * CH:(q + 1) * CH, g // GPT, q * CH:(q + 1) * CH] = layer["glu_w"][g]
    keys = np.stack([layer["peer_k1"].T, layer["peer_k2"].T], axis=1)

    def columns(w):
        return w.reshape(NC, P, -1, P).transpose(2, 1, 0, 3).reshape(-1, P, D)

    w_in = columns(layer["w_in"])
    order = [0, 1, 2, 3] + [i for a4 in range(CT) for i in (CT + a4, 2 * CT + a4)]
    u = layer["peer_u"].reshape(KEYS, KEYS, NC, P).transpose(1, 3, 2, 0).reshape(KEYS, P, D)
    v = layer["peer_v"].reshape(KEYS, KEYS, D).transpose(1, 0, 2)
    w_out = layer["w_out"].reshape(2, CT, P, NC // 2, 2, P).transpose(0, 3, 2, 4, 1, 5).reshape(2, -1, P, D)[::-1]
    tiles = np.concatenate([w_in[order], w_out.reshape(-1, P, D), columns(layer["peer_wq"]), u, v])

    nc = bacc.Bacc("TRN2", target_bir_lowering=False, num_devices=1)
    arrays, args = {}, []
    for name, arr in (("vecs", vecs), ("ssm", ssm), ("xT", xT), ("glu_bd", glu_bd), ("keys", keys),
                      ("tiles", tiles)):
        arrays[name] = np.ascontiguousarray(arr)
        args.append(nc.dram_tensor(name, arrays[name].shape, F32, kind="ExternalInput").ap())
    outT = nc.dram_tensor("outT", (P, NC, T), F32, kind="ExternalOutput").ap()
    build(nc, *args, outT)
    result = run_bass_kernel_spmd(nc, [arrays], core_ids=[0])
    got = result.results[0]["outT"]
    return got.transpose(1, 0, 2).reshape(D, T).T[None]
```

```python
from contextlib import ExitStack

import numpy as np

import concourse.bass as bass
from concourse import mybir

F32 = mybir.dt.float32
F32R = mybir.dt.float32r
F16 = mybir.dt.float16
U32 = mybir.dt.uint32
ALU = mybir.AluOpType
ACT = mybir.ActivationFunctionType
AX_X = mybir.AxisListType.X

P = 128
D = 1024
T = 512
NC = D // P
GROUPS, CH, STATE = 32, 16, 64
PAIRS = GROUPS // 2
SUB = P // CH
NSUB = T // SUB
CT = 4
GPT = GROUPS // CT
WIDTH = 31
DCT = 3
PE_TAP = 19
GP_TAP = 13
PAD = WIDTH - 1
HEADS, KEYS, TOPK = 8, 128, 16
TB = T // P
EPS = 1e-6

WIN, WOUT, WQ = 0, 12, 20
UT = WQ + 2 * HEADS
VT = UT + KEYS
NTILES = VT + KEYS

ALONE = 32
STEP_TOK = 8
SPREAD = T // STEP_TOK
GROUP = 4
GCH = 64
PIECES = 4
OH = 4
GSCALE = 16384.0
GP_OUT = (1, 4, 7)
ZERO_AT = 16
Y_OUT_AT = (28, 30)
SCAN_AT = 13
EXP_AT = 18

V_G1, V_G2, V_GF, V_CB, V_LG, V_LB, V_D, V_GB, V_CW = 0, 8, 16, 24, 28, 32, 36, 40, 44
NV = V_CW + CT * WIDTH
S_LR, S_LI, S_DT, S_BR, S_BI, S_CR, S_CI = 0, 16, 32, 48, 304, 560, 816
NS = 1072
NEG = -3.0e38
TWO_PI = (6.28125, 0.0019350051879882812, 3.019916050e-07)
MAGIC = 12582912.0
PI_IN = 3.1415925


def wait(eng, sem, value):
    if not (isinstance(value, int) and value <= 0):
        eng.wait_ge(sem, value)


class Chain:

    def __init__(self, eng, sem):
        self.eng, self.sem, self.n = eng, sem, 0

    def step(self, ins):
        ins.then_inc(self.sem, 1)
        self.n += 1
        self.eng.wait_ge(self.sem, self.n)


def build(nc, vecs, ssm, xT, glu_bd, keys, tiles, outT):
    with ExitStack() as ctx:
        def sb(name, shape, dt=F32, c=ctx):
            return c.enter_context(nc.sbuf_tensor(name, shape, dt))

        def sem(name):
            return ctx.enter_context(nc.semaphore(name))

        vec = sb("vec", [P, NV])
        ones = sb("ones", [P, P])
        ident = sb("ident", [P, P])
        iota_row = sb("iota_row", [P, P])
        iota16 = sb("iota16", [P, TOPK])
        epsc = sb("epsc", [P, 1])
        gelu_warm = sb("gelu_warm", [P, 1])
        rstd = sb("rstd", [P, T])
        x2 = sb("x2", [P, NC, T])
        rhs_hi = sb("rhs_hi", [P, NC, T], F32R)
        rhs_lo = sb("rhs_lo", [P, NC, T], F32R)
        raw = sb("raw", [P, 2, D])
        w_hi = sb("w_hi", [P, 2, D], F32R)
        w_lo = sb("w_lo", [P, 2, D], F32R)
        keyT = sb("keyT", [P, 2, KEYS])
        PS = ctx.enter_context(nc.psum_tensor("PS", [P, 8, T], F32))

        u_scr = nc.dram_tensor("u_scr", [SUB, CH, GROUPS, NSUB], F32).ap()
        y_scr = nc.dram_tensor("y_scr", [2, SUB, CH, GROUPS // 2, NSUB], F32).ap()
        act_scr = nc.dram_tensor("act_scr", [KEYS, P, T], F32).ap()
        gate_scr = nc.dram_tensor("gate_scr", [P, T // GCH, KEYS * GCH], F32).ap()

        pre = ExitStack()
        prm = sb("prm", [P, NS], F32, pre)
        bd = sb("bd", [P, CT, P], F32, pre)
        xuc = sb("xuc", [P, NC, T], F32, pre)
        hc = sb("hc", [P, CT, PAD + T], F32, pre)
        sg = sb("sg", [P, 2, T], F32, pre)
        names = ("kk", "exps", "phi", "turns", "red", "half", "mag", "sin", "sinh", "cos", "pr", "pi",
                 "fpr", "fpi", "nfpr", "nfpi", "t9")
        tab = {n: sb("tab_" + n, [P, PAIRS, SUB + 1], F32, pre) for n in names}
        rev_r = sb("rev_r", [P, PAIRS, SUB], F32, pre)
        rev_i = sb("rev_i", [P, PAIRS, SUB], F32, pre)
        small = sb("small", [P, 12, PAIRS], F32, pre)
        cp_r = sb("cp_r", [P, PAIRS, SUB + 1, CH], F32, pre)
        cp_i = sb("cp_i", [P, PAIRS, SUB + 1, CH], F32, pre)
        m1 = sb("m1", [P, 2, PAIRS, P], F32, pre)
        rot_r = sb("rot_r", [P, PAIRS, NSUB + 1], F32, pre)
        rot_i = sb("rot_i", [P, PAIRS, NSUB + 1], F32, pre)
        big = sb("big", [P, 8192], F32, pre)
        prod = sb("prod", [P, 2, T], F32, pre)
        pre.close()
        u_t = xuc[:, 0:CT, :]
        cv = xuc[:, CT:NC, :]
        gp_taps = [(DCT, k) for k in range(PE_TAP)] + [(DCT - 1, k) for k in range(GP_TAP, WIDTH)]
        gp_sum = {DCT: cv[:, DCT, :], DCT - 1: sg[:, 0, :]}
        m2 = x2[:].rearrange("p c t -> p (c t)").rearrange("p (g m) -> p g m", g=GROUPS)
        tmp = big[:, 0:PAIRS * (SUB + 1) * CH]
        kimp = big[:, 0:4096].rearrange("p (g m) -> p g m", g=GROUPS)
        za, zb, zc, zt = (big[:, i * 1024:(i + 1) * 1024] for i in range(4))
        ysb = big[:, 0:2048]
        Y_BANKS = (2, 3, 6, 7)
        sq = big[:, 4096:8192].rearrange("p (c t) -> p c t", c=NC)
        ab_r = big[:, 4096:6144].rearrange("p (a j h) -> p a j h", a=PAIRS, j=SUB)
        ab_i = big[:, 6144:8192].rearrange("p (a j h) -> p a j h", a=PAIRS, j=SUB)
        u_sub = big[:, 4096:6144].rearrange("p (g c) -> p g c", g=GROUPS)
        diag = big[:, 6144:8192].rearrange("p (k c) -> p k c", c=P)
        states_r, states_i = m1[:, 0], m1[:, 1]
        y_t = big[:, 4096:6144].rearrange("p (a t) -> p a t", a=CT)

        peer = ExitStack()
        act_sb = sb("act_sb", [P, 2, T], F32, peer)
        q_sb = sb("q_sb", [P, 2, T], F32, peer)
        oh_1 = sb("oh_1", [P, OH, GROUP, KEYS], F16, peer)
        oh_gh = sb("oh_gh", [P, OH, GROUP, KEYS], F16, peer)
        oh_gl = sb("oh_gl", [P, OH, GROUP, KEYS], F16, peer)
        iota_h = sb("iota_h", [P, KEYS], F16, peer)
        e1T = sb("e1T", [P, P], F32, peer)
        e2T = sb("e2T", [P, P], F32, peer)
        gT = sb("gT", [P, P], F32, peer)
        ghT = sb("ghT", [P, P], F16, peer)
        ghTf = sb("ghTf", [P, P], F32, peer)
        glT = sb("glT", [P, P], F32, peer)
        topv = sb("topv", [P, 2, TB, TOPK], F32, peer)
        topi = sb("topi", [P, 2, TB, TOPK], U32, peer)
        selv = sb("selv", [P, TB, TOPK], F32, peer)
        seli = sb("seli", [P, TB, TOPK], U32, peer)
        sel_all = sb("sel_all", [P, TB, HEADS, TOPK], F32, peer)
        ci_all = sb("ci_all", [P, TB, HEADS, TOPK], U32, peer)
        i1_all = sb("i1_all", [P, TB, HEADS, TOPK], F32, peer)
        i2_all = sb("i2_all", [P, TB, HEADS, TOPK], F32, peer)
        pos = sb("pos", [P, TB, P], U32, peer)
        pos_a = sb("pos_a", [P, TB, P], F32, peer)
        pos_b = sb("pos_b", [P, TB, P], F32, peer)
        e1 = sb("e1", [P, TB, P], F32, peer)
        e2 = sb("e2", [P, TB, P], F32, peer)
        sel_now = sb("sel_now", [P, 3, P], F32, peer)
        gsum = sb("gsum", [P, 2, TB * HEADS], F32, peer)
        route = ExitStack()
        s_all = sb("s_all", [P, 2 * HEADS, T], F32, route)
        s_cur = sb("s_cur", [P, 2, TB, KEYS], F32, route)
        s_cut = sb("s_cut", [P, 2, TB, KEYS], F32, route)
        cand = sb("cand", [P, TB, TOPK * TOPK], F32, route)
        cand_cut = sb("cand_cut", [P, TB, TOPK * TOPK], F32, route)
        eq = sb("eq", [P, P * TOPK], F32, route)
        route.close()
        gst = sb("gst", [P, 2, KEYS, GCH], F32, peer)
        peer.close()
        late = ExitStack()
        fsq = sb("fsq", [P, NC, T], F32, late)
        wt = sb("wt", [P, 2, T], F32, late)
        wt_hi = sb("wt_hi", [P, 2, T], F32R, late)
        wt_lo = sb("wt_lo", [P, 2, T], F32R, late)
        g_in = sb("g_in", [P, 2, T // GCH, 2, GCH], F32, late)
        a_in = sb("a_in", [P, 2, 2, T], F32, late)
        xg = sb("xg", [P, 3, T], F32, late)
        late.close()

        vec_in, prm_in, bd_in, key_in, x_again = map(sem, (
            "vec_in", "prm_in", "bd_in", "key_in", "x_again"))
        x_in = [sem(f"x_in{c}") for c in range(NC // 2)]
        raw_full = [sem(f"raw_full{s}") for s in range(2)]
        hi_done = [sem(f"hi_done{s}") for s in range(2)]
        lo_done = [sem(f"lo_done{s}") for s in range(2)]
        mm_done = [sem(f"mm_done{s}") for s in range(2)]
        evacuated = [sem(f"evacuated{s}") for s in range(2)]
        act_stored = [sem(f"act_stored{s}") for s in range(2)]
        const_ok, iota_ok = sem("const_ok"), sem("iota_ok")
        dve_chain = sem("dve_chain")
        sq_done, ms_done, std_done, rhs_hi_done, rhs_done = map(sem, (
            "sq_done", "ms_done", "std_done", "rhs_hi_done", "rhs_done"))
        dt_done, angle_done, trig_done, tab_done, ab_done, cp_done = map(sem, (
            "dt_done", "angle_done", "trig_done", "tab_done", "ab_done", "cp_done"))
        m1_part, m1_out, k_part, k_out, m2_zero, m2_in = map(sem, (
            "m1_part", "m1_out", "k_part", "k_out", "m2_zero", "m2_in"))
        u_stored, u_in, z_done, z_read, sp_done, m2_used, y_done, y_out = map(sem, (
            "u_stored", "u_in", "z_done", "z_read", "sp_done", "m2_used", "y_done", "y_out"))
        y_stored = [sem(f"y_stored{h}") for h in range(2)]
        y_in = [sem(f"y_in{h}") for h in range(2)]
        ypre_done, gelu_done, glu_done, gsig_done, yssm_done = map(sem, (
            "ypre_done", "gelu_done", "glu_done", "gsig_done", "yssm_done"))
        tap_done = [sem(f"tap_done{a}") for a in range(DCT)]
        h_ready, pool_chain, sig_done, prod_done, prod_used, cv3_done = map(sem, (
            "h_ready", "pool_chain", "sig_done", "prod_done", "prod_used", "cv3_done"))
        mean_done, xc_done, csq_done, var_done, cstd_done, hn_done, silu_done = map(
            sem, ("mean_done", "xc_done", "csq_done", "var_done",
                  "cstd_done", "hn_done", "silu_done"))
        half_done, x2_done, states_zero = sem("half_done"), sem("x2_done"), sem("states_zero")
        diag_done, pe_taps = sem("diag_done"), sem("pe_taps")
        last_pair = sem("last_pair")
        pair_done, scaled, rstd_done, out_gp = map(sem, ("pair_done", "scaled", "rstd_done", "out_gp"))
        sum_done, sum2_done, xn_odd = sem("sum_done"), sem("sum2_done"), sem("xn_odd")
        sq2_done, ms2_done, std2_done, xn_done, xhi_done, xn_ready = map(sem, (
            "sq2_done", "ms2_done", "std2_done", "xn_done", "xhi_done", "xn_ready"))
        s_done, s_out, top_done, key_done, sub_done, exp_done, sel_done, selT_done, selT_out, wt_part = map(sem, (
            "s_done", "s_out", "top_done", "key_done", "sub_done", "exp_done", "sel_done", "selT_done", "selT_out",
            "wt_part"))
        oh_done = [sem(f"oh_done{s}") for s in range(OH)]
        g_mm = [sem(f"g_mm{s}") for s in range(OH)]
        g_out = [sem(f"g_out{s}") for s in range(OH)]
        g_stored = [sem(f"g_stored{s}") for s in range(2)]
        ga_in = [sem(f"ga_in{s}") for s in range(2)]
        wt_done = [sem(f"wt_done{s}") for s in range(2)]
        peer_done, fin_done, fsq_done, fms_done, fstd_done, out_ready, out_stored = map(sem, (
            "peer_done", "fin_done", "fsq_done", "fms_done", "fstd_done", "out_ready", "out_stored"))

        block = ctx.enter_context(nc.Block())

        TURN_TILES = SPREAD // TB
        TILE_GROUPS = STEP_TOK // GROUP
        SLOT_USES = P // GROUP // OH
        R_WOUT, R_WQ, R_U, R_V = WOUT // 2, WQ // 2, UT // 2, VT // 2
        R_SPREAD = R_U + ALONE // 2
        R_REST = R_SPREAD + SPREAD // 2

        @block.sync
        def _(sp):
            def load(r, s):
                wait(sp, lo_done[s], r)
                sp.dma_start(raw[:, s, :], tiles[2 * r + s, :, :] if isinstance(r, int) else
                             tiles[bass.ds(r * 2 + s, 1), :, :].rearrange("a p n -> (a p) n")
                             ).then_inc(raw_full[s], 16)

            sp.dma_start(vec[:], vecs).then_inc(vec_in, 16)
            for c in range(NC // 2):
                sp.dma_start(xuc[:, 2 * c:2 * c + 2, :], xT[:, 2 * c:2 * c + 2, :]).then_inc(x_in[c], 16)
                if c == 1:
                    load(0, 0)
            sp.dma_start(prm[:], ssm).then_inc(prm_in, 16)
            load(0, 1)
            sp.dma_start(bd[:], glu_bd).then_inc(bd_in, 16)
            sp.dma_start(keyT[:], keys).then_inc(key_in, 16)
            for r in range(1, 4):
                load(r, 0)
                load(r, 1)
            for s in range(2):
                sp.wait_ge(evacuated[s], 2)
            for q in range(GPT):
                sp.dma_start(u_scr.rearrange("j h (a q) c -> q h a j c", q=GPT)[q],
                             u_t[q * CH:(q + 1) * CH].rearrange("h a (j c) -> h a j c", j=SUB)
                             ).then_inc(u_stored, 16)
            for r in range(4, R_WOUT + 1):
                load(r, 0)
                load(r, 1)
            sp.wait_ge(u_stored, 16 * GPT)
            sp.wait_ge(m1_part, 8)
            sp.dma_start(u_sub, u_scr.rearrange("j h g c -> (j h) g c")).then_inc(u_in, 16)
            sp.wait_ge(m2_zero, 1)
            sp.wait_ge(k_out, 8)
            for j in range(SUB):
                n = (SUB - j) * CH
                sp.dma_start(m2[j * CH:(j + 1) * CH, :, j * CH:P], kimp[0:CH, :, 0:n]).then_inc(m2_in, 16)
            load(R_WOUT + 1, 0)
            load(R_WOUT + 1, 1)
            sp.wait_ge(m2_used, 1)
            sp.dma_start(x2[:], xT).then_inc(x_again, 16)
            for half in range(2):
                cols = slice(half * 1024, (half + 1) * 1024)
                sp.wait_ge(y_out, 2 * half + 2)
                sp.dma_start(y_scr[half].rearrange("i h g c -> (i h) (g c)"), ysb[:, cols]
                             ).then_inc(y_stored[half], 16)
            for half in range(2):
                part = slice(half * CT // 2, (half + 1) * CT // 2)
                sp.wait_ge(y_stored[half], 16)
                for q in range(GPT):
                    sp.dma_start(y_t[q * CH:(q + 1) * CH, part].rearrange("h a (i c) -> h a i c", i=SUB),
                                 y_scr[half].rearrange("i h (a q) c -> q h a i c", q=GPT)[q]
                                 ).then_inc(y_in[half], 16)
            for r in range(R_WOUT + 2, R_WQ + 1):
                load(r, 0)
                load(r, 1)
            with sp.Fori(0, HEADS) as it:
                for s in range(2):
                    load(it + (R_WQ + 1), s)

            def u_step(r, j, s):
                load(r + 1 + s, 1 - s)
                sp.wait_ge(evacuated[s], r + 1)
                sp.dma_start(act_scr[j, :, :] if isinstance(j, int) else
                             act_scr[bass.ds(j, 1), :, :].rearrange("a p t -> (a p) t"),
                             act_sb[:, s, :]).then_inc(act_stored[s], 16)

            load(R_U + 1, 0)
            with sp.Fori(0, ALONE // 2) as it:
                for s in range(2):
                    u_step(it + R_U, it * 2 + s, s)

            def store_piece(turn, half, k):
                if k == 0:
                    for b in range(OH):
                        sp.wait_ge(g_out[b], turn * SLOT_USES + ((half + 1) * SLOT_USES // 2 + 1))
                n = KEYS // PIECES
                chunk = turn * 2 + half
                dst = gate_scr[:, chunk:chunk + 1] if isinstance(turn, int) else gate_scr[:, bass.ds(chunk, 1)]
                sp.dma_start(dst[:, :, k * n * GCH:(k + 1) * n * GCH].rearrange("p a n -> p (a n)"),
                             gst[:, half, k * n:(k + 1) * n].rearrange("p i t -> p (i t)")
                             ).then_inc(g_stored[half], 16)

            def spread_step(turn, q):
                u_step(turn * (TURN_TILES // 2) + (R_SPREAD + q // 2), turn * TURN_TILES + (ALONE + q), q % 2)
                if TURN_TILES // 2 <= q < TURN_TILES // 2 + PIECES:
                    store_piece(turn, 0, q - TURN_TILES // 2)

            for q in range(PIECES):
                spread_step(0, q)
            with sp.Fori(0, TB - 1) as it:
                for q in range(PIECES, TURN_TILES):
                    spread_step(it, q)
                for q in range(PIECES):
                    spread_step(it + 1, q)
                    store_piece(it, 1, q)
            for q in range(PIECES, TURN_TILES):
                spread_step(TB - 1, q)
            for q in range(2 * PIECES):
                u_step(R_REST + q // 2, ALONE + SPREAD + q, q % 2)
                if q % 2 == 1:
                    store_piece(TB - 1, 1, q // 2)
            rest = (KEYS - ALONE - SPREAD) // 2
            with sp.Fori(PIECES, rest - 3) as it:
                for s in range(2):
                    u_step(it + R_REST, it * 2 + (ALONE + SPREAD + s), s)

            g_rows = gate_scr.rearrange("p a (i n) -> i p a n", n=2 * GCH)
            a_rows = act_scr.rearrange("(i b) p t -> i p b t", b=2)

            def load_ga(j, s, k):
                for b in range(2):
                    wait(sp, wt_done[b], k)
                sp.dma_start(g_in[:, s].rearrange("p a b t -> p a (b t)"),
                             g_rows[bass.ds(j, 1)].rearrange("i p a n -> (i p) a n")).then_inc(ga_in[s], 16)
                sp.dma_start(a_in[:, s], a_rows[bass.ds(j, 1)].rearrange("i p b t -> (i p) b t")
                             ).then_inc(ga_in[s], 16)

            for s in range(2):
                sp.wait_ge(g_stored[s], 16 * PIECES * (TB + 1))
                sp.wait_ge(act_stored[s], 16 * (2 + 1))
            for k in range(rest - 3, rest):
                for s in range(2):
                    u_step(R_REST + k, ALONE + SPREAD + 2 * k + s, s)
                if k < rest - 1:
                    load_ga(k - rest + 3, k - rest + 3, 0)
            for s in range(2):
                sp.wait_ge(act_stored[s], 16 * (KEYS // 2 + 1))
            with sp.Fori(0, KEYS // 4 - 1) as it:
                for g in range(2):
                    load(it * 2 + (R_V + 1 + g), 1)
                    load(it * 2 + (R_V + 2 + g), 0)
                    load_ga(it * 2 + (2 + g), g, it * 2 + (1 + g))
            load(R_V + KEYS // 2 - 1, 1)
            n_out = {False: 0, True: 0}
            for c in range(NC):
                by_pool = c in GP_OUT
                n_out[by_pool] += 1
                sp.wait_ge(out_gp if by_pool else out_ready, n_out[by_pool])
                sp.dma_start(outT[:, c, :], x2[:, c, :]).then_inc(out_stored, 16)
            sp.wait_ge(out_stored, 16 * NC)

        @block.gpsimd
        def _(pool):
            def split_lo(r, s):
                pool.wait_ge(hi_done[s], r + 1)
                pool.tensor_tensor(w_lo[:, s, :], raw[:, s, :], w_hi[:, s, :].bitcast(F32), ALU.subtract
                                   ).then_inc(lo_done[s], 1)

            for s in range(2):
                pool.sem_inc(act_stored[s], 16)
                pool.sem_inc(g_stored[s], 16 * PIECES)
            for b in range(OH):
                pool.sem_inc(g_out[b], 1)
                pool.sem_inc(g_mm[b], 1)
            pool.sem_inc(s_out, 1)
            pool.sem_inc(selT_out, 1)
            pool.iota(tab["kk"][:], [[0, PAIRS], [1, SUB + 1]], base=0, channel_multiplier=0,
                      allow_small_or_imprecise_dtypes=True).then_inc(iota_ok, 1)
            pool.memset(ones[:], 1.0).then_inc(const_ok, 1)
            pool.memset(epsc[:], EPS).then_inc(const_ok, 1)
            pool.memset(ident[:], 0.0).then_inc(const_ok, 1)
            pool.wait_ge(const_ok, 3)
            pool.affine_select(out=ident[:], in_=ident[:], compare_op=ALU.not_equal, fill=1.0, base=0,
                               pattern=[[-1, P]], channel_multiplier=1).then_inc(const_ok, 1)
            pool.memset(hc[:, :, 0:PAD], 0.0).then_inc(const_ok, 1)
            pool.iota(iota_row[:], [[1, P]], base=0, channel_multiplier=0,
                      allow_small_or_imprecise_dtypes=True).then_inc(const_ok, 1)
            pool.iota(iota16[:], [[1, TOPK]], base=0, channel_multiplier=0,
                      allow_small_or_imprecise_dtypes=True).then_inc(const_ok, 1)
            pool.memset(m2, 0.0).then_inc(m2_zero, 1)
            chain = Chain(pool, pool_chain)
            step, tt = chain.step, pool.tensor_tensor

            def outer(k, x):
                n = k.shape[-1]
                return (k.rearrange("p a (k o) -> p a k o", o=1).broadcast_to([P, PAIRS, n, CH]),
                        x.rearrange("p (a o h) -> p a o h", a=PAIRS, o=1).broadcast_to([P, PAIRS, n, CH]))

            def cols(c0):
                return prm[:, c0:c0 + PAIRS * CH]

            t8 = tmp[:, 0:PAIRS * SUB * CH].rearrange("p (a k h) -> p a k h", a=PAIRS, k=SUB)
            t9 = tmp.rearrange("p (a k h) -> p a k h", a=PAIRS, k=SUB + 1)
            pool.wait_ge(prm_in, 16)
            pool.wait_ge(tab_done, 1)
            pool.wait_ge(ms_done, 1)
            tt(ab_r, *outer(rev_r[:], cols(S_BR)), ALU.mult)
            step(tt(t8, *outer(rev_i[:], cols(S_BI)), ALU.mult))
            step(tt(ab_r, ab_r, t8, ALU.subtract))
            tt(ab_i, *outer(rev_r[:], cols(S_BI)), ALU.mult)
            step(tt(t8, *outer(rev_i[:], cols(S_BR)), ALU.mult))
            step(tt(ab_i, ab_i, t8, ALU.add))
            pool.sem_inc(ab_done, 1)
            tt(cp_r[:], *outer(tab["fpr"][:], cols(S_CR)), ALU.mult)
            step(tt(t9, *outer(tab["fpi"][:], cols(S_CI)), ALU.mult))
            step(tt(cp_r[:], cp_r[:], t9, ALU.subtract))
            tt(cp_i[:], *outer(tab["nfpr"][:], cols(S_CI)), ALU.mult)
            step(tt(t9, *outer(tab["nfpi"][:], cols(S_CR)), ALU.mult))
            tt(cp_i[:], cp_i[:], t9, ALU.add).then_inc(cp_done, 1)
            split_lo(R_WOUT, 0)
            split_lo(R_WOUT, 1)
            n = 0
            for i, (a, k) in enumerate(gp_taps):
                if i == ZERO_AT:
                    pool.wait_ge(z_done, 1)
                    pool.memset(m1[:], 0.0).then_inc(states_zero, 1)
                if gp_taps[i - 1][0] == a:
                    pool.wait_ge(prod_done, i + 1)
                    wait(pool, prod_used, n)
                    tt(gp_sum[a], gp_sum[a], prod[:, n % 2, :], ALU.add).then_inc(prod_used, 1)
                    n += 1
            for r in range(R_WOUT + 1, R_WQ + 1):
                split_lo(r, 0)
                split_lo(r, 1)
            for c in range(1, NC, 2):
                pool.wait_ge(xhi_done, c + 1)
                tt(rhs_lo[:, c, :], sq[:, c, :], rhs_hi[:, c, :].bitcast(F32), ALU.subtract).then_inc(xn_odd, 1)
            with pool.Fori(R_WQ + 1, NTILES // 2) as r:
                split_lo(r, 0)
                split_lo(r, 1)
            for c in (0, 2, 4):
                pool.wait_ge(fsq_done, c + 2)
                tt(fsq[:, c, :], fsq[:, c, :], fsq[:, c + 1, :], ALU.add).then_inc(pair_done, 1)
            pool.wait_ge(rstd_done, 1)
            for n, c in enumerate(GP_OUT):
                pool.wait_ge(scaled, n + 1)
                tt(x2[:, c, :], xg[:, n, :], rstd[:], ALU.mult).then_inc(out_gp, 1)

        @block.scalar
        def _(act):
            def split_hi(r, s):
                wait(act, mm_done[s], r)
                act.wait_ge(raw_full[s], r * 16 + 16)
                act.activation(w_hi[:, s, :], raw[:, s, :], ACT.Copy).then_inc(hi_done[s], 1)

            act.wait_ge(vec_in, 16)
            for c in range(NC):
                act.wait_ge(x_in[c // 2], 16)
                if c == 4:
                    split_hi(0, 0)
                act.activation(rhs_hi[:, c, :], xuc[:, c, :], ACT.Copy, scale=vec[:, V_G1 + c:V_G1 + c + 1]
                               ).then_inc(rhs_hi_done, 1)
            split_hi(0, 1)
            for c in range(NC):
                act.activation(sq[:, c, :], xuc[:, c, :], ACT.Square).then_inc(sq_done, 1)
            act.wait_ge(prm_in, 16)
            act.activation(small[:, 0, :], prm[:, S_DT:S_DT + PAIRS], ACT.Exp).then_inc(dt_done, 1)
            split_hi(1, 0)
            act.wait_ge(angle_done, 1)
            act.activation(tab["mag"][:], tab["exps"][:], ACT.Exp).then_inc(trig_done, 1)
            act.activation(tab["sin"][:], tab["red"][:], ACT.Sin).then_inc(trig_done, 1)
            act.activation(tab["sinh"][:], tab["half"][:], ACT.Sin).then_inc(trig_done, 1)
            split_hi(1, 1)
            act.wait_ge(ms_done, 1)
            act.wait_ge(const_ok, 7)
            act.activation(rstd[:], PS[:, 4, :], ACT.Sqrt, bias=epsc[:], scale=1.0 / D).then_inc(std_done, 1)
            for n in range(2, WOUT):
                split_hi(n // 2 + 1, n % 2)
                if n >= CT and n % 2 == 1:
                    a = (n - CT) // 2
                    act.wait_ge(evacuated[1], CT // 2 + a + 1)
                    act.activation(sg[:, a % 2, :], sg[:, a % 2, :], ACT.Sigmoid).then_inc(sig_done, 1)
            for k in range(8):
                act.wait_ge(m1_part, k + 1)
                act.activation(m1[:, k // 4, (k % 4) * 4:(k % 4) * 4 + 4, :].rearrange("p a m -> p (a m)"),
                               PS[:, 4 + k % 4, :], ACT.Copy).then_inc(m1_out, 1)
            act.wait_ge(m1_part, 8)
            for k in range(PE_TAP, WIDTH):
                w0 = V_CW + DCT * WIDTH + k
                act.activation(diag[:, k - PE_TAP, :], ident[:], ACT.Copy, scale=vec[:, w0:w0 + 1]
                               ).then_inc(diag_done, 1)
            n_ring = 0

            def tap_product(i):
                nonlocal n_ring
                a, k = gp_taps[i]
                dst = gp_sum[a]
                if gp_taps[i - 1][0] == a:
                    wait(act, prod_used, n_ring - 1)
                    dst = prod[:, n_ring % 2, :]
                    n_ring += 1
                w0 = V_CW + a * WIDTH + k
                act.activation(dst, hc[:, a, k:k + T], ACT.Copy, scale=vec[:, w0:w0 + 1]).then_inc(prod_done, 1)

            for k in range(8):
                act.wait_ge(k_part, k + 1)
                g0 = (k // 2) * 8
                act.activation(kimp[0:CH, g0:g0 + 8, :].rearrange("p (a e) m -> p e a m", e=2)[:, k % 2],
                               PS[0:CH, 4 + k % 4, :].rearrange("p (a m) -> p a m", a=4), ACT.Copy).then_inc(k_out, 1)
                if k == 0:
                    act.wait_ge(h_ready, 1)
                tap_product(k)
            for i in range(8, len(gp_taps)):
                if i in Y_OUT_AT:
                    half = Y_OUT_AT.index(i)
                    for b in (2 * half, 2 * half + 1):
                        act.wait_ge(y_done, b + 1)
                        act.activation(ysb[:, b * T:(b + 1) * T], PS[:, Y_BANKS[b], :], ACT.Copy).then_inc(y_out, 1)
                tap_product(i)
            for a in range(CT):
                act.wait_ge(ypre_done, a + 1)
                act.activation(y_t[:, a, :], y_t[:, a, :], ACT.Gelu).then_inc(gelu_done, 1)
            for a in range(CT):
                act.wait_ge(xc_done, a + 1)
                act.activation(hc[:, a, 0:T], cv[:, a, :], ACT.Square).then_inc(csq_done, 1)
            for a in range(CT):
                act.wait_ge(glu_done, a + 1)
                act.activation(ysb[:, a * T:(a + 1) * T], PS[:, 4 + a, :], ACT.Sigmoid,
                               bias=vec[:, V_GB + a:V_GB + a + 1]).then_inc(gsig_done, 1)
            for a in range(CT):
                act.wait_ge(yssm_done, a + 1)
                act.activation(rhs_hi[:, a, :].rearrange("p (c i) -> p i c", i=SUB),
                               y_t[:, a, :].rearrange("p (i c) -> p i c", i=SUB), ACT.Copy
                               ).then_inc(rhs_hi_done, 1)
            act.wait_ge(var_done, 1)
            act.activation(sg[:, 0, :], PS[:, 1, :], ACT.Sqrt, bias=epsc[:], scale=1.0 / T).then_inc(cstd_done, 1)
            split_hi(R_WOUT + 1, 0)
            for a in range(CT):
                act.wait_ge(hn_done, a + 1)
                act.activation(cv[:, a, :], cv[:, a, :], ACT.Silu, bias=vec[:, V_LB + a:V_LB + a + 1],
                               scale=vec[:, V_LG + a:V_LG + a + 1]).then_inc(silu_done, 1)
            for a in range(CT):
                act.wait_ge(silu_done, a + 1)
                act.activation(rhs_hi[:, CT + a, :], cv[:, a, :], ACT.Copy).then_inc(rhs_hi_done, 1)
            split_hi(R_WOUT + 1, 1)
            split_hi(R_WOUT + 2, 0)
            split_hi(R_WOUT + 2, 1)
            for n in range(NC // 2):
                r, s = R_WOUT + (n + 4) // 2, n % 2
                split_hi(r + 1, s)
                act.wait_ge(x2_done, NC // 2 + n + 1)
                act.activation(sq[:, 2 * n, :], x2[:, 2 * n, :], ACT.Square).then_inc(sq2_done, 1)
                act.wait_ge(evacuated[s], r + 1)
                act.activation(sq[:, 2 * n + 1, :], x2[:, 2 * n + 1, :], ACT.Square).then_inc(sq2_done, 1)
            act.wait_ge(ms2_done, 1)
            act.activation(rstd[:], PS[:, 4, :], ACT.Sqrt, bias=epsc[:], scale=1.0 / D).then_inc(std2_done, 1)
            for c in range(NC):
                act.wait_ge(xn_done, c + 1)
                act.activation(rhs_hi[:, c, :], sq[:, c, :], ACT.Copy).then_inc(xhi_done, 1)
            def query(h, s):
                act.wait_ge(mm_done[s], h + (R_WQ + 1))
                act.activation(q_sb[:, s, :], PS[:, s, :], ACT.Copy).then_inc(evacuated[s], 1)
                split_hi(h + (R_WQ + 1), s)

            def scores_out(h, s):
                row = s_all[:, 2 * h + s] if isinstance(h, int) else s_all[:, bass.ds(h * 2 + s, 1), :].rearrange(
                    "p a t -> p (a t)")
                act.wait_ge(s_done, h * 2 + (s + 1))
                act.activation(row, PS[:, 4 + s, :], ACT.Copy).then_inc(s_out, 1)

            query(0, 0)
            query(0, 1)
            scores_out(0, 0)
            with act.Fori(1, HEADS) as it:
                query(it, 0)
                scores_out(it - 1, 1)
                query(it, 1)
                scores_out(it, 0)

            def u_step(r, k, s):
                act.wait_ge(mm_done[s], r + 1)
                act.wait_ge(act_stored[s], k * 16 + 16)
                act.activation(act_sb[:, s, :], PS[:, s, :], ACT.Gelu).then_inc(evacuated[s], 1)
                split_hi(r + 1, s)

            act.activation(gelu_warm[:], epsc[:], ACT.Gelu)
            u_step(R_U, 0, 0)
            scores_out(HEADS - 1, 1)
            u_step(R_U, 0, 1)
            with act.Fori(1, EXP_AT // 2) as it:
                for s in range(2):
                    u_step(it + R_U, it, s)
            act.wait_ge(sub_done, 1)
            act.activation(sel_all[:], sel_all[:], ACT.Exp).then_inc(exp_done, 1)
            act.activation(gelu_warm[:], epsc[:], ACT.Gelu)
            with act.Fori(EXP_AT // 2, ALONE // 2) as it:
                for s in range(2):
                    u_step(it + R_U, it, s)
            with act.Fori(0, TB) as it:
                for q in range(TURN_TILES):
                    u_step(it * (TURN_TILES // 2) + (R_SPREAD + q // 2),
                           it * (TURN_TILES // 2) + (ALONE // 2 + q // 2), q % 2)
                    half, w = q // (TURN_TILES // 2), q % (TURN_TILES // 2)
                    if w == 0:
                        act.wait_ge(g_stored[half], it * (16 * PIECES) + 16 * PIECES)
                    for b in range(TILE_GROUPS):
                        t0, o = w * STEP_TOK + b * GROUP, (q % 2) * TILE_GROUPS + b
                        act.wait_ge(g_mm[o], it * SLOT_USES + (q // 2 + 2))
                        act.activation(gst[:, half, :, t0:t0 + GROUP].rearrange("p i t -> p t i"),
                                       PS[:, 2 + o, :].rearrange("p (t i) -> p t i", t=GROUP), ACT.Copy,
                                       scale=1.0 / GSCALE).then_inc(g_out[o], 1)
            with act.Fori(0, (KEYS - ALONE - SPREAD) // 2) as it:
                for s in range(2):
                    u_step(it + R_REST, it + (ALONE + SPREAD) // 2, s)
            with act.Fori(0, KEYS // 2 - 1) as it:
                for s in range(2):
                    split_hi(it + (R_V + 1), s)
            for c in range(NC):
                act.wait_ge(fin_done, c + 1)
                act.activation(fsq[:, c, :], x2[:, c, :], ACT.Square).then_inc(fsq_done, 1)
            for n, c in enumerate(GP_OUT):
                act.activation(xg[:, n, :], x2[:, c, :], ACT.Copy, scale=vec[:, V_GF + c:V_GF + c + 1]
                               ).then_inc(scaled, 1)
            act.wait_ge(fms_done, 1)
            act.activation(rstd[:], PS[:, 0, :], ACT.Sqrt, bias=epsc[:], scale=1.0 / D).then_inc(fstd_done, 1)

        @block.tensor
        def _(pe):
            def product(r, s, out, ready=None):
                pe.wait_ge(lo_done[s], r + 1)
                for c in range(NC):
                    if ready:
                        pe.wait_ge(*ready(c))
                    hi, lo = w_hi[:, s, c * P:(c + 1) * P], w_lo[:, s, c * P:(c + 1) * P]
                    pe.matmul(out, hi, rhs_hi[:, c, :], start=(c == 0), stop=False)
                    pe.matmul(out, hi, rhs_lo[:, c, :], start=False, stop=False)
                    mm = pe.matmul(out, lo, rhs_hi[:, c, :], start=False, stop=(c == NC - 1))
                mm.then_inc(mm_done[s], 1)

            def stream(r, s, ready=None):
                wait(pe, evacuated[s], r)
                product(r, s, PS[:, s, :], ready)

            product(0, 0, PS[:, 0, :], lambda c: (rhs_done, c + 1))
            product(0, 1, PS[:, 1, :])
            pe.wait_ge(const_ok, 7)
            pe.wait_ge(sum_done, NC - 1)
            pe.matmul(PS[:, 4, :], ones[:], sq[:, 0, :], start=True, stop=True).then_inc(ms_done, 1)
            product(1, 0, PS[:, 2, :])
            product(1, 1, PS[:, 3, :])
            for s in range(2):
                pe.wait_ge(evacuated[s], 1)
                product(2, s, PS[:, s, :])
            for r in range(3, R_WOUT):
                stream(r, 0)
                stream(r, 1)
            for k in range(8):
                pe.wait_ge(ab_done, 1)
                if k >= 4:
                    pe.wait_ge(m1_out, k - 3)
                for a in range(4):
                    src = (ab_r, ab_i)[k // 4][:, (k % 4) * 4 + a].rearrange("p j h -> p (j h)")
                    mm = pe.transpose(PS[:, 4 + k % 4, a * P:(a + 1) * P], src, ident[:])
                mm.then_inc(m1_part, 1)
            for k in range(8):
                pe.wait_ge(cp_done, 1)
                pe.wait_ge(m1_out if k < 4 else k_out, 5 + k if k < 4 else k - 3)
                for w in range(4):
                    a, rows = (k // 2) * 4 + w, slice((k % 2) * STATE, (k % 2 + 1) * STATE)
                    for ri, (b0, cp) in enumerate(((S_BR, cp_r), (S_BI, cp_i))):
                        mm = pe.matmul(PS[0:CH, 4 + k % 4, w * P:(w + 1) * P],
                                       prm[rows, b0 + a * CH:b0 + (a + 1) * CH],
                                       cp[rows, a, 0:SUB, :].rearrange("p k h -> p (k h)"),
                                       start=(ri == 0), stop=(ri == 1))
                mm.then_inc(k_part, 1)
            pe.wait_ge(u_in, 16)
            pe.wait_ge(k_out, 8)
            for ri in range(2):
                for g in range(GROUPS):
                    a, rows = g // 2, slice((g % 2) * STATE, (g % 2 + 1) * STATE)
                    mm = pe.matmul(PS[rows, 4 + 2 * ri + a // 8, (a % 8) * NSUB:(a % 8 + 1) * NSUB],
                                   m1[:, ri, a, rows], u_sub[:, g, :], start=True, stop=True)
            mm.then_inc(z_done, 1)
            pe.wait_ge(m2_in, 16 * SUB)

            def y_part(g, n):
                b, o = divmod(g, GROUPS // 4)
                return PS[:, Y_BANKS[b], o * NSUB:(o + n) * NSUB]

            for g in range(GROUPS):
                if g == GROUPS // 2:
                    pe.wait_ge(z_read, 1)
                mm = pe.matmul(y_part(g, 1), m2[:, g, :], u_sub[:, g, :], start=(g % 8 == 0), stop=False,
                               skip_group_check=True)
            mm.then_inc(m2_used, 1)
            for ri, (cp, states) in enumerate(((cp_r, states_r), (cp_i, states_i))):
                pe.wait_ge(sp_done, ri + 1)
                for a in range(PAIRS):
                    mm = pe.matmul(y_part(2 * a, 2), cp[:, a, 1:SUB + 1, :].rearrange("p k h -> p (k h)"),
                                   states[:, a, :], start=False, stop=(ri == 1), skip_group_check=True)
                    if ri == 1 and a % 4 == 3:
                        mm.then_inc(y_done, 1)
            pe.wait_ge(h_ready, 1)
            pe.wait_ge(diag_done, WIDTH - PE_TAP)
            for k in range(PE_TAP, WIDTH):
                mm = pe.matmul(PS[:, 1, :], diag[:, k - PE_TAP, :], hc[:, DCT, k:k + T], start=(k == PE_TAP),
                               stop=(k == WIDTH - 1))
            mm.then_inc(pe_taps, 1)
            pe.wait_ge(cv3_done, 1)
            for n, a in enumerate((DCT, 0, 1, 2)):
                if a < DCT:
                    pe.wait_ge(tap_done[a], WIDTH if a < DCT - 1 else GP_TAP + 1)
                mm = pe.matmul(PS[:, 0, :], ones[:], cv[:, a, :], start=(n == 0), stop=(n == CT - 1))
            mm.then_inc(mean_done, 1)
            pe.wait_ge(bd_in, 16)
            pe.wait_ge(y_out, 4)
            for a in range(CT):
                pe.wait_ge(gelu_done, a + 1)
                pe.matmul(PS[:, 4 + a, :], bd[:, a, :], y_t[:, a, :], start=True, stop=True).then_inc(glu_done, 1)
            for a in range(CT):
                pe.wait_ge(csq_done, a + 1)
                mm = pe.matmul(PS[:, 1, :], ones[:], hc[:, a, 0:T], start=(a == 0), stop=(a == CT - 1))
            mm.then_inc(var_done, 1)

            def w_out_tile(n):
                r, s, first = R_WOUT + n // 2, n % 2, n % 4 == 0
                pe.wait_ge(evacuated[s], r)
                pe.wait_ge(lo_done[s], r + 1)
                for m in range(2):
                    for i in range(CT):
                        if first and m == 0:
                            pe.wait_ge(rhs_done, NC + (n // 4) * CT + i + 1)
                        c, out = CT * (n // 4) + i, PS[:, 2 * (1 - s) + m, :]
                        cut = slice((m * CT + i) * P, (m * CT + i + 1) * P)
                        pe.matmul(out, w_hi[:, s, cut], rhs_hi[:, c, :], start=(i == 0), stop=False)
                        pe.matmul(out, w_hi[:, s, cut], rhs_lo[:, c, :], start=False, stop=False)
                        mm = pe.matmul(out, w_lo[:, s, cut], rhs_hi[:, c, :], start=False, stop=(i == CT - 1))
                    mm.then_inc(mm_done[s] if m else half_done, 1)

            for n in range(4):
                if n == 1:
                    pe.wait_ge(cstd_done, 1)
                w_out_tile(n)

            for n in range(4, 8):
                w_out_tile(n)
            pe.wait_ge(sum2_done, NC - 3)
            pe.matmul(PS[:, 4, :], ones[:], sq[:, 0, :], start=True, stop=False)
            for c in (NC - 2, NC - 1):
                pe.wait_ge(sq2_done, c + 1)
                mm = pe.matmul(PS[:, 4, :], ones[:], sq[:, c, :], start=False, stop=(c == NC - 1))
            mm.then_inc(ms2_done, 1)

            def scores(h, s):
                pe.wait_ge(evacuated[s], h + (R_WQ + 1))
                wait(pe, s_out, 2 * h + s if isinstance(h, int) else h * 2 + s)
                for b in range(TB):
                    out, cut = PS[:, 4 + s, b * P:(b + 1) * P], slice(b * P, (b + 1) * P)
                    mm = pe.matmul(out, q_sb[:, s, cut], keyT[:, s, :], start=True, stop=True)
                mm.then_inc(s_done, 1)

            stream(R_WQ, 0, lambda c: ((xn_ready, xn_odd)[c % 2], c // 2 + 1))
            stream(R_WQ, 1)
            pe.wait_ge(key_in, 16)
            scores(0, 0)
            with pe.Fori(1, HEADS) as it:
                stream(it + R_WQ, 0)
                scores(it - 1, 1)
                stream(it + R_WQ, 1)
                scores(it, 0)
            stream(R_U, 0)
            scores(HEADS - 1, 1)
            stream(R_U, 1)
            with pe.Fori(1, ALONE // 2 - 1) as it:
                for s in range(2):
                    stream(it + R_U, s)

            def selections(turn):
                pe.wait_ge(sel_done, turn + 1)
                pe.wait_ge(selT_out, turn * 2 + 1)
                for k in range(3):
                    mm = pe.transpose(PS[:, 6, k * P:(k + 1) * P], sel_now[:, k, :], ident[:])
                mm.then_inc(selT_done, 1)

            def spread_turn(turn, last):
                for q in range(TURN_TILES):
                    stream(turn * (TURN_TILES // 2) + (R_SPREAD + q // 2), q % 2)
                    if q == TURN_TILES - 1 and not last:
                        selections(turn + 1)
                    for b in range(TILE_GROUPS):
                        n, o = turn * SLOT_USES + q // 2, (q % 2) * TILE_GROUPS + b
                        pe.wait_ge(oh_done[o], n + 1)
                        pe.wait_ge(g_out[o], n + 1)
                        for t in range(GROUP):
                            out = PS[:, 2 + o, t * P:(t + 1) * P]
                            pe.matmul(out, oh_1[:, o, t, :], oh_gh[:, o, t, :], start=True, stop=False)
                            mm = pe.matmul(out, oh_1[:, o, t, :], oh_gl[:, o, t, :], start=False, stop=True)
                        mm.then_inc(g_mm[o], 1)

            stream(R_SPREAD - 1, 0)
            selections(0)
            stream(R_SPREAD - 1, 1)
            with pe.Fori(0, TB - 1) as it:
                spread_turn(it, False)
            spread_turn(TB - 1, True)
            with pe.Fori(0, (KEYS - ALONE - SPREAD) // 2) as it:
                for s in range(2):
                    stream(it + R_REST, s)

            def v_step(r, k, s, first, last):
                pe.wait_ge(lo_done[s], r + 1)
                pe.wait_ge(wt_done[s], k + 1)
                for m in [*range(2, NC), 0, 1] if first else range(NC):
                    if first and m < 2:
                        pe.wait_ge(evacuated[m], R_V)
                    hi, lo = w_hi[:, s, m * P:(m + 1) * P], w_lo[:, s, m * P:(m + 1) * P]
                    pe.matmul(PS[:, m, :], hi, wt_hi[:, s, :], start=first, stop=False, skip_group_check=True)
                    pe.matmul(PS[:, m, :], hi, wt_lo[:, s, :], start=False, stop=False, skip_group_check=True)
                    mm = pe.matmul(PS[:, m, :], lo, wt_hi[:, s, :], start=False, stop=last, skip_group_check=True)
                    if last:
                        mm.then_inc(peer_done, 1)
                if not last:
                    mm.then_inc(mm_done[s], 1)

            for s in range(2):
                pe.wait_ge(g_out[s], TB * SLOT_USES + 1)
                pe.wait_ge(g_out[s + 2], TB * SLOT_USES + 1)
            for s in range(2):
                v_step(R_V, 0, s, s == 0, False)
            with pe.Fori(0, KEYS // 2 - 2) as it:
                for s in range(2):
                    v_step(it + (R_V + 1), it + 1, s, False, False)
            for s in range(2):
                v_step(R_V + KEYS // 2 - 1, KEYS // 2 - 1, s, False, s == 1)
            for c in range(0, NC, 2):
                pe.wait_ge(*((pair_done, c // 2 + 1) if c < NC - 2 else (last_pair, 1)))
                mm = pe.matmul(PS[:, 0, :], ones[:], fsq[:, c, :], start=(c == 0), stop=(c == NC - 2))
            mm.then_inc(fms_done, 1)

        @block.vector
        def _(dve):
            ch = Chain(dve, dve_chain)
            step = ch.step
            tt, ts, stt = dve.tensor_tensor, dve.tensor_scalar, dve.scalar_tensor_tensor
            dt, lrdt, lidt, den, fr, fi, t1, t2, nr = (small[:, i, :] for i in range(9))
            lr, li = prm[:, S_LR:S_LR + PAIRS], prm[:, S_LI:S_LI + PAIRS]

            def per_k(x):
                return x.rearrange("p (a k) -> p a k", k=1).broadcast_to([P, PAIRS, SUB + 1])

            def angles():
                dve.wait_ge(dt_done, 1)
                dve.wait_ge(iota_ok, 1)
                tt(lrdt, lr, dt, ALU.mult)
                step(tt(lidt, li, dt, ALU.mult))
                tt(tab["exps"][:], per_k(lrdt), tab["kk"][:], ALU.mult)
                step(tt(tab["phi"][:], per_k(lidt), tab["kk"][:], ALU.mult))
                step(ts(tab["turns"][:], tab["phi"][:], 0.15915494309189535, MAGIC, ALU.mult, ALU.add))
                step(ts(tab["turns"][:], tab["turns"][:], -MAGIC, None, ALU.add))
                step(stt(tab["red"][:], tab["turns"][:], -TWO_PI[0], tab["phi"][:], ALU.mult, ALU.add))
                step(stt(tab["phi"][:], tab["turns"][:], -TWO_PI[1], tab["red"][:], ALU.mult, ALU.add))
                step(stt(tab["red"][:], tab["turns"][:], -TWO_PI[2], tab["phi"][:], ALU.mult, ALU.add))
                step(ts(tab["red"][:], tab["red"][:], PI_IN, -PI_IN, ALU.min, ALU.max))
                ts(tab["half"][:], tab["red"][:], 0.5, None, ALU.mult).then_inc(angle_done, 1)

            def powers():
                dve.wait_ge(trig_done, 3)
                step(tt(tab["cos"][:], tab["sinh"][:], tab["sinh"][:], ALU.mult))
                step(ts(tab["cos"][:], tab["cos"][:], -2.0, 1.0, ALU.mult, ALU.add))
                tt(tab["pr"][:], tab["mag"][:], tab["cos"][:], ALU.mult)
                step(tt(tab["pi"][:], tab["mag"][:], tab["sin"][:], ALU.mult))
                a_i = tab["pi"][:, :, 1]
                ts(nr, tab["pr"][:, :, 1], -1.0, None, ALU.add)
                tt(t1, lr, lr, ALU.mult)
                step(tt(t2, li, li, ALU.mult))
                step(tt(den, t1, t2, ALU.add))
                dve.reciprocal(den, den)
                tt(t1, nr, lr, ALU.mult)
                tt(small[:, 9, :], a_i, lr, ALU.mult)
                tt(small[:, 10, :], nr, li, ALU.mult)
                step(tt(t2, a_i, li, ALU.mult))
                tt(fr, t1, t2, ALU.add)
                step(tt(fi, small[:, 9, :], small[:, 10, :], ALU.subtract))
                tt(fr, fr, den, ALU.mult)
                step(tt(fi, fi, den, ALU.mult))

            def f_powers():
                tt(tab["fpr"][:], per_k(fr), tab["pr"][:], ALU.mult)
                tt(tab["fpi"][:], per_k(fr), tab["pi"][:], ALU.mult)
                step(tt(tab["t9"][:], per_k(fi), tab["pi"][:], ALU.mult))
                step(tt(tab["fpr"][:], tab["fpr"][:], tab["t9"][:], ALU.subtract))
                step(tt(tab["t9"][:], per_k(fi), tab["pr"][:], ALU.mult))
                step(tt(tab["fpi"][:], tab["fpi"][:], tab["t9"][:], ALU.add))
                ts(tab["nfpr"][:], tab["fpr"][:], -1.0, None, ALU.mult)
                ts(tab["nfpi"][:], tab["fpi"][:], -1.0, None, ALU.mult)
                for j in range(SUB):
                    dve.tensor_copy(rev_r[:, :, j], tab["pr"][:, :, SUB - 1 - j])
                    ins = dve.tensor_copy(rev_i[:, :, j], tab["pi"][:, :, SUB - 1 - j])
                ins.then_inc(tab_done, 1)

            def rotations(n):
                if n == 1:
                    dve.memset(rot_r[:, :, 0:1], 1.0)
                    dve.memset(rot_i[:, :, 0:1], 0.0)
                    dve.tensor_copy(rot_r[:, :, 1:2], tab["cos"][:, :, SUB:SUB + 1])
                    step(dve.tensor_copy(rot_i[:, :, 1:2], tab["sin"][:, :, SUB:SUB + 1]))
                lo, hi = slice(1, n + 1), slice(n + 1, 2 * n + 1)
                wr = rot_r[:, :, n:n + 1].broadcast_to([P, PAIRS, n])
                wi = rot_i[:, :, n:n + 1].broadcast_to([P, PAIRS, n])
                ta = hc[:, 1, PAD:PAD + PAIRS * n].rearrange("p (a k) -> p a k", a=PAIRS)
                tb = hc[:, 2, PAD:PAD + PAIRS * n].rearrange("p (a k) -> p a k", a=PAIRS)
                tt(rot_r[:, :, hi], rot_r[:, :, lo], wr, ALU.mult)
                tt(ta, rot_i[:, :, lo], wi, ALU.mult)
                tt(rot_i[:, :, hi], rot_r[:, :, lo], wi, ALU.mult)
                step(tt(tb, rot_i[:, :, lo], wr, ALU.mult))
                tt(rot_r[:, :, hi], rot_r[:, :, hi], ta, ALU.subtract)
                step(tt(rot_i[:, :, hi], rot_i[:, :, hi], tb, ALU.add))

            def tap(a, k):
                w = vec[:, V_CW + a * WIDTH + k:V_CW + a * WIDTH + k + 1]
                if k == 0:
                    ins = ts(cv[:, a, :], hc[:, a, 0:T], w, vec[:, V_CB + a:V_CB + a + 1], ALU.mult, ALU.add)
                else:
                    dve.wait_ge(tap_done[a], k)
                    ins = stt(cv[:, a, :], hc[:, a, k:k + T], w, cv[:, a, :], ALU.mult, ALU.add)
                ins.then_inc(tap_done[a], 1)

            def scale_row(dst, src, g0, c, done):
                stt(dst[:, c, :], src[:, c, :], vec[:, g0 + c:g0 + c + 1], rstd[:], ALU.mult, ALU.mult
                    ).then_inc(done, 1)

            def split_lo(n):
                r, s = n // 2, n % 2
                dve.wait_ge(hi_done[s], r + 1)
                tt(w_lo[:, s, :], raw[:, s, :], w_hi[:, s, :].bitcast(F32), ALU.subtract).then_inc(lo_done[s], 1)

            def gate_h(a):
                dve.wait_ge(sig_done, a + 1)
                step(tt(hc[:, a, PAD:PAD + T], hc[:, a, PAD:PAD + T], sg[:, a % 2, :], ALU.mult))
                if a < DCT:
                    tap(a, 0)
                else:
                    dve.sem_inc(h_ready, 1)

            dve.wait_ge(vec_in, 16)
            for c in range(NC):
                dve.wait_ge(rhs_hi_done, c + 1)
                if c == 4:
                    split_lo(0)
                stt(rhs_lo[:, c, :], xuc[:, c, :], vec[:, V_G1 + c:V_G1 + c + 1], rhs_hi[:, c, :].bitcast(F32),
                    ALU.mult, ALU.subtract).then_inc(rhs_done, 1)
            split_lo(1)
            angles()

            def sum_squares(c, squared, done):
                dve.wait_ge(squared, c + 1)
                wait(dve, done, c - 1)
                tt(sq[:, 0, :], sq[:, 0, :], sq[:, c, :], ALU.add).then_inc(done, 1)

            for c in range(1, 4):
                sum_squares(c, sq_done, sum_done)
            split_lo(2)
            for c in range(4, NC):
                sum_squares(c, sq_done, sum_done)
            split_lo(3)
            dve.wait_ge(std_done, 1)
            step(dve.reciprocal(rstd[:], rstd[:]))
            dve.wait_ge(const_ok, 7)
            between = {0: [powers], 1: [f_powers], 2: [lambda: [rotations(n) for n in (1, 2, 4, 8)]],
                       3: [lambda: rotations(16)], 4: [lambda: rotations(32)]}
            TAPS_A_TILE = 4
            n_taps = 1
            for n in range(WOUT):
                r, s, a = n // 2, n % 2, (n - CT) // 2
                dve.wait_ge(mm_done[s], r + 1)
                if n < CT:
                    tt(u_t[:, n, :].rearrange("p (j c) -> p c j", j=SUB),
                       PS[:, n, :].rearrange("p (c j) -> p c j", j=SUB),
                       rstd[:].rearrange("p (c j) -> p c j", j=SUB), ALU.mult).then_inc(evacuated[s], 1)
                elif s == 0:
                    tt(hc[:, a, PAD:PAD + T], PS[:, 0, :], rstd[:], ALU.mult).then_inc(evacuated[0], 1)
                else:
                    tt(sg[:, a % 2, :], PS[:, 1, :], rstd[:], ALU.mult).then_inc(evacuated[1], 1)
                if 2 <= n < WOUT - 2:
                    split_lo(n + 2)
                for work in between.get(n, []):
                    work()
                if n > CT and s == 0:
                    gate_h(a - 1)
                if n > CT + 1:
                    for k in range(n_taps, n_taps + TAPS_A_TILE):
                        tap(0, k)
                    n_taps += TAPS_A_TILE
            gate_h(CT - 1)
            for k in range(n_taps, WIDTH):
                tap(0, k)
            def taps(k0, k1, conv_tiles):
                with dve.Fori(k0, k1) as k:
                    for a in conv_tiles:
                        dve.wait_ge(tap_done[a], k)
                        w = vec[:, bass.ds(k + (V_CW + a * WIDTH), 1)]
                        stt(cv[:, a, :], hc[:, a, bass.ds(k, T)], w, cv[:, a, :], ALU.mult, ALU.add
                            ).then_inc(tap_done[a], 1)

            taps(1, SCAN_AT, (1, 2))
            dve.wait_ge(z_done, 1)
            dve.wait_ge(m2_in, 16 * SUB)
            z_r = PS[:, 4:6, :].rearrange("p b (a c) -> p (b a) c", a=8)
            z_i = PS[:, 6:8, :].rearrange("p b (a c) -> p (b a) c", a=8)
            v3 = lambda x: x.rearrange("p (a c) -> p a c", a=PAIRS)
            rr, ri = rot_r[:, :, 0:NSUB], rot_i[:, :, 0:NSUB]
            tt(v3(za), z_r, rr, ALU.mult)
            step(tt(v3(zt), z_i, ri, ALU.mult))
            step(tt(za, za, zt, ALU.add))
            tt(v3(zb), z_i, rr, ALU.mult)
            tt(v3(zt), z_r, ri, ALU.mult).then_inc(z_read, 1)
            dve.wait_ge(z_read, 1)
            step(tt(zb, zb, zt, ALU.subtract))
            dve.tensor_copy(v3(zt), tab["mag"][:, :, SUB:SUB + 1].broadcast_to([P, PAIRS, NSUB]))
            step(dve.memset(small[:, 11, :], 0.0))
            step(dve.tensor_copy(v3(zt)[:, :, 0], small[:, 11, :]))
            step(dve.tensor_tensor_scan(zc, zt, za, 0.0, ALU.mult, ALU.add))
            step(dve.tensor_tensor_scan(za, zt, zb, 0.0, ALU.mult, ALU.add))
            tt(v3(zb), v3(zc), rr, ALU.mult)
            step(tt(v3(zt), v3(za), ri, ALU.mult))

            def state_parts(states, x, y, op):
                for e in range(2):
                    rows = slice(e * STATE, (e + 1) * STATE)
                    ins = tt(states[rows, :, e * NSUB + 1:(e + 1) * NSUB], v3(x)[rows, :, 0:NSUB - 1],
                             v3(y)[rows, :, 0:NSUB - 1], op)
                ins.then_inc(sp_done, 1)

            dve.wait_ge(states_zero, 1)
            state_parts(states_r, zb, zt, ALU.subtract)
            dve.wait_ge(sp_done, 1)
            tt(v3(zc), v3(zc), ri, ALU.mult)
            step(tt(v3(zb), v3(za), rr, ALU.mult))
            state_parts(states_i, zc, zb, ALU.add)
            if SCAN_AT < GP_TAP:
                taps(SCAN_AT, GP_TAP, (1, 2))
            taps(GP_TAP, WIDTH, (1,))
            dve.wait_ge(prod_used, PE_TAP - 1)
            dve.wait_ge(pe_taps, 1)
            stt(cv[:, DCT, :], PS[:, 1, :], vec[:, V_CB + DCT:V_CB + DCT + 1], cv[:, DCT, :], ALU.add, ALU.add
                ).then_inc(cv3_done, 1)
            dve.wait_ge(prod_used, len(gp_taps) - 2)
            dve.wait_ge(tap_done[DCT - 1], GP_TAP)
            tt(cv[:, DCT - 1, :], cv[:, DCT - 1, :], sg[:, 0, :], ALU.add).then_inc(tap_done[DCT - 1], 1)

            for a in range(CT):
                dve.wait_ge(y_in[a // 2], 16 * GPT)
                stt(y_t[:, a, :], u_t[:, a, :], vec[:, V_D + a:V_D + a + 1], y_t[:, a, :], ALU.mult, ALU.add
                    ).then_inc(ypre_done, 1)
            dve.wait_ge(mean_done, 1)
            step(ts(sg[:, 1, :], PS[:, 0, :], 1.0 / (CT * P), None, ALU.mult))
            for a in range(CT):
                tt(cv[:, a, :], cv[:, a, :], sg[:, 1, :], ALU.subtract).then_inc(xc_done, 1)
            for a in range(CT):
                dve.wait_ge(gsig_done, a + 1)
                tt(y_t[:, a, :], y_t[:, a, :], ysb[:, a * T:(a + 1) * T], ALU.mult).then_inc(yssm_done, 1)
            for a in range(CT):
                dve.wait_ge(rhs_hi_done, NC + a + 1)
                order = "p (c i) -> p i c"
                tt(rhs_lo[:, a, :].rearrange(order, i=SUB), y_t[:, a, :].rearrange("p (i c) -> p i c", i=SUB),
                   rhs_hi[:, a, :].bitcast(F32).rearrange(order, i=SUB), ALU.subtract).then_inc(rhs_done, 1)

            def residual(n):
                r, s = R_WOUT + n // 2, n % 2
                if n >= 4:
                    dve.wait_ge(evacuated[s], r - 1)
                dve.wait_ge(half_done, n + 1)
                m, b = (n % 4) * 2, 2 * (1 - s)
                tt(x2[:, m, :], PS[:, b, :], x2[:, m, :], ALU.add).then_inc(x2_done, 1)
                dve.wait_ge(mm_done[s], r + 1)
                tt(x2[:, m + 1, :], PS[:, b + 1, :], x2[:, m + 1, :], ALU.add).then_inc(evacuated[s], 1)

            dve.wait_ge(cstd_done, 1)
            step(dve.reciprocal(sg[:, 0, :], sg[:, 0, :]))
            dve.wait_ge(x_again, 16)
            residual(0)
            for a in range(CT):
                dve.wait_ge(csq_done, a + 1)
                dve.wait_ge(xc_done, a + 1)
                tt(cv[:, a, :], cv[:, a, :], sg[:, 0, :], ALU.mult).then_inc(hn_done, 1)
            residual(1)
            for a in range(CT):
                dve.wait_ge(rhs_hi_done, NC + CT + a + 1)
                tt(rhs_lo[:, CT + a, :], cv[:, a, :], rhs_hi[:, CT + a, :].bitcast(F32), ALU.subtract
                   ).then_inc(rhs_done, 1)
            for n in range(2, NC):
                if n > NC // 2:
                    for c in (2 * (n - 5), 2 * (n - 5) + 1):
                        if c > 0:
                            sum_squares(c, sq2_done, sum2_done)
                residual(n)
            dve.wait_ge(std2_done, 1)
            step(dve.reciprocal(rstd[:], rstd[:]))
            for c in range(NC + 2):
                if c < NC:
                    scale_row(sq, x2, V_G2, c, xn_done)
                if c % 2 == 0 and c >= 2:
                    dve.wait_ge(xhi_done, c - 1)
                    tt(rhs_lo[:, c - 2, :], sq[:, c - 2, :], rhs_hi[:, c - 2, :].bitcast(F32), ALU.subtract
                       ).then_inc(xn_ready, 1)

            blocks = range(TB)
            halves = [(h, b) for h in range(2) for b in blocks]
            STAGES = 11
            with dve.Fori(0, HEADS) as it:
                n = 0

                def stage(ins):
                    nonlocal n
                    n += 1
                    ins.then_inc(top_done, 1)
                    dve.wait_ge(top_done, it * STAGES + n)
                    dve.tensor_copy(gsum[:, 1, 0:1], epsc[:])

                def top16(v, i, src, cut):
                    rows = range(len(v))
                    for j in rows:
                        ins = dve.max(v[j][:, 0:8], src[j])
                    stage(ins)
                    for j in rows:
                        dve.max_index(i[j][:, 0:8], v[j][:, 0:8], src[j])
                        ins = dve.match_replace(cut[j], v[j][:, 0:8], src[j], NEG)
                    stage(ins)
                    for j in rows:
                        ins = dve.max(v[j][:, 8:16], cut[j])
                    stage(ins)
                    for j in rows:
                        ins = dve.max_index(i[j][:, 8:16], v[j][:, 8:16], cut[j])
                    stage(ins)

                dve.wait_ge(s_out, it * 2 + 3)
                stage(dve.tensor_copy(s_cur[:].rearrange("p a b n -> p a (b n)"), s_all[:, bass.ds(it * 2, 2), :]))
                top16([topv[:, h, b, :] for h, b in halves], [topi[:, h, b, :] for h, b in halves],
                      [s_cur[:, h, b, :] for h, b in halves], [s_cut[:, h, b, :] for h, b in halves])
                for k, dst in enumerate((i1_all, i2_all)):
                    dve.tensor_copy(dst[:, :, bass.ds(it, 1), :].rearrange("p b o k -> p b (o k)"), topi[:, k])
                for b in blocks:
                    ins = tt(cand[:, b, :].rearrange("p (i j) -> p i j", i=TOPK),
                             topv[:, 0, b, :].rearrange("p (i j) -> p i j", j=1).broadcast_to([P, TOPK, TOPK]),
                             topv[:, 1, b, :].rearrange("p (i j) -> p i j", i=1).broadcast_to([P, TOPK, TOPK]),
                             ALU.add)
                stage(ins)
                top16([selv[:, b, :] for b in blocks], [seli[:, b, :] for b in blocks],
                      [cand[:, b, :] for b in blocks], [cand_cut[:, b, :] for b in blocks])
                dve.tensor_copy(sel_all[:, :, bass.ds(it, 1), :].rearrange("p b o k -> p b (o k)"), selv[:])
                stage(dve.tensor_copy(ci_all[:, :, bass.ds(it, 1), :].rearrange("p b o k -> p b (o k)"), seli[:]))
            scores = sel_all[:].rearrange("p b h k -> p (b h) k")
            per_head = lambda x: x.rearrange("p (n o) -> p n o", o=1).broadcast_to([P, TB * HEADS, TOPK])
            step(dve.tensor_copy(gsum[:, 0, :], scores[:, :, 0]))
            tt(scores, scores, per_head(gsum[:, 0, :]), ALU.subtract).then_inc(sub_done, 1)
            ci = ci_all[:].rearrange("p b h k -> p b (h k)")
            step(ts(pos[:], ci, 4, None, ALU.logical_shift_right))
            step(dve.tensor_copy(pos_a[:], pos[:]))
            step(ts(pos[:], ci, TOPK - 1, None, ALU.bitwise_and))
            step(dve.tensor_copy(pos_b[:], pos[:]))
            eq3 = eq[:].rearrange("p (n j) -> p n j", j=TOPK)
            eq4 = eq[:].rearrange("p (h k j) -> p h k j", h=HEADS, k=TOPK)
            with dve.Fori(0, TB) as it:
                for k, (where, idx, dst) in enumerate(((pos_a, i1_all, e1), (pos_b, i2_all, e2))):
                    w = where[:, bass.ds(it, 1), :].rearrange("p b (n o) -> p (b n) o", o=1)
                    tt(eq3, w.broadcast_to([P, P, TOPK]),
                       iota16[:].rearrange("p (n j) -> p n j", n=1).broadcast_to([P, P, TOPK]), ALU.is_equal
                       ).then_inc(key_done, 1)
                    dve.wait_ge(key_done, it * 6 + (3 * k + 1))
                    i4 = idx[:, bass.ds(it, 1), :, :].rearrange("p b h (o j) -> p (b h) o j", o=1)
                    tt(eq4, eq4, i4.broadcast_to([P, HEADS, TOPK, TOPK]), ALU.mult).then_inc(key_done, 1)
                    dve.wait_ge(key_done, it * 6 + (3 * k + 2))
                    dve.tensor_reduce(dst[:, bass.ds(it, 1), :].rearrange("p b n -> p (b n)"), eq3, AX_X, ALU.add
                                      ).then_inc(key_done, 1)
                    dve.wait_ge(key_done, it * 6 + (3 * k + 3))
            dve.wait_ge(exp_done, 1)
            step(dve.tensor_reduce(gsum[:, 0, :], scores, AX_X, ALU.add))
            step(dve.reciprocal(gsum[:, 1, :], gsum[:, 0, :]))
            step(tt(scores, scores, per_head(gsum[:, 1, :]), ALU.mult))
            dve.tensor_copy(iota_h[:], iota_row[:])
            with dve.Fori(0, TB) as it:
                for k, src in enumerate((e1, e2, sel_all)):
                    view = src[:] if k < 2 else src[:].rearrange("p b h k -> p b (h k)")
                    ins = dve.tensor_copy(sel_now[:, k, :], view[:, bass.ds(it, 1), :].rearrange("p a n -> p (a n)"))
                ins.then_inc(sel_done, 1)
                dve.wait_ge(selT_done, it + 1)
                dve.tensor_copy(e1T[:], PS[:, 6, 0:P])
                dve.tensor_copy(e2T[:], PS[:, 6, P:2 * P])
                ts(gT[:], PS[:, 6, 2 * P:3 * P], GSCALE, None, ALU.mult)
                ts(ghT[:], PS[:, 6, 2 * P:3 * P], GSCALE, None, ALU.mult).then_inc(selT_out, 1)
                dve.wait_ge(selT_out, it * 2 + 2)
                dve.tensor_copy(ghTf[:], ghT[:])
                tt(glT[:], gT[:], ghT[:], ALU.subtract).then_inc(selT_out, 1)
                dve.wait_ge(selT_out, it * 2 + 3)
                for q in range(TURN_TILES):
                    for b in range(TILE_GROUPS):
                        o = (q % 2) * TILE_GROUPS + b
                        dve.wait_ge(g_mm[o], it * SLOT_USES + (q // 2 + 1))
                        for t in range(GROUP):
                            col = slice(q * STEP_TOK + b * GROUP + t, q * STEP_TOK + b * GROUP + t + 1)
                            ts(oh_1[:, o, t, :], iota_h[:], e1T[:, col], None, ALU.is_equal)
                            ts(oh_gh[:, o, t, :], iota_h[:], e2T[:, col], ghTf[:, col], ALU.is_equal, ALU.mult)
                            ins = ts(oh_gl[:, o, t, :], iota_h[:], e2T[:, col], glT[:, col],
                                     ALU.is_equal, ALU.mult)
                        ins.then_inc(oh_done[o], 1)
            with dve.Fori(0, KEYS // 4) as it:
                for g in range(2):
                    dve.wait_ge(ga_in[g], it * 32 + 32)
                    for s in range(2):
                        dve.wait_ge(mm_done[s], it * 2 + (R_V + g))
                        n = it * 8 + (4 * g + 2 * s)
                        tt(wt[:, s, :].rearrange("p (a t) -> p a t", t=GCH),
                           a_in[:, g, s, :].rearrange("p (a t) -> p a t", t=GCH), g_in[:, g, :, s, :], ALU.mult
                           ).then_inc(wt_part, 1)
                        dve.wait_ge(wt_part, n + 1)
                        dve.tensor_copy(wt_hi[:, s, :], wt[:, s, :]).then_inc(wt_part, 1)
                        dve.wait_ge(wt_part, n + 2)
                        tt(wt_lo[:, s, :], wt[:, s, :], wt_hi[:, s, :].bitcast(F32), ALU.subtract
                           ).then_inc(wt_done[s], 1)
            for m in range(NC):
                dve.wait_ge(peer_done, m + 1)
                tt(x2[:, m, :], PS[:, m, :], x2[:, m, :], ALU.add).then_inc(fin_done, 1)
            dve.wait_ge(fsq_done, NC)
            tt(fsq[:, NC - 2, :], fsq[:, NC - 2, :], fsq[:, NC - 1, :], ALU.add).then_inc(last_pair, 1)
            dve.wait_ge(fstd_done, 1)
            dve.reciprocal(rstd[:], rstd[:]).then_inc(rstd_done, 1)
            dve.wait_ge(rstd_done, 1)
            for c in range(NC):
                if c not in GP_OUT:
                    scale_row(x2, x2, V_GF, c, out_ready)


def kernel(**inputs):
    import concourse.bacc as bacc
    from concourse.bass_utils import run_bass_kernel_spmd

    a = {k: np.asarray(v) for k, v in inputs.items()}
    layer = {k: v[0] for k, v in a.items() if k not in ("x", "final_g")}

    def channels(v):
        return v.reshape(-1, P).T

    def states(v):
        return v.reshape(PAIRS, 2, STATE, -1).transpose(1, 2, 0, 3).reshape(P, -1)

    cw = layer["conv_w"].T.reshape(CT, P, WIDTH).transpose(1, 0, 2).reshape(P, -1)
    vecs = np.concatenate([channels(layer["norm1_g"]), channels(layer["norm2_g"]), channels(a["final_g"]),
                           channels(layer["conv_b"]), channels(layer["conv_ln_g"]), channels(layer["conv_ln_b"]),
                           channels(layer["ssm_d"]), channels(layer["glu_b"]), cw], axis=1)
    log_dt = np.broadcast_to(layer["log_dt"][:, None], (GROUPS, STATE))
    ssm = np.concatenate([states(layer["lam_re"]), states(layer["lam_im"]), states(log_dt),
                          states(layer["ssm_b_re"]), states(layer["ssm_b_im"]),
                          states(layer["ssm_c_re"].transpose(0, 2, 1)),
                          states(layer["ssm_c_im"].transpose(0, 2, 1))], axis=1)
    xT = a["x"][0].T.reshape(NC, P, T).transpose(1, 0, 2)
    glu_bd = np.zeros((P, CT, P), np.float32)
    for g in range(GROUPS):
        q = g % GPT
        glu_bd[q * CH:(q + 1) * CH, g // GPT, q * CH:(q + 1) * CH] = layer["glu_w"][g]
    keys = np.stack([layer["peer_k1"].T, layer["peer_k2"].T], axis=1)

    def columns(w):
        return w.reshape(NC, P, -1, P).transpose(2, 1, 0, 3).reshape(-1, P, D)

    w_in = columns(layer["w_in"])
    order = [0, 1, 2, 3] + [i for a4 in range(CT) for i in (CT + a4, 2 * CT + a4)]
    u = layer["peer_u"].reshape(KEYS, KEYS, NC, P).transpose(1, 3, 2, 0).reshape(KEYS, P, D)
    v = layer["peer_v"].reshape(KEYS, KEYS, D).transpose(1, 0, 2)
    w_out = layer["w_out"].reshape(2, CT, P, NC // 2, 2, P).transpose(0, 3, 2, 4, 1, 5).reshape(-1, P, D)
    tiles = np.concatenate([w_in[order], w_out, columns(layer["peer_wq"]), u, v])

    nc = bacc.Bacc("TRN2", target_bir_lowering=False, num_devices=1)
    arrays, args = {}, []
    for name, arr in (("vecs", vecs), ("ssm", ssm), ("xT", xT), ("glu_bd", glu_bd), ("keys", keys),
                      ("tiles", tiles)):
        arrays[name] = np.ascontiguousarray(arr)
        args.append(nc.dram_tensor(name, arrays[name].shape, F32, kind="ExternalInput").ap())
    outT = nc.dram_tensor("outT", (P, NC, T), F32, kind="ExternalOutput").ap()
    build(nc, *args, outT)
    result = run_bass_kernel_spmd(nc, [arrays], core_ids=[0])
    got = result.results[0]["outT"]
    return got.transpose(1, 0, 2).reshape(D, T).T[None]
```
